# Optimizing a Trainium2 kernel written in Bass

```python
import math
import jax, jax.numpy as jnp
from jax import lax
import numpy as np

D_MODEL = 1024
BATCH = 1
SEQ = 1024
DEPTH = 1
DEC_BATCH = 8
DEC_SEQ = 8
PAST_LEN = 4096
PAGE_SIZE = 128

HD = 64
NSA_HEADS = 8
NSA_KV_HEADS = 2
NSA_GROUP = NSA_HEADS // NSA_KV_HEADS
NSA_BLOCK = 64
NSA_TOPN = 16
NSA_WINDOW = 512
NSA_KINDS = 6
DIFF_HEADS = 4
DIFF_VD = 2 * HD
D_FF = 2816
Q_BLOCK = 128
EPS = 1e-6
FORCE_SCORE = 1e4
SPLITS = (NSA_HEADS * HD, NSA_KINDS * NSA_KV_HEADS * HD, 3 * NSA_HEADS,
          DIFF_HEADS * 2 * HD, DIFF_HEADS * 2 * HD, DIFF_HEADS * DIFF_VD, 2 * D_MODEL)
IN_WIDTH = sum(SPLITS)

kernel_name = 'nsa_diffattn_macaron_hybrid_step'

def rmsnorm(x, g):
    xf = x.astype(jnp.float32)
    y = xf * lax.rsqrt(jnp.mean(xf * xf, axis=-1, keepdims=True) + EPS)
    return (y * g.astype(jnp.float32)).astype(x.dtype)

def swiglu(x, w1, w3, w2):
    return (jax.nn.silu(x @ w1) * (x @ w3)) @ w2

def alibi_slopes(n):
    return 2.0 ** (-8.0 * jnp.arange(1, n + 1, dtype=jnp.float32) / n)

def masked_softmax(s, mask, axes):
    s = jnp.where(mask, s.astype(jnp.float32), -1e30)
    m = jnp.max(s, axis=axes, keepdims=True)
    p = jnp.where(mask, jnp.exp(s - m), 0.0)
    return p / jnp.maximum(jnp.sum(p, axis=axes, keepdims=True), 1e-30)

def project(h, w_in):
    B_, T = h.shape[:2]
    offs = [int(o) for o in np.cumsum(SPLITS)[:-1]]
    nq, nkv, ng, dq, dk, dv, mg = jnp.split(h @ w_in, offs, axis=-1)
    nq = nq.reshape(B_, T, NSA_KV_HEADS, NSA_GROUP, HD)
    nkv = nkv.reshape(B_, T, NSA_KINDS, NSA_KV_HEADS, HD)
    ng = jax.nn.sigmoid(ng.reshape(B_, T, NSA_KV_HEADS, NSA_GROUP, 3))
    dq = dq.reshape(B_, T, DIFF_HEADS, 2, HD)
    dk = dk.reshape(B_, T, DIFF_HEADS, 2, HD)
    dv = dv.reshape(B_, T, DIFF_HEADS, DIFF_VD)
    mg = jax.nn.sigmoid(mg.reshape(B_, T, 2, D_MODEL))
    return nq, nkv, ng, dq, dk, dv, mg

def nsa_compress(kb, w1, b1, w2):
    hid = jax.nn.gelu(jnp.einsum('bnphd,pde->bnhe', kb, w1) + b1)
    return hid @ w2

def nsa_prepare(kv4, cmp_w1, cmp_b1, cmp_w2):
    B_, L = kv4.shape[:2]
    blocks = kv4.reshape(B_, L // NSA_BLOCK, NSA_BLOCK, 4, NSA_KV_HEADS, HD)
    ck = nsa_compress(blocks[:, :, :, 0], cmp_w1[0], cmp_b1[0], cmp_w2[0])
    cv = nsa_compress(blocks[:, :, :, 1], cmp_w1[1], cmp_b1[1], cmp_w2[1])
    ks_b = jnp.transpose(blocks[:, :, :, 2], (0, 3, 1, 2, 4))
    vs_b = jnp.transpose(blocks[:, :, :, 3], (0, 3, 1, 2, 4))
    return ck, cv, ks_b, vs_b

def nsa_cmp_sel(q, qpos, ck, cv, ks_b, vs_b, slopes):
    B_, nb = ck.shape[0], ck.shape[1]
    scale = HD ** -0.5
    blk = jnp.arange(nb, dtype=jnp.int32)
    dist_c = (qpos[:, None] - ((blk + 1) * NSA_BLOCK - 1)[None, :]).astype(jnp.float32)
    valid_c = dist_c >= 0.0
    s = jnp.einsum('bthgd,bnhd->bthgn', q, ck).astype(jnp.float32) * scale
    s = s - slopes[None, None, :, :, None] * dist_c[None, :, None, None, :]
    p_c = masked_softmax(s, valid_c[None, :, None, None, :], -1)
    o_c = jnp.einsum('bthgn,bnhd->bthgd', p_c.astype(cv.dtype), cv)
    cur = qpos // NSA_BLOCK
    imp = jnp.sum(p_c, axis=3)
    forced = (blk[None, :] == cur[:, None]) | (blk[None, :] == 0)
    allowed = blk[None, :] <= cur[:, None]
    imp = jnp.where(forced[None, :, None, :], FORCE_SCORE,
                    jnp.where(allowed[None, :, None, :], imp, -1.0))
    n_sel = min(NSA_TOPN, nb)
    top_v, top_i = lax.top_k(imp, n_sel)
    sel_ok = top_v >= 0.0
    bi = jnp.arange(B_)[:, None, None, None]
    hi = jnp.arange(NSA_KV_HEADS)[None, None, :, None]
    kg = ks_b[bi, hi, top_i]
    vg = vs_b[bi, hi, top_i]
    kpos = top_i[..., None] * NSA_BLOCK + jnp.arange(NSA_BLOCK, dtype=jnp.int32)
    dist_s = (qpos[None, :, None, None, None] - kpos).astype(jnp.float32)
    valid_s = sel_ok[..., None] & (dist_s >= 0.0)
    s2 = jnp.einsum('bthgd,bthjkd->bthgjk', q, kg).astype(jnp.float32) * scale
    s2 = s2 - slopes[None, None, :, :, None, None] * dist_s[:, :, :, None]
    p_s = masked_softmax(s2, valid_s[:, :, :, None], (-2, -1))
    o_s = jnp.einsum('bthgjk,bthjkd->bthgd', p_s.astype(vg.dtype), vg)
    return o_c, o_s

def window_attn(q, qpos, k, v, kpos, slopes):
    dist = qpos[:, None] - kpos[None, :]
    valid = (dist >= 0) & (dist < NSA_WINDOW) & (kpos[None, :] >= 0)
    s = jnp.einsum('bthgd,bshd->bthgs', q, k).astype(jnp.float32) * (HD ** -0.5)
    s = s - slopes[None, None, :, :, None] * dist.astype(jnp.float32)[None, :, None, None, :]
    p = masked_softmax(s, valid[None, :, None, None, :], -1)
    return jnp.einsum('bthgs,bshd->bthgd', p.astype(v.dtype), v)

def diff_lambda(lqk, lam_init):
    l = lqk.astype(jnp.float32)
    return jnp.exp(jnp.sum(l[0] * l[1])) - jnp.exp(jnp.sum(l[2] * l[3])) + lam_init

def diff_attn(q, k, v, qpos, kpos, lam, slopes):
    dist = qpos[:, None] - kpos[None, :]
    valid = dist >= 0
    s = jnp.einsum('bthcd,bshcd->bhcts', q, k).astype(jnp.float32) * (HD ** -0.5)
    s = s - slopes[None, :, None, None, None] * dist.astype(jnp.float32)[None, None, None]
    p = masked_softmax(s, valid[None, None, None], -1)
    a = p[:, :, 0] - lam * p[:, :, 1]
    return jnp.einsum('bhts,bshe->bthe', a.astype(v.dtype), v)

def gate_nsa(g, o_c, o_s, o_w):
    return g[..., 0:1] * o_c + g[..., 1:2] * o_s + g[..., 2:3] * o_w

def merge(o_nsa, o_diff, mg, P, lam_init):
    B_, T = o_diff.shape[:2]
    od = (rmsnorm(o_diff, P['g_diff_subln']) * (1.0 - lam_init)).reshape(B_, T, DIFF_HEADS * DIFF_VD)
    m = mg[:, :, 0] * (o_nsa @ P['w_up_nsa']) + mg[:, :, 1] * (od @ P['w_up_diff'])
    return m @ P['w_out']

def prompt_mix(h, P, lam_init):
    B_, T = h.shape[:2]
    nq, nkv, ng, dq, dk, dv, mg = project(h, P['w_in'])
    lam = diff_lambda(P['lambda_qk'], lam_init)
    nsl = alibi_slopes(NSA_HEADS).reshape(NSA_KV_HEADS, NSA_GROUP)
    dsl = alibi_slopes(DIFF_HEADS)
    ck, cv, ks_b, vs_b = nsa_prepare(nkv[:, :, :4], P['cmp_w1'], P['cmp_b1'], P['cmp_w2'])
    pad = ((0, 0), (NSA_WINDOW, 0), (0, 0), (0, 0))
    kw_pad = jnp.pad(nkv[:, :, 4], pad)
    vw_pad = jnp.pad(nkv[:, :, 5], pad)
    pos = jnp.arange(T, dtype=jnp.int32)

    def block(i):
        s0 = i * Q_BLOCK
        qpos = s0 + jnp.arange(Q_BLOCK, dtype=jnp.int32)
        qb = lax.dynamic_slice_in_dim(nq, s0, Q_BLOCK, axis=1)
        gb = lax.dynamic_slice_in_dim(ng, s0, Q_BLOCK, axis=1)
        o_c, o_s = nsa_cmp_sel(qb, qpos, ck, cv, ks_b, vs_b, nsl)
        kwb = lax.dynamic_slice_in_dim(kw_pad, s0, NSA_WINDOW + Q_BLOCK, axis=1)
        vwb = lax.dynamic_slice_in_dim(vw_pad, s0, NSA_WINDOW + Q_BLOCK, axis=1)
        kpos = s0 - NSA_WINDOW + jnp.arange(NSA_WINDOW + Q_BLOCK, dtype=jnp.int32)
        o_w = window_attn(qb, qpos, kwb, vwb, kpos, nsl)
        dqb = lax.dynamic_slice_in_dim(dq, s0, Q_BLOCK, axis=1)
        o_d = diff_attn(dqb, dk, dv, qpos, pos, lam, dsl)
        return gate_nsa(gb, o_c, o_s, o_w), o_d

    o_nsa, o_d = lax.map(block, jnp.arange(T // Q_BLOCK, dtype=jnp.int32))
    o_nsa = jnp.moveaxis(o_nsa, 0, 1).reshape(B_, T, NSA_HEADS * HD)
    o_d = jnp.moveaxis(o_d, 0, 1).reshape(B_, T, DIFF_HEADS, DIFF_VD)
    out = merge(o_nsa, o_d, mg, P, lam_init)
    w_rows = min(NSA_WINDOW, T)
    new_nsa = nkv[:, :, :4]
    new_diff = jnp.stack([dk.reshape(B_, T, DIFF_HEADS, 2 * HD), dv], axis=2)
    new_win = nkv[:, T - w_rows:, 4:]
    return out, (new_nsa, new_diff, new_win)

def sample_mix(h, c_nsa, c_diff, win, page_table, P, lam_init):
    Bd, Tn = h.shape[:2]
    past = page_table.shape[1] * c_nsa.shape[1]
    L = past + Tn
    Lp = -(-L // NSA_BLOCK) * NSA_BLOCK
    nq, nkv, ng, dq, dk, dv, mg = project(h, P['w_in'])
    lam = diff_lambda(P['lambda_qk'], lam_init)
    nsl = alibi_slopes(NSA_HEADS).reshape(NSA_KV_HEADS, NSA_GROUP)
    dsl = alibi_slopes(DIFF_HEADS)
    qpos = past + jnp.arange(Tn, dtype=jnp.int32)
    new_nsa = nkv[:, :, :4]
    full = jnp.concatenate([c_nsa[page_table].reshape(Bd, past, 4, NSA_KV_HEADS, HD), new_nsa], axis=1)
    full = jnp.pad(full, ((0, 0), (0, Lp - L), (0, 0), (0, 0), (0, 0)))
    ck, cv, ks_b, vs_b = nsa_prepare(full, P['cmp_w1'], P['cmp_b1'], P['cmp_w2'])
    o_c, o_s = nsa_cmp_sel(nq, qpos, ck, cv, ks_b, vs_b, nsl)
    wb = win.shape[1]
    kw = jnp.concatenate([win[:, :, 0], nkv[:, :, 4]], axis=1)
    vw = jnp.concatenate([win[:, :, 1], nkv[:, :, 5]], axis=1)
    kpos_w = past - wb + jnp.arange(wb + Tn, dtype=jnp.int32)
    o_w = window_attn(nq, qpos, kw, vw, kpos_w, nsl)
    o_nsa = gate_nsa(ng, o_c, o_s, o_w).reshape(Bd, Tn, NSA_HEADS * HD)
    new_diff = jnp.stack([dk.reshape(Bd, Tn, DIFF_HEADS, 2 * HD), dv], axis=2)
    full_d = jnp.concatenate([c_diff[page_table].reshape(Bd, past, 2, DIFF_HEADS, 2 * HD), new_diff], axis=1)
    kd = full_d[:, :, 0].reshape(Bd, L, DIFF_HEADS, 2, HD)
    vd = full_d[:, :, 1]
    o_d = diff_attn(dq, kd, vd, qpos, jnp.arange(L, dtype=jnp.int32), lam, dsl)
    out = merge(o_nsa, o_d, mg, P, lam_init)
    new_win = jnp.concatenate([win, nkv[:, :, 4:]], axis=1)[:, Tn:]
    return out, (new_nsa, new_diff, new_win)

def sandwich_layer(x, mix_fn, P):
    f1 = swiglu(rmsnorm(x, P['g_ffn1_pre']), P['ffn1_w1'], P['ffn1_w3'], P['ffn1_w2'])
    x = x + 0.5 * rmsnorm(f1, P['g_ffn1_post'])
    o, st = mix_fn(rmsnorm(x, P['g_mix_pre']))
    x = x + rmsnorm(o, P['g_mix_post'])
    f2 = swiglu(rmsnorm(x, P['g_ffn2_pre']), P['ffn2_w1'], P['ffn2_w3'], P['ffn2_w2'])
    x = x + 0.5 * rmsnorm(f2, P['g_ffn2_post'])
    return x, st

def setup_inputs(seed: int = 0) -> dict:
    key = jax.random.key(seed)
    k = jax.random.split(key, 40)
    f32 = jnp.float32

    def nrm(i, shape, scale):
        return scale * jax.random.normal(k[i], shape, f32)

    def gain(i, n):
        return 1.0 + 0.05 * jax.random.normal(k[i], (DEPTH, n), f32)

    n_pages = PAST_LEN // PAGE_SIZE
    n_used = DEC_BATCH * n_pages
    n_pool = (5 * n_used + 3) // 4
    page_table = jax.random.permutation(k[3], n_pool)[:n_used].reshape(DEC_BATCH, n_pages).astype(jnp.int32)
    win_buf = min(NSA_WINDOW, PAST_LEN)
    return {
        'x_prompt': nrm(0, (BATCH, SEQ, D_MODEL), 1.0),
        'x_sample': nrm(1, (DEC_BATCH, DEC_SEQ, D_MODEL), 1.0),
        'cache_nsa_kv': nrm(2, (DEPTH, n_pool, PAGE_SIZE, 4, NSA_KV_HEADS, HD), 1.0),
        'cache_diff_kv': nrm(4, (DEPTH, n_pool, PAGE_SIZE, 2, DIFF_HEADS, 2 * HD), 1.0),
        'state_win_kv': nrm(5, (DEPTH, DEC_BATCH, win_buf, 2, NSA_KV_HEADS, HD), 1.0),
        'page_table': page_table,
        'g_ffn1_pre': gain(6, D_MODEL),
        'ffn1_w1': nrm(7, (DEPTH, D_MODEL, D_FF), D_MODEL ** -0.5),
        'ffn1_w3': nrm(8, (DEPTH, D_MODEL, D_FF), D_MODEL ** -0.5),
        'ffn1_w2': nrm(9, (DEPTH, D_FF, D_MODEL), D_FF ** -0.5),
        'g_ffn1_post': gain(10, D_MODEL),
        'g_mix_pre': gain(11, D_MODEL),
        'w_in': nrm(12, (DEPTH, D_MODEL, IN_WIDTH), D_MODEL ** -0.5),
        'cmp_w1': nrm(13, (DEPTH, 2, NSA_BLOCK, HD, HD), (NSA_BLOCK * HD) ** -0.5),
        'cmp_b1': nrm(14, (DEPTH, 2, HD), 0.02),
        'cmp_w2': nrm(15, (DEPTH, 2, HD, HD), HD ** -0.5),
        'lambda_qk': nrm(16, (DEPTH, 4, HD), 0.1),
        'g_diff_subln': gain(17, DIFF_VD),
        'w_up_nsa': nrm(18, (DEPTH, NSA_HEADS * HD, D_MODEL), (NSA_HEADS * HD) ** -0.5),
        'w_up_diff': nrm(19, (DEPTH, DIFF_HEADS * DIFF_VD, D_MODEL), (DIFF_HEADS * DIFF_VD) ** -0.5),
        'w_out': nrm(20, (DEPTH, D_MODEL, D_MODEL), D_MODEL ** -0.5),
        'g_mix_post': gain(21, D_MODEL),
        'g_ffn2_pre': gain(22, D_MODEL),
        'ffn2_w1': nrm(23, (DEPTH, D_MODEL, D_FF), D_MODEL ** -0.5),
        'ffn2_w3': nrm(24, (DEPTH, D_MODEL, D_FF), D_MODEL ** -0.5),
        'ffn2_w2': nrm(25, (DEPTH, D_FF, D_MODEL), D_FF ** -0.5),
        'g_ffn2_post': gain(26, D_MODEL),
    }

def reference(x_prompt, x_sample, cache_nsa_kv, cache_diff_kv, state_win_kv, page_table,
              g_ffn1_pre, ffn1_w1, ffn1_w3, ffn1_w2, g_ffn1_post,
              g_mix_pre, w_in, cmp_w1, cmp_b1, cmp_w2, lambda_qk, g_diff_subln,
              w_up_nsa, w_up_diff, w_out, g_mix_post,
              g_ffn2_pre, ffn2_w1, ffn2_w3, ffn2_w2, g_ffn2_post):
    y_p, y_s = x_prompt, x_sample
    nsa_p, diff_p, win_p, nsa_s, diff_s, win_s = [], [], [], [], [], []
    for l in range(DEPTH):
        lam_init = 0.8 - 0.6 * math.exp(-0.3 * l)
        P = {
            'g_ffn1_pre': g_ffn1_pre[l], 'ffn1_w1': ffn1_w1[l], 'ffn1_w3': ffn1_w3[l],
            'ffn1_w2': ffn1_w2[l], 'g_ffn1_post': g_ffn1_post[l],
            'g_mix_pre': g_mix_pre[l], 'w_in': w_in[l], 'cmp_w1': cmp_w1[l],
            'cmp_b1': cmp_b1[l], 'cmp_w2': cmp_w2[l], 'lambda_qk': lambda_qk[l],
            'g_diff_subln': g_diff_subln[l], 'w_up_nsa': w_up_nsa[l],
            'w_up_diff': w_up_diff[l], 'w_out': w_out[l], 'g_mix_post': g_mix_post[l],
            'g_ffn2_pre': g_ffn2_pre[l], 'ffn2_w1': ffn2_w1[l], 'ffn2_w3': ffn2_w3[l],
            'ffn2_w2': ffn2_w2[l], 'g_ffn2_post': g_ffn2_post[l],
        }
        y_p, (a_p, b_p, c_p) = sandwich_layer(y_p, lambda h: prompt_mix(h, P, lam_init), P)
        y_s, (a_s, b_s, c_s) = sandwich_layer(
            y_s, lambda h: sample_mix(h, cache_nsa_kv[l], cache_diff_kv[l], state_win_kv[l],
                                      page_table, P, lam_init), P)
        nsa_p.append(a_p); diff_p.append(b_p); win_p.append(c_p)
        nsa_s.append(a_s); diff_s.append(b_s); win_s.append(c_s)
    return (y_p, y_s, jnp.stack(nsa_p), jnp.stack(nsa_s), jnp.stack(diff_p), jnp.stack(diff_s),
            jnp.stack(win_p), jnp.stack(win_s))


_drawn_inputs = setup_inputs


def setup_inputs(seed=0):
    import zlib

    import numpy as np

    out = dict(_drawn_inputs(seed))
    spreads = {}
    factors = {'cmp_b1': 8.0, 'g_ffn2_post': 3.533}
    for name, (base, spread) in spreads.items():
        noise = np.random.default_rng([zlib.crc32(name.encode()), seed]).standard_normal(out[name].shape)
        drawn = base * np.exp(spread * noise) if base else spread * noise
        out[name] = __import__('jax').numpy.asarray(drawn.astype(out[name].dtype))
    for name, factor in factors.items():
        out[name] = (out[name] * factor).astype(out[name].dtype)
    return out
```

```python
from contextlib import ExitStack

import concourse.bass as bass
from concourse import mybir

F32 = mybir.dt.float32
F32R = mybir.dt.float32r
I32 = mybir.dt.int32
ALU = mybir.AluOpType
ACT = mybir.ActivationFunctionType
AX = mybir.AxisListType.X

P = 128
D = 1024
KD = D // P
SEQ = 1024
NB = 8
TS = 8
NS = NB * TS
NCH = 3
CH = 364
NT = NCH * CH
D_FF = 2816
KF = D_FF // P
EPS = 1e-6
PAIRS = ((0, 0), (0, 1), (1, 0))


class Parts:
    pass


def sem_maker(nc, ctx, stage):
    made = []

    def give_back():
        nc.clear_and_free_semaphores(made)
        nc.all_engine_barrier()

    ctx.callback(give_back)

    def sem(name):
        made.append(nc.alloc_semaphore(f"{stage}_{name}"))
        return made[-1]
    return sem


def chunks(ap):
    return ap.rearrange("p (c n) -> p c n", c=NCH)


def load_tokens(nc, G):
    tiles = SEQ // P + 1
    with ExitStack() as ctx:
        sem = sem_maker(nc, ctx, "lt")
        rows = ctx.enter_context(nc.sbuf_tensor("lt_rows", [P, tiles, D], F32))
        row_in = [sem(f"row_in{i}") for i in range(tiles)]
        const_in, const_set, transposed, evacuated = sem("const_in"), sem("const_set"), sem("transposed"), sem("evacuated")
        block = ctx.enter_context(nc.Block())

        def size(i):
            return P if i < tiles - 1 else NS

        @block.sync
        def _(sp):
            sp.dma_start(G.ident[:], G.c_ident).then_inc(const_in, 16)
            for i in range(tiles):
                src = G.x_prompt[i * P:(i + 1) * P, :] if i < tiles - 1 else G.x_sample
                sp.dma_start(rows[0:size(i), i, :], src).then_inc(row_in[i], 16)

        @block.gpsimd
        def _(pool):
            pool.memset(G.ones[:], 1.0).then_inc(const_set, 1)
            pool.memset(G.eps[:], EPS).then_inc(const_set, 1)
            pool.memset(G.xT[:, :, SEQ + NS:NT], 0.0).then_inc(const_set, 1)

        @block.tensor
        def _(pe):
            pe.wait_ge(const_in, 16)
            for i in range(tiles):
                pe.wait_ge(row_in[i], 16)
                for half in range(2):
                    n = 2 * i + half
                    if n >= 2:
                        pe.wait_ge(evacuated, n - 1)
                    for j in range(4):
                        k = 4 * half + j
                        last = pe.transpose(G.ps[:, n % 2, j * P:j * P + size(i)], rows[0:size(i), i, k * P:(k + 1) * P],
                                            G.ident[0:size(i), 0:size(i)])
                    last.then_inc(transposed, 1)

        @block.vector
        def _(dve):
            for i in range(tiles):
                for half in range(2):
                    n = 2 * i + half
                    dve.wait_ge(transposed, n + 1)
                    src = G.ps[:, n % 2, :].rearrange("p (j t) -> p j t", j=4)[:, :, 0:size(i)]
                    dve.tensor_copy(G.xT[:, 4 * half:4 * half + 4, i * P:i * P + size(i)], src).then_inc(evacuated, 1)
            dve.wait_ge(const_set, 3)


def rms_engines(nc, G, sem, src, tmp):
    squared, gathered, summed, rooted, scale_ready = (sem(x) for x in ("squared", "gathered", "summed", "rooted", "scale_ready"))

    def act_part(act):
        for k in range(KD):
            if k >= 3:
                act.wait_ge(gathered, k - 2)
            act.activation(tmp[k % 2][:] if k else G.rms[:], src[:, k, :], ACT.Square).then_inc(squared, 1)
        act.wait_ge(summed, 1)
        act.activation(chunks(G.rms[:]), G.ps[:, 0:NCH, 0:CH], ACT.Sqrt, bias=G.eps[:], scale=1.0 / D).then_inc(rooted, 1)

    def pe_part(pe):
        pe.wait_ge(gathered, KD - 1)
        for c in range(NCH):
            last = pe.matmul(G.ps[:, c, 0:CH], G.ones[:], G.rms[:, c * CH:(c + 1) * CH], start=True, stop=True)
        last.then_inc(summed, 1)

    def dve_part(dve):
        for k in range(1, KD):
            dve.wait_ge(squared, k + 1)
            if k >= 2:
                dve.wait_ge(gathered, k - 1)
            dve.tensor_tensor(G.rms[:], G.rms[:], tmp[k % 2][:], ALU.add).then_inc(gathered, 1)
        dve.wait_ge(rooted, 1)
        dve.reciprocal(G.rms[:], G.rms[:]).then_inc(scale_ready, 1)

    return act_part, pe_part, dve_part, scale_ready


def norm_split(nc, G, stage, gain, hh, hl, tmp):
    with ExitStack() as ctx:
        sem = sem_maker(nc, ctx, stage)
        act_part, pe_part, dve_part, scale_ready = rms_engines(nc, G, sem, G.xT, tmp)
        gain_in, normed, high = sem("gain_in"), sem("normed"), sem("high")
        low = [sem("low_even"), sem("low_odd")]
        block = ctx.enter_context(nc.Block())

        @block.sync
        def _(sp):
            sp.dma_start(G.gain[:], gain).then_inc(gain_in, 16)

        @block.scalar
        def _(act):
            act_part(act)
            for k in range(KD):
                act.wait_ge(normed, k + 1)
                act.activation(hh[:, k, :], tmp[k % 2][:], ACT.Copy).then_inc(high, 1)

        @block.tensor
        def _(pe):
            pe_part(pe)

        def lo(eng, k):
            eng.wait_ge(high, k + 1)
            eng.tensor_tensor(hl[:, k, :], tmp[k % 2][:], hh[:, k, :].bitcast(F32), ALU.subtract).then_inc(low[k % 2], 1)

        @block.gpsimd
        def _(pool):
            for k in range(1, KD, 2):
                lo(pool, k)

        @block.vector
        def _(dve):
            dve_part(dve)
            dve.wait_ge(gain_in, 16)
            dve.wait_ge(scale_ready, 1)
            for k in range(KD):
                if k >= 2:
                    dve.wait_ge(low[k % 2], k // 2)
                dve.scalar_tensor_tensor(tmp[k % 2][:], G.xT[:, k, :], G.gain[:, k:k + 1], G.rms[:],
                                         ALU.mult, ALU.mult).then_inc(normed, 1)
                if k % 2:
                    lo(dve, k - 1)


def norm_add(nc, G, stage, gain, src, factor, tmp):
    with ExitStack() as ctx:
        sem = sem_maker(nc, ctx, stage)
        act_part, pe_part, dve_part, scale_ready = rms_engines(nc, G, sem, src, tmp)
        gain_in, gain_scaled, normed = sem("gain_in"), sem("gain_scaled"), sem("normed")
        added = [sem("added_even"), sem("added_odd")]
        block = ctx.enter_context(nc.Block())

        @block.sync
        def _(sp):
            sp.dma_start(G.gain[:], gain).then_inc(gain_in, 16)

        @block.scalar
        def _(act):
            act_part(act)

        @block.tensor
        def _(pe):
            pe_part(pe)

        def add(eng, k):
            eng.wait_ge(normed, k + 1)
            eng.tensor_tensor(G.xT[:, k, :], G.xT[:, k, :], tmp[k % 2][:], ALU.add).then_inc(added[k % 2], 1)

        @block.gpsimd
        def _(pool):
            for k in range(1, KD, 2):
                add(pool, k)

        @block.vector
        def _(dve):
            dve.wait_ge(gain_in, 16)
            dve.tensor_scalar(G.gain[:], G.gain[:], factor, None, ALU.mult).then_inc(gain_scaled, 1)
            dve_part(dve)
            dve.wait_ge(gain_scaled, 1)
            dve.wait_ge(scale_ready, 1)
            for k in range(KD):
                if k >= 2:
                    dve.wait_ge(added[k % 2], k // 2)
                dve.scalar_tensor_tensor(tmp[k % 2][:], src[:, k, :], G.gain[:, k:k + 1], G.rms[:],
                                         ALU.mult, ALU.mult).then_inc(normed, 1)
                if k % 2:
                    add(dve, k - 1)


def ffn(nc, G, stage, w1, w3, w2, g_pre, g_post):
    rounds = KF // 2
    with ExitStack() as ctx:
        def sb(name, shape, dt):
            return ctx.enter_context(nc.sbuf_tensor(f"{stage}_{name}", shape, dt))
        hh, hl = sb("hh", [P, KD, NT], F32R), sb("hl", [P, KD, NT], F32R)
        tmp = [sb(f"tmp{i}", [P, NT], F32) for i in range(2)]
        f = sb("f", [P, KD, NT], F32)
        norm_split(nc, G, f"{stage}n", g_pre, hh, hl, tmp)
        with ExitStack() as inner:
            def sbi(name, shape, dt):
                return inner.enter_context(nc.sbuf_tensor(f"{stage}_{name}", shape, dt))
            raw = sbi("raw", [P, 3, D], F32)
            wh, wl = sbi("wh", [P, 3, D], F32R), sbi("wl", [P, 3, D], F32R)
            uh, ul = sbi("uh", [P, 2, NT], F32R), sbi("ul", [P, 2, NT], F32R)
            gate, u = chunks(tmp[0][:]), chunks(tmp[1][:])
            sem = sem_maker(nc, inner, stage)
            raw_in = [sem(f"raw_in{i}") for i in range(3)]
            w_high, w_split = sem("w_high"), sem("w_split")
            up1_ready, up3_ready, gated, u_made, u_high, u_split = (
                sem("up1_ready"), sem("up3_ready"), sem("gated"), sem("u_made"), sem("u_high"), sem("u_split"))
            down_ready, f_cleared = sem("down_ready"), sem("f_cleared")
            down_added = [sem("down_added_even"), sem("down_added_odd")]
            block = inner.enter_context(nc.Block())
            w = (wh, wl)
            h = (hh, hl)
            uu = (uh, ul)

            def piece_source(g, j):
                if j < 4:
                    wt = (w1, w3)[j % 2]
                    return wt[:, bass.ds((g * 2 + j // 2) * P, P)].rearrange("(k p) n -> p k n", p=P)
                return w2[bass.ds((g * 2 + j - 4) * P, P), :]

            def piece_buffer(buf, j):
                if j < 4:
                    return buf[:, j % 3, :].rearrange("p (k n) -> p k n", k=KD)
                return buf[:, j % 3, :]

            @block.sync
            def _(sp):
                for j in range(3):
                    sp.dma_start(piece_buffer(raw, j), piece_source(0, j)).then_inc(raw_in[j], 16)
                with sp.Fori(0, rounds - 1) as g:
                    for n in range(3, 9):
                        j = n % 6
                        sp.wait_ge(w_split, g * 6 + n - 2)
                        sp.dma_start(piece_buffer(raw, j), piece_source(g + n // 6, j)).then_inc(raw_in[n % 3], 16)
                for j in range(3, 6):
                    sp.wait_ge(w_split, (rounds - 1) * 6 + j - 2)
                    sp.dma_start(piece_buffer(raw, j), piece_source(rounds - 1, j)).then_inc(raw_in[j % 3], 16)

            @block.gpsimd
            def _(pool):
                pool.memset(f[:], 0.0).then_inc(f_cleared, 1)

            @block.scalar
            def _(act):
                def w_hi(g, j):
                    act.wait_ge(raw_in[j % 3], g * 32 + 16 * (j // 3 + 1))
                    freed, value = ((up3_ready, g * 6), (down_ready, g * KD), (down_ready, g * KD),
                                    (up1_ready, g * 6 + 3), (up3_ready, g * 6 + 3), (up1_ready, g * 6 + 6))[j]
                    act.wait_ge(freed, value)
                    act.activation(wh[:, j % 3, :], raw[:, j % 3, :], ACT.Copy).then_inc(w_high, 1)

                def silu(g, m, c):
                    act.wait_ge(up1_ready, g * 6 + m * NCH + c + 1)
                    act.wait_ge(u_made, g * 6 + m * (c + 1))
                    act.activation(gate[:, c, :], G.ps[:, c, 0:CH], ACT.Silu).then_inc(gated, 1)

                def u_hi(g, m, c):
                    act.wait_ge(u_made, g * 6 + m * NCH + c + 1)
                    act.activation(chunks(uh[:, m, :])[:, c, :], u[:, c, :], ACT.Copy).then_inc(u_high, 1)

                with act.Fori(0, rounds) as g:
                    for j in range(3):
                        w_hi(g, j)
                    for m in range(2):
                        for c in range(NCH):
                            silu(g, m, c)
                        for j in ((3,), (4, 5))[m]:
                            w_hi(g, j)
                        for c in range(NCH):
                            u_hi(g, m, c)

            @block.vector
            def _(dve):
                def w_lo(g, j):
                    dve.wait_ge(w_high, g * 6 + j + 1)
                    dve.tensor_tensor(wl[:, j % 3, :], raw[:, j % 3, :], wh[:, j % 3, :].bitcast(F32),
                                      ALU.subtract).then_inc(w_split, 1)

                def u_mul(g, m, c):
                    n = m * NCH + c
                    dve.wait_ge(up3_ready, g * 6 + n + 1)
                    dve.wait_ge(gated, g * 6 + n + 1)
                    dve.wait_ge(u_split, g * 6 + m * (c + 1))
                    dve.tensor_tensor(u[:, c, :], gate[:, c, :], G.ps[:, 3 + c, 0:CH], ALU.mult).then_inc(u_made, 1)

                def u_lo(g, m, c):
                    dve.wait_ge(u_high, g * 6 + m * NCH + c + 1)
                    dve.tensor_tensor(chunks(ul[:, m, :])[:, c, :], u[:, c, :], chunks(uh[:, m, :])[:, c, :].bitcast(F32),
                                      ALU.subtract).then_inc(u_split, 1)

                dve.wait_ge(f_cleared, 1)
                with dve.Fori(0, rounds) as g:
                    for j in range(3):
                        w_lo(g, j)
                    for m in range(2):
                        for j in ((3,), (4, 5))[m]:
                            w_lo(g, j)
                        for c in range(NCH):
                            u_mul(g, m, c)
                            if c > 0:
                                u_lo(g, m, c - 1)
                        u_lo(g, m, NCH - 1)
                    for o in range(KD):
                        dve.wait_ge(down_ready, g * KD + o + 1)
                        acc = chunks(f[:, o, :])
                        s = 3 * (o % 2)
                        dve.tensor_tensor(acc, G.ps[:, s:s + NCH, 0:CH], acc, ALU.add).then_inc(down_added[o % 2], 1)

            @block.tensor
            def _(pe):
                def up(g, j):
                    s = 3 * (j % 2)
                    pe.wait_ge(w_split, g * 6 + j + 1)
                    if j < 2:
                        pe.wait_ge(down_added[j], g * (KD // 2))
                    for c in range(NCH):
                        if j == 2:
                            pe.wait_ge(gated, g * 6 + c + 1)
                        if j == 3:
                            pe.wait_ge(u_made, g * 6 + c + 1)
                        for k in range(KD):
                            for n, (a, b) in enumerate(PAIRS):
                                last = pe.matmul(G.ps[:, s + c, 0:CH], w[a][:, j % 3, k * P:(k + 1) * P],
                                                 h[b][:, k, c * CH:(c + 1) * CH],
                                                 start=(k == 0 and n == 0), stop=(k == KD - 1 and n == 2))
                        last.then_inc((up1_ready, up3_ready)[j % 2], 1)

                def down(g, o):
                    s = 3 * (o % 2)
                    if o >= 2:
                        pe.wait_ge(down_added[o % 2], g * (KD // 2) + o // 2)
                    for m in range(2):
                        if o == 0:
                            pe.wait_ge(w_split, g * 6 + 5 + m)
                        for c in range(NCH):
                            if o == 0:
                                pe.wait_ge(u_split, g * 6 + m * NCH + c + 1)
                                if m == 0:
                                    pe.wait_ge(gated, g * 6 + NCH + c + 1)
                            if o == 1 and m == 0:
                                pe.wait_ge(u_made, g * 6 + NCH + c + 1)
                            for n, (a, b) in enumerate(PAIRS):
                                last = pe.matmul(G.ps[:, s + c, 0:CH], w[a][:, (4 + m) % 3, o * P:(o + 1) * P],
                                                 uu[b][:, m, c * CH:(c + 1) * CH],
                                                 start=(m == 0 and n == 0), stop=(m == 1 and n == 2))
                    last.then_inc(down_ready, 1)

                with pe.Fori(0, rounds) as g:
                    for j in range(4):
                        up(g, j)
                    for o in range(KD):
                        down(g, o)
        norm_add(nc, G, f"{stage}p", g_post, f, 0.5, tmp)


NSA_H, KVH, GRP, HD, DIFF_H = 8, 2, 4, 64, 4
Z_NQ, Z_NKV, Z_DQ, Z_DK, Z_DV, Z_MG, Z_NG = 0, 4, 10, 14, 18, 22, 38
N_GATE = 3 * NSA_H
NG_COL = 10 * P


def project(nc, G):
    with ExitStack() as ctx:
        def sb(name, shape, dt):
            return ctx.enter_context(nc.sbuf_tensor(f"pj_{name}", shape, dt))
        hh, hl = sb("hh", [P, KD, NT], F32R), sb("hl", [P, KD, NT], F32R)
        tmp = [sb(f"tmp{i}", [P, NT], F32) for i in range(2)]
        norm_split(nc, G, "pjn", G.gains["g_mix_pre"], hh, hl, tmp)
        raw = sb("raw", [P, 2, D], F32)
        wh, wl = sb("wh", [P, 2, D], F32R), sb("wl", [P, 2, D], F32R)
        z = sb("z", [P, 2, NT], F32)
        sem = sem_maker(nc, ctx, "pj")
        raw_in, w_high, w_split, z_ready, z_copied, z_out = (
            [sem(f"{what}{j}") for j in range(2)] for what in ("raw_in", "w_high", "w_split", "z_ready", "z_copied", "z_out"))
        x_stored = sem("x_stored")
        w, h = (wh, wl), (hh, hl)
        block = ctx.enter_context(nc.Block())
        before = NG_COL // P // 2
        rounds = Z_NG // 2

        @block.sync
        def _(sp):
            for k in range(KD):
                sp.dma_start(G.x_kept[k], G.xT[:, k, :]).then_inc(x_stored, 16)

            def load(g, j, skipped, cols):
                sp.wait_ge(w_split[j], g)
                sp.dma_start(raw[:, j, 0:KD * cols].rearrange("p (k n) -> p k n", k=KD),
                             G.w_in[:, bass.ds(g * (2 * P) + (j * P + skipped), cols)].rearrange("(k p) n -> p k n", p=P)
                             ).then_inc(raw_in[j], 16)

            for first, end, skipped in ((0, before, 0), (before, rounds, N_GATE)):
                with sp.Fori(first, end) as g:
                    for j in range(2):
                        load(g, j, skipped, P)
            sp.wait_ge(w_split[0], rounds)
            sp.dma_start(raw[:, 0, 0:KD * N_GATE].rearrange("p (k n) -> p k n", k=KD),
                         G.w_in[:, NG_COL:NG_COL + N_GATE].rearrange("(k p) n -> p k n", p=P)).then_inc(raw_in[0], 16)
            sp.wait_ge(x_stored, 16 * KD)

        @block.gpsimd
        def _(pool):
            with pool.Fori(0, rounds) as g:
                for j in range(2):
                    pool.wait_ge(z_copied[j], g + 1)
                    pool.dma_start(G.z[bass.ds(g * 2 + j, 1), :, :].rearrange("a p n -> (a p) n"), z[:, j, :]).then_inc(z_out[j], 16)
            pool.wait_ge(z_copied[0], rounds + 1)
            pool.dma_start(G.z[Z_NG, 0:N_GATE, :], z[0:N_GATE, 0, :]).then_inc(z_out[0], 16)
            pool.wait_ge(z_out[0], 16 * (rounds + 1))
            pool.wait_ge(z_out[1], 16 * rounds)

        @block.scalar
        def _(act):
            def hi(g, j):
                act.wait_ge(raw_in[j], (g + 1) * 16)
                act.wait_ge(z_ready[j], g)
                act.activation(wh[:, j, :], raw[:, j, :], ACT.Copy).then_inc(w_high[j], 1)

            def send(g, j, rows):
                act.wait_ge(z_ready[j], g + 1)
                act.wait_ge(z_out[j], g * 16)
                act.activation(chunks(z[0:rows, j, :]), G.ps[0:rows, 3 * j:3 * j + NCH, 0:CH], ACT.Copy).then_inc(z_copied[j], 1)

            hi(0, 0)
            hi(0, 1)
            with act.Fori(0, rounds - 1) as g:
                for j in range(2):
                    send(g, j, P)
                    hi(g + 1, j)
            send(rounds - 1, 0, P)
            hi(rounds, 0)
            send(rounds - 1, 1, P)
            send(rounds, 0, N_GATE)

        @block.vector
        def _(dve):
            def lo(g, j):
                dve.wait_ge(w_high[j], g + 1)
                dve.tensor_tensor(wl[:, j, :], raw[:, j, :], wh[:, j, :].bitcast(F32), ALU.subtract).then_inc(w_split[j], 1)

            with dve.Fori(0, rounds) as g:
                lo(g, 0)
                lo(g, 1)
            lo(rounds, 0)

        @block.tensor
        def _(pe):
            def tile(g, j, cols):
                pe.wait_ge(w_split[j], g + 1)
                pe.wait_ge(z_copied[j], g)
                for c in range(NCH):
                    for k in range(KD):
                        for n, (a, b) in enumerate(PAIRS):
                            last = pe.matmul(G.ps[0:cols, 3 * j + c, 0:CH], w[a][:, j, k * cols:(k + 1) * cols],
                                             h[b][:, k, c * CH:(c + 1) * CH],
                                             start=(k == 0 and n == 0), stop=(k == KD - 1 and n == 2))
                last.then_inc(z_ready[j], 1)

            with pe.Fori(0, rounds) as g:
                tile(g, 0, P)
                tile(g, 1, P)
            tile(rounds, 0, N_GATE)


TOK = 14
WIN = 512


def token_rows(nc, G):
    tiles = SEQ // P + 1
    with ExitStack() as ctx:
        feat = ctx.enter_context(nc.sbuf_tensor("tr_feat", [P, TOK, SEQ + NS], F32))
        rows = ctx.enter_context(nc.sbuf_tensor("tr_rows", [P, 3, TOK * P], F32))
        sem = sem_maker(nc, ctx, "tr")
        feat_in, window_moved, transposed = sem("feat_in"), sem("window_moved"), sem("transposed")
        copied = [sem("copied_act"), sem("copied_dve")]
        rows_out = [sem(f"rows_out{i}") for i in range(3)]
        block = ctx.enter_context(nc.Block())
        groups = (TOK + 3) // 4

        def size(i):
            return P if i < tiles - 1 else NS

        def in_group(q):
            return min(4, TOK - 4 * q)

        @block.gpsimd
        def _(pool):
            pool.dma_start(G.win_s[:, 0:WIN - TS, :], G.win[:, TS:WIN, :]).then_inc(window_moved, 16)
            pool.wait_ge(window_moved, 16)

        @block.sync
        def _(sp):
            sp.dma_start(feat[:, 0:6, :], G.z[Z_NKV:Z_NKV + 6, :, 0:SEQ + NS].rearrange("m p n -> p m n")).then_inc(feat_in, 16)
            sp.dma_start(feat[:, 6:TOK, :], G.z[Z_DK:Z_DK + 8, :, 0:SEQ + NS].rearrange("m p n -> p m n")).then_inc(feat_in, 16)
            stores = [0, 0, 0]
            for i in range(tiles):
                for a in range(2):
                    sp.wait_ge(copied[a], (i + 1) * (groups // 2))
                r = rows[0:size(i), i % 3, :]
                if i < tiles - 1:
                    t = slice(i * P, (i + 1) * P)
                    outs = [(G.nsa_p[t, :], r[:, 0:512]), (G.diff_p[t, :], r[:, 768:1792])]
                    if i >= tiles - 1 - WIN // P:
                        o = i * P - (SEQ - WIN)
                        outs.append((G.win_p[o:o + P, :], r[:, 512:768]))
                else:
                    outs = [(G.nsa_s, r[:, 0:512]), (G.diff_s, r[:, 768:1792])]
                    outs += [(G.win_s[b, WIN - TS:WIN, :], rows[b * TS:(b + 1) * TS, i % 3, 512:768]) for b in range(NB)]
                for dst, src in outs + [(G.kvw[i * P:i * P + size(i), :], r[:, 512:768])]:
                    sp.dma_start(dst, src).then_inc(rows_out[i % 3], 16)
                    stores[i % 3] += 1
                G.tr_stores[i] = stores[i % 3]
            for i in range(3):
                sp.wait_ge(rows_out[i], 16 * stores[i])

        @block.tensor
        def _(pe):
            pe.wait_ge(feat_in, 32)
            n = 0
            for i in range(tiles):
                for q in range(groups):
                    if n >= 2:
                        pe.wait_ge(copied[n % 2], n // 2)
                    for j in range(in_group(q)):
                        last = pe.transpose(G.ps[0:size(i), n % 2, j * P:(j + 1) * P], feat[:, 4 * q + j, i * P:i * P + size(i)],
                                            G.ident[:])
                    last.then_inc(transposed, 1)
                    n += 1

        def copy_groups(eng, parity, copy):
            stores = {}
            for i in range(tiles):
                for q in range(parity, groups, 2):
                    n = i * groups + q
                    eng.wait_ge(transposed, n + 1)
                    if i >= 3 and q == parity:
                        eng.wait_ge(rows_out[i % 3], 16 * G.tr_stores[i - 3])
                    w = in_group(q) * P
                    copy(rows[0:size(i), i % 3, 4 * q * P:4 * q * P + w], G.ps[0:size(i), n % 2, 0:w]).then_inc(copied[parity], 1)

        @block.scalar
        def _(act):
            copy_groups(act, 0, lambda dst, src: act.activation(dst, src, ACT.Copy))

        @block.vector
        def _(dve):
            copy_groups(dve, 1, lambda dst, src: dve.tensor_copy(dst, src))


TILES = SEQ // P
VD = 2 * HD
LAM_INIT = 0.2


def lambda_scale(nc, G):
    with ExitStack() as ctx:
        sem = sem_maker(nc, ctx, "lam")
        l = ctx.enter_context(nc.sbuf_tensor("lam_l", [P, 2, 2, HD], F32))
        dots = ctx.enter_context(nc.sbuf_tensor("lam_dots", [P, 2], F32))
        l_in, stepped, exped = sem("l_in"), sem("stepped"), sem("exped")
        block = ctx.enter_context(nc.Block())

        @block.sync
        def _(sp):
            sp.dma_start(l[:].rearrange("p a b d -> p (a b d)"), G.lambda_qk.rearrange("(o a) d -> o (a d)", o=1).to_broadcast([P, 4 * HD])).then_inc(l_in, 16)

        @block.vector
        def _(dve):
            dve.wait_ge(l_in, 16)
            dve.tensor_tensor(l[:, :, 0, :], l[:, :, 0, :], l[:, :, 1, :], ALU.mult).then_inc(stepped, 1)
            dve.wait_ge(stepped, 1)
            dve.tensor_reduce(dots[:], l[:, :, 0, :], AX, ALU.add).then_inc(stepped, 1)
            dve.wait_ge(exped, 1)
            dve.tensor_tensor(G.nlam[:], dots[:, 1:2], dots[:, 0:1], ALU.subtract).then_inc(stepped, 1)
            dve.wait_ge(stepped, 3)
            dve.tensor_scalar(G.nlam[:], G.nlam[:], -LAM_INIT, None, ALU.add).then_inc(stepped, 1)

        @block.scalar
        def _(act):
            act.wait_ge(stepped, 2)
            act.activation(dots[:], dots[:], ACT.Exp).then_inc(exped, 1)


def prompt_diff(nc, G):
    with ExitStack() as ctx:
        def sb(name, shape, dt=F32):
            return ctx.enter_context(nc.sbuf_tensor(f"pd_{name}", shape, dt))
        q, k, v = sb("q", [P, 2, 2, SEQ]), sb("k", [P, 2, SEQ]), sb("v", [P, 2, TILES, VD])
        bias = sb("bias", [P, 2, SEQ])
        probs = sb("probs", [P, 4, 2, SEQ])
        carrier = sb("carrier", [P, 2 * 2 * TILES])
        aT = sb("aT", [P, 2, SEQ])
        nmax, total, inv = sb("nmax", [P, 4, 2]), sb("total", [P, 4, 2]), sb("inv", [P, 4, 2])
        sem = sem_maker(nc, ctx, "pd")
        head_in = [sem(f"head_in{j}") for j in range(2)]
        q_scaled = sem("q_scaled")
        s_ready, biased, exped = ([sem(f"{what}{c}") for c in range(2)] for what in ("s_ready", "biased", "exped"))
        q_cleared, bias_made = sem("q_cleared"), sem("bias_made")
        inverted, weighed, scaled, combined = sem("inverted"), sem("weighed"), sem("scaled"), sem("combined")
        t_ready, t_copied, pv_done, o_copied = sem("t_ready"), sem("t_copied"), sem("pv_done"), sem("o_copied")
        block = ctx.enter_context(nc.Block())
        U = 2 * TILES
        rounds = DIFF_H // 2

        @block.gpsimd
        def _(pool):
            pool.memset(q[HD:P, :, 0, :], 0.0).then_inc(q_cleared, 1)
            pool.memset(q[0:HD, :, 1, :], 0.0).then_inc(q_cleared, 1)

        @block.sync
        def _(sp):
            for h in range(DIFF_H):
                if h >= 2:
                    sp.wait_ge(pv_done, (h - 1) * TILES)
                j = h % 2
                sp.dma_start(q[0:HD, j, 0, :], G.z[Z_DQ + h, 0:HD, 0:SEQ]).then_inc(head_in[j], 16)
                sp.dma_start(q[HD:P, j, 1, :], G.z[Z_DQ + h, HD:P, 0:SEQ]).then_inc(head_in[j], 16)
                sp.dma_start(k[:, j, :], G.z[Z_DK + h, :, 0:SEQ]).then_inc(head_in[j], 16)
                sp.dma_start(v[:, j, :, :], G.diff_p[:, 512 + h * VD:512 + (h + 1) * VD].rearrange("(i p) d -> p i d", p=P)).then_inc(head_in[j], 16)

        @block.tensor
        def _(pe):
            def scores(g, u, c):
                i, j = u % TILES, u // TILES
                n = (i + 1) * P
                if i == 0 and c == 0:
                    pe.wait_ge(q_scaled, g * 2 + j + 1)
                pe.wait_ge(biased[c], g * U + u)
                for n0 in range(0, n, 512):
                    m = min(512, n - n0)
                    last = pe.matmul(G.ps[:, 2 * c + n0 // 512, 0:m], q[:, j, c, i * P:(i + 1) * P], k[:, j, n0:n0 + m],
                                     start=True, stop=True)
                last.then_inc(s_ready[c], 1)

            def turn(g, u):
                pe.wait_ge(combined, g * U + u + 1)
                pe.wait_ge(t_copied, g * U + u)
                for t in range(u % TILES + 1):
                    last = pe.transpose(G.ps[:, 4 + t // 4, (t % 4) * P:(t % 4 + 1) * P], probs[:, u % 4, 0, t * P:(t + 1) * P], G.ident[:])
                last.then_inc(t_ready, 1)

            def values(g, u):
                i, j = u % TILES, u // TILES
                pe.wait_ge(t_copied, g * U + u + 1)
                pe.wait_ge(o_copied, g * U + max(u - 1, 0))
                for t in range(i + 1):
                    last = pe.matmul(G.ps[:, 6 + u % 2, 0:VD], aT[:, u % 2, t * P:(t + 1) * P], v[:, j, t, :], start=(t == 0), stop=(t == i))
                last.then_inc(pv_done, 1)

            with pe.Fori(0, rounds) as g:
                for u in range(U + 2):
                    if u < U:
                        scores(g, u, 0)
                    if u >= 2:
                        turn(g, u - 2)
                    if u < U:
                        scores(g, u, 1)
                    if u >= 2:
                        values(g, u - 2)

        @block.vector
        def _(dve):
            def negated_scores(g, u, c):
                i, j = u % TILES, u // TILES
                n = (i + 1) * P
                if i == 0 and c == 0:
                    dve.wait_ge(bias_made, g * 2 + j + 1)
                    dve.wait_ge(head_in[j], g * 64 + 64)
                    dve.wait_ge(q_cleared, 2)
                    dve.tensor_scalar(q[:, j, :, :], q[:, j, :, :], -HD ** -0.5, None, ALU.mult).then_inc(q_scaled, 1)
                dve.wait_ge(s_ready[c], g * U + u + 1)
                if c == 0:
                    dve.wait_ge(t_ready, g * U + max(u - 3, 0))
                    dve.wait_ge(combined, g * U + max(u - 3, 0))
                dve.memset(carrier[:, 2 * u + c:2 * u + c + 1], 0.0)
                dve.tensor_tensor_reduce(out=probs[:, u % 4, c, 0:n], in0=G.ps[:, 2 * c:2 * c + 2, :].rearrange("p a n -> p (a n)")[:, 0:n],
                                         in1=bias[:, j, SEQ - n:SEQ], scale=1.0, scalar=3e38, op0=ALU.add, op1=ALU.min,
                                         accum_out=nmax[:, u % 4, c:c + 1]).then_inc(biased[c], 1)

            def combine(g, u):
                n = (u % TILES + 1) * P
                p0, p1 = probs[:, u % 4, 0, 0:n], probs[:, u % 4, 1, 0:n]
                for c in range(2):
                    dve.wait_ge(exped[c], g * U + u + 1)
                dve.reciprocal(inv[:, u % 4, :], total[:, u % 4, :]).then_inc(inverted, 1)
                dve.wait_ge(inverted, g * U + u + 1)
                dve.tensor_scalar(p0, p0, inv[:, u % 4, 0:1], None, ALU.mult).then_inc(scaled, 1)
                dve.tensor_tensor(inv[:, u % 4, 1:2], inv[:, u % 4, 1:2], G.nlam[:], ALU.mult).then_inc(weighed, 1)
                dve.wait_ge(scaled, g * U + u + 1)
                dve.wait_ge(weighed, g * U + u + 1)
                dve.scalar_tensor_tensor(p0, p1, inv[:, u % 4, 1:2], p0, ALU.mult, ALU.add).then_inc(combined, 1)

            with dve.Fori(0, rounds) as g:
                for u in range(U + 1):
                    if u < U:
                        negated_scores(g, u, 0)
                    if u >= 1:
                        combine(g, u - 1)
                    if u < U:
                        negated_scores(g, u, 1)

        @block.scalar
        def _(act):
            def exps(g, u):
                n = (u % TILES + 1) * P
                if u == 0:
                    act.wait_ge(biased[1], g * U)
                    for j in range(2):
                        act.activation(bias[:, j, :], G.causal[:], ACT.Copy, scale=G.slopes[:, bass.ds(g * 2 + j, 1)]).then_inc(bias_made, 1)
                for c in range(2):
                    act.wait_ge(biased[c], g * U + u + 1)
                    act.activation(probs[:, u % 4, c, 0:n], probs[:, u % 4, c, 0:n], ACT.Exp, bias=nmax[:, u % 4, c:c + 1], scale=-1.0,
                                   accum_out=total[:, u % 4, c:c + 1]).then_inc(exped[c], 1)

            def copy_t(g, u):
                n = (u % TILES + 1) * P
                act.wait_ge(t_ready, g * U + u + 1)
                act.wait_ge(pv_done, g * U + max(u - 1, 0))
                act.activation(aT[:, u % 2, 0:n], G.ps[:, 4:6, :].rearrange("p a n -> p (a n)")[:, 0:n], ACT.Copy).then_inc(t_copied, 1)

            def copy_o(g, u):
                i, j = u % TILES, u // TILES
                act.wait_ge(pv_done, g * U + u + 1)
                act.activation(G.od[:, i, bass.ds(g * (2 * VD) + j * VD, VD)], G.ps[:, 6 + u % 2, 0:VD], ACT.Copy).then_inc(o_copied, 1)

            with act.Fori(0, rounds) as g:
                for u in range(U + 3):
                    if 2 <= u < U + 2:
                        copy_t(g, u - 2)
                    if u < U:
                        exps(g, u)
                    if u >= 3:
                        copy_o(g, u - 3)


PAGE = 128
PAGES = 32
BLK = 64
NBLK = 64
N_POOL = 320


def compress(nc, G):
    trio = 3
    chunk = trio * PAGES // 2
    share = chunk // 3
    rounds = (NB + 1) // trio
    npages = trio * PAGES
    with ExitStack() as ctx:
        def sb(name, shape, dt=F32):
            return ctx.enter_context(nc.sbuf_tensor(f"cp_{name}", shape, dt))
        w1 = sb("w1", [P, 2, HD, 2 * HD])
        w2k, w2v, b1 = sb("w2k", [P, 2, KVH, P]), sb("w2v", [P, 2, HD]), sb("b1", [P, 2])
        pages = sb("pages", [P, 2, chunk, 2, KVH, HD])
        hid = sb("hid", [P, 2, npages, KVH])
        sem = sem_maker(nc, ctx, "cp")
        cleared, w1_cleared, weights_in, table_in = sem("cleared"), sem("w1_cleared"), sem("weights_in"), sem("table_in")
        hid_ready, hid_done = sem("hid_ready"), [sem(f"hid_done{kind}") for kind in range(2)]
        page_in = [[sem(f"page_in{c}_{s}") for s in range(3)] for c in range(2)]
        multiplied = [sem(f"multiplied{c}") for c in range(2)]
        c_ready, c_copied = sem("c_ready"), sem("c_copied")
        block = ctx.enter_context(nc.Block())
        unroll = 8

        def load_pages(eng, which, g, c, s):
            eng.wait_ge(table_in, 16)
            eng.wait_ge(multiplied[c], g)
            with eng.Fori(0, share // unroll) as p:
                _, numbers = nc.values_load_multi_w_load_instructions(
                    G.pt[0:1, bass.ds(g * npages + c * chunk + s * share + p * unroll, unroll)], engines=[which], min_val=0, max_val=N_POOL - 1)
                for n, page in enumerate(numbers):
                    eng.dma_start(pages[:, c, bass.ds(p * unroll + (s * share + n), 1), :, :, :].rearrange("t a k h d -> t (a k h d)"),
                                  G.cache_nsa[bass.ds(page, 1), :, 0:2 * P].rearrange("a t n -> (a t) n")).then_inc(page_in[c][s], 16)

        @block.gpsimd
        def _(pool):
            pool.memset(w1[HD:P, :, :, 0:HD], 0.0).then_inc(cleared, 1)
            pool.wait_ge(cleared, 1)
            pool.memset(w2k[:], 0.0).then_inc(cleared, 1)
            pool.memset(w2v[:], 0.0).then_inc(cleared, 1)
            with pool.Fori(0, rounds - 1) as g:
                for c in range(2):
                    load_pages(pool, mybir.EngineType.Pool, g, c, 2)
            load_pages(pool, mybir.EngineType.Pool, rounds - 1, 0, 2)
            pool.wait_ge(multiplied[1], rounds - 1)
            pool.dma_start(pages[:, 1, share:share + TILES, :, :, :].rearrange("t a k h d -> t a (k h d)"),
                           G.nsa_p[:, 0:2 * P].rearrange("(a t) n -> t a n", t=P)).then_inc(page_in[1][2], 16)

        @block.sync
        def _(sp):
            sp.dma_start(G.pt[:], G.page_table).then_inc(table_in, 16)

            with sp.Fori(0, rounds) as g:
                for c in range(2):
                    load_pages(sp, mybir.EngineType.SP, g, c, 0)

        @block.tensor
        def _(pe):
            def hidden(g, c, last=False):
                for s in range(3):
                    pe.wait_ge(page_in[c][s], g * (16 * share) + (16 * share, 0, 16)[s if last else 0])
                for kind in range(2):
                    pe.wait_ge(hid_done[kind], g * 2 + c)
                    for d in range(HD):
                        mm = pe.matmul(G.ps[:, kind, 0:chunk * KVH], w1[:, kind, d, :], pages[:, c, :, kind, :, d],
                                       start=(d == 0), stop=(d == HD - 1))
                        if d == HD - 1 and kind == 0:
                            mm.then_inc(hid_ready, 1)
                mm.then_inc(multiplied[c], 1)

            def project_blocks(g):
                pe.wait_ge(hid_done[0], g * 2 + 2)
                pe.wait_ge(c_copied, g)
                for half in range(2):
                    keys = G.ps[:, 2, 0:2 * npages].rearrange("d (a b) -> d a b", b=2)[:, :, half]
                    for h in range(KVH):
                        pe.matmul(keys, w2k[:, half, h, :], hid[:, 0, :, h], start=(h == 0), stop=(h == KVH - 1))
                pe.wait_ge(hid_done[1], g * 2 + 2)
                for s in range(trio):
                    for half in range(2):
                        for h in range(KVH):
                            last = pe.matmul(G.ps[half * PAGES:(half + 1) * PAGES, 3, s * P + h * HD:s * P + (h + 1) * HD],
                                             hid[:, 1, s * PAGES:(s + 1) * PAGES, h], w2v[:, half, :], start=True, stop=True)
                last.then_inc(c_ready, 1)

            pe.wait_ge(weights_in, 16 * 12)
            with pe.Fori(0, rounds - 1) as g:
                hidden(g, 0)
                hidden(g, 1)
                project_blocks(g)
            hidden(rounds - 1, 0)
            hidden(rounds - 1, 1, last=True)
            project_blocks(rounds - 1)

        @block.scalar
        def _(act):
            def load(g, c):
                load_pages(act, mybir.EngineType.Activation, g, c, 1)

            load(0, 0)
            act.wait_ge(cleared, 3)
            act.wait_ge(w1_cleared, 1)
            for kind in range(2):
                for half in range(2):
                    part = slice(half * HD, (half + 1) * HD)
                    act.dma_start(w1[part, kind, :, part], G.cmp_w1[kind]).then_inc(weights_in, 16)
                    for h in range(KVH):
                        dst = w2k[part, half, h, h * HD:(h + 1) * HD] if kind == 0 else w2v[part, half, :]
                        if kind == 0 or h == 0:
                            act.dma_start(dst, G.cmp_w2[kind]).then_inc(weights_in, 16)
            for half in range(2):
                act.dma_start(b1[half * HD:(half + 1) * HD, :], G.cmp_b1).then_inc(weights_in, 16)

            def gelu(g, c):
                for kind in range(2):
                    ready, count = ((hid_ready, g * 2 + c + 1), (multiplied[c], g + 1))[kind]
                    act.wait_ge(weights_in, 16 * 12)
                    act.wait_ge(ready, count)
                    act.wait_ge(c_ready, g)
                    act.activation(hid[:, kind, c * chunk:(c + 1) * chunk, :], G.ps[:, kind, 0:chunk * KVH].rearrange("p (a h) -> p a h", h=KVH),
                                   ACT.Gelu_apprx_tanh, bias=b1[:, kind:kind + 1]).then_inc(hid_done[kind], 1)

            load(0, 1)
            with act.Fori(0, rounds - 2) as g:
                for c in range(2):
                    gelu(g, c)
                    load(g + 1, c)
            gelu(rounds - 2, 0)
            load(rounds - 1, 0)
            gelu(rounds - 2, 1)
            for c in range(2):
                gelu(rounds - 1, c)

        @block.vector
        def _(dve):
            dve.memset(w1[0:HD, :, :, HD:P], 0.0).then_inc(w1_cleared, 1)
            with dve.Fori(0, rounds) as g:
                dve.wait_ge(c_ready, g + 1)
                dve.tensor_copy(G.ckT[:, bass.ds(g * trio, trio), :], G.ps[:, 2, 0:2 * npages].rearrange("p (s b) -> p s b", s=trio))
                dve.tensor_copy(G.cv[:, bass.ds(g * trio, trio), :], G.ps[0:2 * PAGES, 3, 0:trio * P].rearrange("p (s b) -> p s b", s=trio)
                                ).then_inc(c_copied, 1)


N_TOP = 16
ROWS = KVH * GRP * TS
ROW0 = SEQ


def sample_select(nc, G):
    with ExitStack() as ctx:
        def sb(name, shape, dt=F32):
            return ctx.enter_context(nc.sbuf_tensor(f"ss_{name}", shape, dt))
        q = sb("q", [P, NB, ROWS])
        s, p = sb("s", [ROWS, NB, NBLK]), sb("p", [ROWS, NB, NBLK])
        work, top = sb("work", [ROWS, NB, NBLK + 2]), sb("top", [ROWS, NB, 2, 8])
        least, total = sb("least", [ROWS, NB]), sb("total", [ROWS, NB])
        pT = sb("pT", [NBLK, NB, ROWS])
        sem = sem_maker(nc, ctx, "ss")
        q_cleared, q_in, step, scored, exped = sem("q_cleared"), sem("q_in"), sem("step"), sem("scored"), sem("exped")
        normed, summed, turned, turned_copied, valued = sem("normed"), sem("summed"), sem("turned"), sem("turned_copied"), sem("valued")
        block = ctx.enter_context(nc.Block())

        @block.gpsimd
        def _(pool):
            pool.memset(q[:], 0.0).then_inc(q_cleared, 1)

        @block.sync
        def _(sp):
            sp.wait_ge(q_cleared, 1)
            rows = G.z.rearrange("m p n -> (m p) n")
            for h in range(KVH):
                for g in range(GRP):
                    r = Z_NQ * P + (h * GRP + g) * HD
                    c = (h * GRP + g) * TS
                    sp.dma_start(q[h * HD:(h + 1) * HD, :, c:c + TS],
                                 rows[r:r + HD, ROW0:ROW0 + NS].rearrange("d (b t) -> d b t", t=TS)).then_inc(q_in, 16)

        @block.tensor
        def _(pe):
            pe.wait_ge(step, 1)
            for b in range(NB):
                last = pe.matmul(G.ps[0:ROWS, 0, b * NBLK:(b + 1) * NBLK], q[:, b, :],
                                 G.ckT[:, b, :].rearrange("d (a c) -> d c a", c=2), start=True, stop=True)
            last.then_inc(scored, 1)
            pe.wait_ge(normed, 1)
            pe.matmul(G.ps[0:ROWS, 1, :], G.group_sum[:], p[:].rearrange("r b n -> r (b n)"), start=True, stop=True).then_inc(summed, 1)
            for b in range(NB):
                last = pe.transpose(G.ps[0:NBLK, 2, b * ROWS:(b + 1) * ROWS], p[:, b, :], G.ident[0:ROWS, 0:ROWS])
            last.then_inc(turned, 1)
            pe.wait_ge(turned_copied, 1)
            for b in range(NB):
                last = pe.matmul(G.ps[0:ROWS, 3 + b // 4, (b % 4) * P:(b % 4 + 1) * P], pT[:, b, :], G.cv[:, b, :], start=True, stop=True)
            last.then_inc(valued, 1)

        @block.scalar
        def _(act):
            act.wait_ge(step, 4)
            act.activation(p[:], s[:], ACT.Exp, scale=-1.0).then_inc(exped, 1)
            act.wait_ge(turned, 1)
            act.activation(pT[:].rearrange("n b r -> n (b r)"), G.ps[0:NBLK, 2, :], ACT.Copy).then_inc(turned_copied, 1)
            act.wait_ge(valued, 1)
            for a in range(2):
                act.activation(G.o_cmp[:, 4 * a:4 * a + 4, :].rearrange("r b d -> r (b d)"), G.ps[0:ROWS, 3 + a, :], ACT.Copy)

        @block.vector
        def _(dve):
            n = [0]

            def then(ins):
                n[0] += 1
                ins.then_inc(step, 1)
                dve.wait_ge(step, n[0])

            dve.wait_ge(q_in, 16 * NSA_H)
            then(dve.tensor_scalar(q[:], q[:], -HD ** -0.5, None, ALU.mult))
            dve.wait_ge(scored, 1)
            then(dve.tensor_tensor(s[:], G.ps[0:ROWS, 0, :].rearrange("r (b n) -> r b n", b=NB),
                                   G.bias_cmp[:].rearrange("r (o n) -> r o n", o=1).to_broadcast([ROWS, NB, NBLK]), ALU.add))
            then(dve.tensor_reduce(least[:], s[:], AX, ALU.min))
            then(dve.tensor_tensor(s[:], s[:], least[:].rearrange("r (b o) -> r b o", o=1).to_broadcast([ROWS, NB, NBLK]), ALU.subtract))
            dve.wait_ge(exped, 1)
            then(dve.tensor_reduce(total[:], p[:], AX, ALU.add))
            then(dve.reciprocal(total[:], total[:]))
            dve.tensor_tensor(p[:], p[:], total[:].rearrange("r (b o) -> r b o", o=1).to_broadcast([ROWS, NB, NBLK]), ALU.mult).then_inc(normed, 1)
            dve.wait_ge(summed, 1)
            dve.memset(work[:, :, NBLK:NBLK + 2], -5.0)
            for half in range(2):
                last = dve.tensor_copy(work[:, :, 0:NBLK].rearrange("r b (a c) -> r b a c", c=2)[:, :, :, half],
                                       G.ps[0:ROWS, 1, :].rearrange("r (b c a) -> r b c a", b=NB, c=2)[:, :, half, :])
            then(last)
            then(dve.memset(work[:, :, 0:1], -3.0))
            for b in range(NB):
                last = dve.max(top[:, b, 0, :], work[:, b, :])
            then(last)
            for b in range(NB):
                last = dve.match_replace(out=work[:, b, :], in_to_replace=top[:, b, 0, :], in_values=work[:, b, :], imm_value=-1.0)
            then(last)
            for b in range(NB):
                last = dve.max(top[:, b, 1, :], work[:, b, :])
            then(last)
            then(dve.memset(top[:, :, 1, N_TOP - 2 - 8:8], -5.0))
            for b in range(NB):
                last = dve.match_replace(out=work[:, b, :], in_to_replace=top[:, b, 1, :], in_values=work[:, b, :], imm_value=-1.0)
            then(last)
            then(dve.tensor_scalar(G.drop[:], work[:, :, 0:NBLK], -1.0, 1e30, ALU.not_equal, ALU.mult))
            dve.memset(G.drop[:, :, 0:1], 0.0)


QUAD = 4
QT = QUAD * PAGE
QUADS = PAGES // QUAD
STEPS = QUADS + 2
S_WIN, S_NEW = QUADS, QUADS + 1
KV1 = KVH * HD
RING = 4
FOLDS = 7


def sample_attend(nc, G):
    rounds = NB // 2
    N = 2 * STEPS
    PAGE_STEPS = [n for n in range(N) if n % STEPS < QUADS]
    D_STEPS = [n for n in range(N) if n % STEPS != S_WIN]
    ND, NN = QUADS + 1, QUADS + 3
    NSUM = NN + 1

    def seq(n):
        return n // STEPS

    def is_page(n):
        return n % STEPS < QUADS

    def quad(n):
        return seq(n) * QUADS + n % STEPS

    def wait(eng, sem, value):
        if not isinstance(value, int) or value > 0:
            eng.wait_ge(sem, value)

    def at(g, n, lag):
        if n >= lag:
            return (g, n - lag) if n - lag < N else None
        return None if isinstance(g, int) and g == 0 else (g - 1, n - lag + N)

    def ended(g, n, lag):
        if n - lag in (STEPS, N):
            return [(g, (n - lag) // STEPS - 1)]
        return [(g - 1, 1)] if n == lag and not isinstance(g, int) else []

    def all_beats(eng, beat):
        for n in range(N):
            beat(0, n)
        with eng.Fori(1, rounds) as g:
            for n in range(N):
                beat(g, n)
        for n in range(N, N + 5):
            beat(rounds - 1, n)

    def before(steps, n):
        return sum(1 for m in steps if m < n)

    def tiles(n):
        return 5 if is_page(n) else 1 if n % STEPS == S_WIN else 0

    def turned_before(n, t):
        order = [(m, u) for m in range(N) for u in (range(5) if is_page(m) else (4,) if tiles(m) else ())]
        seen = [x for x in order if x < (n, t)]
        return len(seen), sum(1 for x in seen if x[1] % 2 == 0), sum(1 for x in seen if x[1] % 2)

    ALL_T, EVEN_T, ODD_T = turned_before(N, 0)
    KEY_BANKS = (0, 1, 7)
    N_SOFT = N + 2

    def soft_before(n):
        return n + before([m for m in range(N) if m % STEPS == S_NEW], n)

    def key_tiles(n):
        return tuple(range(5)) if is_page(n) else (4,) if tiles(n) else ()

    with ExitStack() as ctx:
        def sb(name, shape, dt=F32):
            return ctx.enter_context(nc.sbuf_tensor(f"sa_{name}", shape, dt))
        dpage = sb("dpage", [P, RING, QUAD, 2, DIFF_H * VD])
        npage = sb("npage", [P, RING, QUAD, 2, KV1])
        window = sb("window", [P, 2, QUAD, 2, KV1])
        qd, qn = sb("qd", [P, 2, DIFF_H, 32]), sb("qn", [P, 2, ROWS])
        new_k = sb("new_k", [P, 2, 6, TS])
        new_v = sb("new_v", [P, 2, DIFF_H * VD + 2 * KV1])
        kT = sb("kT", [P, 2, 5, QT])
        pd, pn = sb("pd", [P, 2, QT]), sb("pn", [P, 2, QT])
        pdT, pnT = sb("pdT", [P, 2, QT]), sb("pnT", [P, 2, QUAD * ROWS])
        masked = sb("masked", [ROWS, 2, QT])
        od, on = sb("od", [P, 2, ND, VD]), sb("on", [ROWS, 2, NSUM, KV1])
        min_d, min_n = sb("min_d", [P, 2, ND]), sb("min_n", [ROWS, 2, NN])
        tot_d, tot_n = sb("tot_d", [P, 2, ND]), sb("tot_n", [ROWS, 2, NN])
        w_d, w_n = sb("w_d", [P, ND]), sb("w_n", [ROWS, NSUM])
        wt_d, wt_n = sb("wt_d", [P, ND]), sb("wt_n", [ROWS, NN])
        base_d, base_n = sb("base_d", [P, 1]), sb("base_n", [ROWS, 2])
        join_d, join_n = sb("join_d", [P, ND, 32]), sb("join_n", [ROWS, NSUM, ROWS])
        carrier = sb("carrier", [P, 3 * N])
        sem = sem_maker(nc, ctx, "sa")
        cleared, scaled, small_in = sem("cleared"), sem("scaled"), [sem(f"small_in{j}") for j in range(2)]
        d_in, n_in = [sem(f"d_in{r}") for r in range(RING)], [sem(f"n_in{r}") for r in range(RING)]
        k_turned, k_even, k_odd = sem("k_turned"), sem("k_even"), sem("k_odd")
        sd_ready, sn_ready, soft_d, soft_n, exp_d, exp_n = (sem(x) for x in ("sd_ready", "sn_ready", "soft_d", "soft_n", "exp_d", "exp_n"))
        mask_made, p_turned, p_copied, o_copied = sem("mask_made"), sem("p_turned"), sem("p_copied"), sem("o_copied")
        used = [sem(f"used{r}") for r in range(RING)]
        tail = [sem(f"tail{j}") for j in range(2)]
        weighed, folded, join_ready, join_copied = (sem(x) for x in ("weighed", "folded", "join_ready", "join_copied"))
        joined = [sem(f"joined{j}") for j in range(2)]
        block = ctx.enter_context(nc.Block())
        z_rows = G.z.rearrange("m p n -> (m p) n")

        def page_numbers(eng, which, g, q, extra=0):
            _, numbers = nc.values_load_multi_w_load_instructions(
                G.pt[0:1, bass.ds(g * (2 * PAGES) + q * QUAD + extra, QUAD)], engines=[which], min_val=0, max_val=N_POOL - 1)
            return numbers

        SMALL = 16 * 10

        @block.sync
        def _(sp):
            def small(g, j):
                sp.wait_ge(cleared, 4)
                wait(sp, tail[j], g * 2)
                col = bass.ds(g * (2 * TS) + (ROW0 + j * TS), TS)
                row = bass.ds(g * (2 * TS) + j * TS, TS)
                loads = []
                for c in range(2):
                    part = slice(c * HD, (c + 1) * HD)
                    loads.append((qd[part, j, :, c * TS:(c + 1) * TS], G.z[Z_DQ:Z_DQ + DIFF_H, part, col].rearrange("h d t -> d h t")))
                for h in range(KVH):
                    r = (Z_NQ * P) + h * GRP * HD
                    loads.append((qn[h * HD:(h + 1) * HD, j, h * GRP * TS:(h + 1) * GRP * TS].rearrange("d (g t) -> d g t", g=GRP),
                                  z_rows[r:r + GRP * HD, col].rearrange("(g d) t -> d g t", g=GRP)))
                loads.append((new_k[:, j, 0:4, :], G.z[Z_DK:Z_DK + 4, :, col].rearrange("h d t -> d h t")))
                loads.append((new_k[:, j, 4:6, :], G.z[Z_NKV + 2:Z_NKV + 5:2, :, col].rearrange("h d t -> d h t")))
                loads.append((new_v[0:TS, j, 0:512], G.diff_s[row, 512:1024]))
                loads.append((new_v[0:TS, j, 512:640], G.nsa_s[row, 384:512]))
                loads.append((new_v[0:TS, j, 640:768], G.kvw[bass.ds(g * (2 * TS) + (SEQ + j * TS), TS), 128:256]))
                loads.append((window[:, j, :, :, :].rearrange("p a k d -> p a (k d)"),
                              G.win[bass.ds(g * 2 + j, 1), :, :].rearrange("o (a p) n -> p (o a) n", p=P)))
                for dst, src in loads:
                    sp.dma_start(dst, src).then_inc(small_in[j], 16)

            def round_(g):
                for q in range(2 * QUADS):
                    r = q % RING
                    if not isinstance(g, int):
                        sp.wait_ge(cleared, 4)
                    wait(sp, used[r], g * (2 * QUADS // RING) + q // RING)
                    for a, page in enumerate(page_numbers(sp, mybir.EngineType.SP, g, q)):
                        sp.dma_start(dpage[:, r, a, :, :].rearrange("t k n -> t (k n)"),
                                     G.cache_diff[bass.ds(page, 1), :, :].rearrange("o t n -> (o t) n")).then_inc(d_in[r], 16)
                    if q in (0, 4):
                        small(g, q // 4)

            round_(0)
            with sp.Fori(1, rounds) as g:
                round_(g)

        @block.gpsimd
        def _(pool):
            def load(g, q):
                r = q % RING
                if not isinstance(g, int):
                    pool.wait_ge(cleared, 4)
                wait(pool, used[r], g * (2 * QUADS // RING) + q // RING)
                for a, page in enumerate(page_numbers(pool, mybir.EngineType.Pool, g, q)):
                    pool.dma_start(npage[:, r, a, :, :].rearrange("t k n -> t (k n)"),
                                   G.cache_nsa[bass.ds(page, 1), :, 256:512].rearrange("o t n -> (o t) n")).then_inc(n_in[r], 16)

            for q in range(3):
                load(0, q)
            for x in (qd, qn):
                pool.memset(x[:], 0.0).then_inc(cleared, 1)
            pool.memset(new_v[:], 0.0).then_inc(cleared, 1)
            pool.wait_ge(cleared, 3)
            pool.memset(pn[ROWS:P, :, :], 0.0).then_inc(cleared, 1)

            def mask(g, q):
                n = PAGE_STEPS[q]
                m = PAGE_STEPS[q - 2] if q >= 2 else None
                pool.wait_ge(cleared, 4)
                wait(pool, soft_n, g * N_SOFT + (soft_before(m) + 1 if q >= 2 else 0))
                blocks = G.drop[:, bass.ds(g * 2 + seq(n), 1), (q % QUADS) * 8:(q % QUADS + 1) * 8]
                pool.tensor_tensor(masked[:, q % 2, :].rearrange("r (a b) -> r a b", b=BLK),
                                   G.bias_n[:].rearrange("r (a b) -> r a b", b=BLK),
                                   blocks.rearrange("r o (a b) -> r (o a) b", b=1).to_broadcast([ROWS, 8, BLK]), ALU.add).then_inc(mask_made, 1)

            def round_(g, last):
                for q in range(2 * QUADS):
                    mask(g, q)
                    if q + 3 < 2 * QUADS:
                        load(g, q + 3)
                    elif not last:
                        load(g + 1, q + 3 - 2 * QUADS)

            round_(0, False)
            with pool.Fori(1, rounds - 1) as g:
                round_(g, False)
            round_(rounds - 1, True)

        @block.tensor
        def _(pe):
            def turn_keys(g, n):
                if is_page(n):
                    r = quad(n) % RING
                    arrived = g * (16 * QUAD * (2 * QUADS // RING)) + 16 * QUAD * (quad(n) // RING + 1)
                    pe.wait_ge(d_in[r], arrived)
                    pe.wait_ge(n_in[r], arrived)
                elif tiles(n):
                    pe.wait_ge(small_in[seq(n)], g * SMALL + SMALL)
                for t in key_tiles(n):
                    m, _, _ = turned_before(n, t)
                    if m >= len(KEY_BANKS):
                        a, b = [(x, u) for x in range(N) for u in key_tiles(x)][m - len(KEY_BANKS)]
                        _, even, odd = turned_before(a, b)
                        if b % 2 == 0:
                            pe.wait_ge(k_even, g * EVEN_T + even + 1)
                        else:
                            pe.wait_ge(k_odd, g * ODD_T + odd + 1)
                    else:
                        wait(pe, k_even, g * EVEN_T)
                        wait(pe, k_odd, g * ODD_T)
                    for a in range(QUAD):
                        if not is_page(n):
                            keys = window[:, seq(n), a, 0, :]
                        elif t < 4:
                            keys = dpage[:, quad(n) % RING, a, 0, t * P:(t + 1) * P]
                        else:
                            keys = npage[:, quad(n) % RING, a, 0, :]
                        last = pe.transpose(G.ps[:, KEY_BANKS[m % len(KEY_BANKS)], a * PAGE:(a + 1) * PAGE], keys, G.ident[:])
                    last.then_inc(k_turned, 1)

            def scores(g, n):
                j = seq(n)
                if n % STEPS == 0:
                    pe.wait_ge(scaled, g * 4 + 2 * j + 2)
                _, even, odd = turned_before(n + 1, 0)
                if tiles(n):
                    pe.wait_ge(k_even, g * EVEN_T + even)
                    pe.wait_ge(k_odd, g * ODD_T + odd)
                new = n % STEPS == S_NEW
                width = TS if new else QT
                if n in D_STEPS:
                    wait(pe, soft_d, g * len(D_STEPS) + before(D_STEPS, n))
                    for h in range(DIFF_H):
                        keys = new_k[:, j, h, :] if new else kT[:, n % 2, h, :]
                        last = pe.matmul(G.ps[32 * h:32 * h + 32, 2, 0:width], qd[:, j, h, :], keys, start=True, stop=True)
                    last.then_inc(sd_ready, 1)
                wait(pe, soft_n, g * N_SOFT + soft_before(n))
                for part in range(2 if new else 1):
                    for h in range(KVH):
                        keys = new_k[:, j, 4 + part, :] if new else kT[:, n % 2, 4, :]
                        last = pe.matmul(G.ps[32 * h:32 * h + 32, 3, part * TS:part * TS + width], qn[:, j, 32 * h:32 * h + 32], keys,
                                         start=True, stop=True)
                last.then_inc(sn_ready, 1)

            def turn_probs(g, n):
                new = n % STEPS == S_NEW
                wait(pe, p_copied, g * N + n)
                if n in D_STEPS:
                    pe.wait_ge(exp_d, g * len(D_STEPS) + before(D_STEPS, n) + 1)
                pe.wait_ge(exp_n, g * N_SOFT + soft_before(n + 1))
                if new:
                    pe.transpose(G.ps[0:TS, 4, 0:P], pd[:, n % 2, 0:TS], G.ident[:])
                    for part in range(2):
                        last = pe.transpose(G.ps[0:TS, 5, part * ROWS:(part + 1) * ROWS], pn[0:ROWS, n % 2, part * TS:(part + 1) * TS],
                                            G.ident[0:ROWS, 0:ROWS])
                else:
                    for a in range(QUAD):
                        if n in D_STEPS:
                            pe.transpose(G.ps[:, 4, a * P:(a + 1) * P], pd[:, n % 2, a * PAGE:(a + 1) * PAGE], G.ident[:])
                        rows = ROWS if a else P
                        last = pe.transpose(G.ps[:, 5, a * ROWS:a * ROWS + rows], pn[0:rows, n % 2, a * PAGE:(a + 1) * PAGE],
                                            G.ident[0:rows, 0:rows])
                last.then_inc(p_turned, 1)

            def values(g, n):
                j, new = seq(n), n % STEPS == S_NEW
                pe.wait_ge(p_copied, g * N + n + 1)
                wait(pe, o_copied, g * N + n)
                wait(pe, join_copied, g * 2 + (1 if n > STEPS + 2 else 0) - (1 if n <= 2 else 0))
                if new:
                    for h in range(DIFF_H):
                        pe.matmul(G.ps[32 * h:32 * h + 32, 6, 0:VD], pdT[:, n % 2, 32 * h:32 * h + 32],
                                  new_v[:, j, h * VD:(h + 1) * VD], start=True, stop=True)
                    for part in range(2):
                        last = pe.matmul(G.ps[0:ROWS, 6, VD + part * P:VD + (part + 1) * P], pnT[:, n % 2, part * ROWS:(part + 1) * ROWS],
                                         new_v[:, j, 512 + part * P:512 + (part + 1) * P], start=True, stop=True)
                    last.then_inc(tail[j], 1)
                    return
                if n in D_STEPS:
                    for a in range(QUAD):
                        for h in range(DIFF_H):
                            pe.matmul(G.ps[32 * h:32 * h + 32, 6, 0:VD], pdT[:, n % 2, a * P + 32 * h:a * P + 32 * h + 32],
                                      dpage[:, quad(n) % RING, a, 1, h * VD:(h + 1) * VD], start=(a == 0), stop=(a == QUAD - 1))
                for a in range(QUAD):
                    v = npage[:, quad(n) % RING, a, 1, :] if is_page(n) else window[:, j, a, 1, :]
                    last = pe.matmul(G.ps[0:ROWS, 6, VD:VD + KV1], pnT[:, n % 2, a * ROWS:(a + 1) * ROWS], v,
                                     start=(a == 0), stop=(a == QUAD - 1))
                last.then_inc(used[quad(n) % RING] if is_page(n) else tail[j], 1)

            def join(g, j, last):
                pe.wait_ge(join_ready, g * 4 + 2 * j + 2)
                pe.wait_ge(o_copied, g * N + (N if last else (j + 1) * STEPS + 3))
                wait(pe, join_copied, g * 2 + j)
                for s in range(ND):
                    pe.matmul(G.ps[:, 6, 0:32], od[:, j, s, :], join_d[:, s, :], start=(s == 0), stop=(s == ND - 1))
                for s in range(NSUM):
                    last = pe.matmul(G.ps[:, 6, VD:VD + ROWS], on[:, j, s, :], join_n[:, s, :], start=(s == 0), stop=(s == NSUM - 1))
                last.then_inc(joined[j], 1)

            def beat(g, n):
                now, one, two = (at(g, n, lag) for lag in range(3))
                if one:
                    scores(*one)
                if two:
                    values(*two)
                if now:
                    turn_keys(*now)
                if one:
                    turn_probs(*one)
                for which in ended(g, n, 4):
                    join(*which, n >= N)

            all_beats(pe, beat)

        def key_copies(eng, g, n, t, copied, copy):
            m, _, _ = turned_before(n, t)
            wait(eng, sn_ready, g * N + (n - 1))
            eng.wait_ge(k_turned, g * ALL_T + m + 1)
            copy(kT[:, n % 2, t, :], G.ps[:, KEY_BANKS[m % len(KEY_BANKS)], :]).then_inc(copied, 1)

        def slots(n):
            i = n % STEPS
            return (i, i, 1) if i < QUADS else (None, QUADS + 1, 1) if i == S_WIN else (QUADS, QUADS, 2)

        @block.scalar
        def _(act):
            def exps_d(g, n):
                if n not in D_STEPS:
                    return
                width, slot = (TS if n % STEPS == S_NEW else QT), slots(n)[0]
                act.wait_ge(soft_d, g * len(D_STEPS) + before(D_STEPS, n) + 1)
                act.activation(pd[:, n % 2, 0:width], pd[:, n % 2, 0:width], ACT.Exp, bias=min_d[:, seq(n), slot:slot + 1], scale=-1.0,
                               accum_out=tot_d[:, seq(n), slot:slot + 1]).then_inc(exp_d, 1)

            def exps_n(g, n):
                _, slot, parts = slots(n)
                width = TS if n % STEPS == S_NEW else QT
                for part in range(parts):
                    act.wait_ge(soft_n, g * N_SOFT + soft_before(n) + part + 1)
                    x = pn[0:ROWS, n % 2, part * TS:part * TS + width]
                    o = slot + 2 * part
                    act.activation(x, x, ACT.Exp, bias=min_n[:, seq(n), o:o + 1], scale=-1.0,
                                   accum_out=tot_n[:, seq(n), o:o + 1]).then_inc(exp_n, 1)

            def copy_o(g, n):
                j = seq(n)
                d_slot, n_slot, parts = slots(n)
                if is_page(n):
                    act.wait_ge(used[quad(n) % RING], g * (2 * QUADS // RING) + quad(n) // RING + 1)
                else:
                    act.wait_ge(tail[j], g * 2 + n % STEPS - S_WIN + 1)
                wait(act, joined[j], g)
                if d_slot is not None:
                    act.activation(od[:, j, d_slot, :], G.ps[:, 6, 0:VD], ACT.Copy)
                if n % STEPS == S_WIN:
                    act.activation(on[:, j, NN:NN + 1, :], G.o_cmp[:, bass.ds(g * 2 + j, 1), :], ACT.Copy)
                if parts == 2:
                    act.activation(on[:, j, n_slot:n_slot + 3:2, :], G.ps[0:ROWS, 6, VD:VD + 2 * P].rearrange("p (a n) -> p a n", a=2),
                                   ACT.Copy).then_inc(o_copied, 1)
                else:
                    act.activation(on[:, j, n_slot, :], G.ps[0:ROWS, 6, VD:VD + KV1], ACT.Copy).then_inc(o_copied, 1)

            def weigh(g, j):
                act.wait_ge(folded, (g * 2 + j) * FOLDS + 2)
                act.activation(w_d[:], wt_d[:], ACT.Exp, bias=base_d[:], scale=-1.0).then_inc(weighed, 1)
                act.activation(w_n[:, 0:QUADS + 1], wt_n[:, 0:QUADS + 1], ACT.Exp, bias=base_n[:, 0:1], scale=-1.0).then_inc(weighed, 1)
                act.activation(w_n[:, QUADS + 1:NN], wt_n[:, QUADS + 1:NN], ACT.Exp, bias=base_n[:, 1:2], scale=-1.0).then_inc(weighed, 1)

            def copy_joined(g, j):
                act.wait_ge(joined[j], g + 1)
                b = bass.ds(g * 2 + j, 1)
                act.activation(G.s_odT[:, :, b, :], G.ps[:, 6, 0:32].rearrange("p (h b t) -> p h b t", b=1, t=TS), ACT.Copy)
                for h in range(KVH):
                    part = slice(h * HD, (h + 1) * HD)
                    last = act.activation(G.s_onT[part, :, b, :],
                                          G.ps[part, 6, VD + h * 32:VD + (h + 1) * 32].rearrange("p (a b t) -> p a b t", b=1, t=TS), ACT.Copy)
                last.then_inc(join_copied, 1)

            def beat(g, n):
                now, one, two = (at(g, n, lag) for lag in range(3))
                even = [t for t in (key_tiles(n) if now else ()) if t % 2 == 0]
                for i in range(3):
                    if i < len(even):
                        key_copies(act, g, n, even[i], k_even, lambda dst, src: act.activation(dst, src, ACT.Copy))
                    if one and i < 2:
                        (exps_d, exps_n)[i](*one)
                if two:
                    copy_o(*two)
                for which in ended(g, n, 1):
                    weigh(*which)
                for which in ended(g, n, 4):
                    copy_joined(*which)

            all_beats(act, beat)

        @block.vector
        def _(dve):
            def soft(g, n):
                new = n % STEPS == S_NEW
                d_slot, n_slot, parts = slots(n)
                width = TS if new else QT
                if n in D_STEPS:
                    wait(dve, p_turned, g * N + (n - 1))
                    dve.wait_ge(sd_ready, g * len(D_STEPS) + before(D_STEPS, n) + 1)
                    dve.memset(carrier[:, 3 * n:3 * n + 1], 0.0)
                    dve.tensor_tensor_reduce(out=pd[:, n % 2, 0:width], in0=G.ps[:, 2, 0:width], in1=(G.bias_new_d if new else G.bias_d)[:],
                                             scale=1.0, scalar=3e38, op0=ALU.add, op1=ALU.min,
                                             accum_out=min_d[:, seq(n), d_slot:d_slot + 1]).then_inc(soft_d, 1)
                wait(dve, p_turned, g * N + (n - 1))
                dve.wait_ge(sn_ready, g * N + n + 1)
                if is_page(n):
                    dve.wait_ge(mask_made, g * (2 * QUADS) + quad(n) + 1)
                dve.memset(carrier[:, 3 * n + 1:3 * n + 2], 0.0)
                bias = masked[:, quad(n) % 2, :] if is_page(n) else (G.bias_new_n if new else G.bias_w)[:]
                for part in range(parts):
                    o = n_slot + 2 * part
                    x = slice(part * TS, part * TS + width)
                    dve.tensor_tensor_reduce(out=pn[0:ROWS, n % 2, x], in0=G.ps[0:ROWS, 3, x], in1=bias,
                                             scale=1.0, scalar=3e38, op0=ALU.add, op1=ALU.min,
                                             accum_out=min_n[:, seq(n), o:o + 1]).then_inc(soft_n, 1)

            def copy_p(g, n):
                new = n % STEPS == S_NEW
                dve.wait_ge(p_turned, g * N + n + 1)
                wait(dve, o_copied, g * N + (n - 1))
                rows, dw, nw = (TS, P, 2 * ROWS) if new else (P, QT, QUAD * ROWS)
                if n in D_STEPS:
                    dve.tensor_copy(pdT[0:rows, n % 2, 0:dw], G.ps[0:rows, 4, 0:dw])
                dve.tensor_copy(pnT[0:rows, n % 2, 0:nw], G.ps[0:rows, 5, 0:nw]).then_inc(p_copied, 1)

            def fold(g, j):
                done = [0]

                def then(last):
                    done[0] += 1
                    last.then_inc(folded, 1)
                    dve.wait_ge(folded, (g * 2 + j) * FOLDS + done[0])

                sel, win = slice(0, QUADS + 1), slice(QUADS + 1, NN)
                wait(dve, joined[1 - j], g + j)
                dve.wait_ge(exp_d, g * len(D_STEPS) + before(D_STEPS, (j + 1) * STEPS))
                dve.wait_ge(exp_n, g * N_SOFT + soft_before((j + 1) * STEPS))
                dve.tensor_tensor(wt_d[:], min_d[:, j, :], G.off_d[:], ALU.add)
                then(dve.tensor_tensor(wt_n[:], min_n[:, j, :], G.off_n[:], ALU.add))
                dve.tensor_reduce(base_d[:], wt_d[:], AX, ALU.min)
                dve.tensor_reduce(base_n[:, 0:1], wt_n[:, sel], AX, ALU.min)
                then(dve.tensor_reduce(base_n[:, 1:2], wt_n[:, win], AX, ALU.min))
                dve.wait_ge(weighed, (g * 2 + j) * 3 + 3)
                dve.tensor_tensor(wt_d[:], w_d[:], tot_d[:, j, :], ALU.mult)
                then(dve.tensor_tensor(wt_n[:], w_n[:, 0:NN], tot_n[:, j, :], ALU.mult))
                dve.tensor_reduce(base_d[:], wt_d[:], AX, ALU.add)
                dve.tensor_reduce(base_n[:, 0:1], wt_n[:, sel], AX, ALU.add)
                then(dve.tensor_reduce(base_n[:, 1:2], wt_n[:, win], AX, ALU.add))
                dve.reciprocal(base_d[:], base_d[:])
                then(dve.reciprocal(base_n[:], base_n[:]))
                gate = G.gates_s[:, bass.ds(g * 2 + j, 1), :].rearrange("p o k -> p (o k)")
                dve.tensor_tensor(base_d[:], base_d[:], G.sgn_d[:], ALU.mult)
                dve.tensor_copy(w_n[:, NN:NSUM], gate[:, 0:1])
                then(dve.tensor_tensor(base_n[:], base_n[:], gate[:, 1:3], ALU.mult))
                dve.tensor_scalar(w_d[:], w_d[:], base_d[:], None, ALU.mult)
                dve.tensor_scalar(w_n[:, sel], w_n[:, sel], base_n[:, 0:1], None, ALU.mult)
                then(dve.tensor_scalar(w_n[:, win], w_n[:, win], base_n[:, 1:2], None, ALU.mult))
                dve.tensor_tensor(join_d[:], G.comb_d[:].rearrange("p (o n) -> p o n", o=1).to_broadcast([P, ND, 32]),
                                  w_d[:].rearrange("p (s o) -> p s o", o=1).to_broadcast([P, ND, 32]), ALU.mult).then_inc(join_ready, 1)
                dve.tensor_tensor(join_n[:], G.ident[0:ROWS, 0:ROWS].rearrange("p (o n) -> p o n", o=1).to_broadcast([ROWS, NSUM, ROWS]),
                                  w_n[:].rearrange("p (s o) -> p s o", o=1).to_broadcast([ROWS, NSUM, ROWS]), ALU.mult).then_inc(join_ready, 1)

            def beat(g, n):
                now, one = (at(g, n, lag) for lag in range(2))
                if now and n % STEPS == 0:
                    j = seq(n)
                    dve.wait_ge(small_in[j], g * SMALL + SMALL)
                    dve.tensor_scalar(qd[:, j, :, :], qd[:, j, :, :], -HD ** -0.5, None, ALU.mult).then_inc(scaled, 1)
                    dve.tensor_scalar(qn[:, j, :], qn[:, j, :], -HD ** -0.5, None, ALU.mult).then_inc(scaled, 1)
                if one:
                    soft(*one)
                for t in (key_tiles(n) if now else ()):
                    if t % 2:
                        key_copies(dve, g, n, t, k_odd, lambda dst, src: dve.tensor_copy(dst, src))
                if one:
                    copy_p(*one)
                for which in ended(g, n, 1):
                    fold(*which)

            all_beats(dve, beat)


def fill(nc, G, stage, pairs):
    with ExitStack() as ctx:
        filled = sem_maker(nc, ctx, stage)("filled")
        block = ctx.enter_context(nc.Block())

        @block.sync
        def _(sp):
            for dst, src in pairs:
                sp.dma_start(dst, src).then_inc(filled, 16)
            sp.wait_ge(filled, 16 * len(pairs))


def gates(nc, G):
    with ExitStack() as ctx:
        raw = ctx.enter_context(nc.sbuf_tensor("gt_raw", [N_GATE, SEQ], F32))
        sem = sem_maker(nc, ctx, "gt")
        raw_in, sample_in, turned, opened = sem("raw_in"), sem("sample_in"), sem("turned"), sem("opened")
        block = ctx.enter_context(nc.Block())

        @block.sync
        def _(sp):
            sp.dma_start(raw[:], G.z[Z_NG, 0:N_GATE, 0:SEQ]).then_inc(raw_in, 16)
            for n in range(NSA_H):
                for k in range(3):
                    sp.dma_start(G.gates_s[n * TS:(n + 1) * TS, :, k],
                                 G.z[Z_NG, n * 3 + k, ROW0:ROW0 + NS].rearrange("(b t) -> t b", t=TS)).then_inc(sample_in, 16)

        @block.tensor
        def _(pe):
            pe.wait_ge(raw_in, 16)
            for i in range(TILES):
                last = pe.transpose(G.ps[:, 0, i * N_GATE:(i + 1) * N_GATE], raw[:, i * P:(i + 1) * P], G.ident[0:N_GATE, 0:N_GATE])
            last.then_inc(turned, 1)

        @block.scalar
        def _(act):
            act.wait_ge(turned, 1)
            act.activation(G.gates_t[:], G.ps[:, 0, 0:TILES * N_GATE].rearrange("p (i n) -> p i n", i=TILES), ACT.Sigmoid).then_inc(opened, 1)
            act.wait_ge(sample_in, 16 * N_GATE)
            act.activation(G.gates_s[:], G.gates_s[:], ACT.Sigmoid)

        @block.vector
        def _(dve):
            dve.wait_ge(opened, 1)
            g = G.gates_t[:, 0, 0:N_GATE:3]
            dve.tensor_scalar(g, g, G.row_valid[:], None, ALU.mult)


W_TILES = WIN // P + 1
NCB = 2 * PAGES


def prompt_nsa(nc, G):
    U = 2 * TILES
    WK = W_TILES * P
    with ExitStack() as ctx:
        def sb(name, shape, dt=F32):
            return ctx.enter_context(nc.sbuf_tensor(f"pn_{name}", shape, dt))
        q, k, v = sb("q", [P, 2, SEQ]), sb("k", [P, 2, SEQ]), sb("v", [P, 2, TILES, P])
        bias_s, bias_w, bias_c = sb("bias_s", [P, 2, SEQ]), sb("bias_w", [P, 2, WK]), sb("bias_c", [P, 2, TILES * NCB])
        probs_s, probs_w = sb("probs_s", [P, 4, SEQ]), sb("probs_w", [P, 4, WK + NCB])
        sT, wT = sb("sT", [P, 2, SEQ]), sb("wT", [P, 2, WK + P])
        least, total, share = sb("least", [P, 4, 3]), sb("total", [P, 4, 3]), sb("share", [P, 4, 3])
        carrier = sb("carrier", [P, 3 * U + 2])
        sem = sem_maker(nc, ctx, "pn")
        q_cleared, kv_in, bias_made, q_scaled = sem("q_cleared"), sem("kv_in"), sem("bias_made"), sem("q_scaled")
        q_in, head_scored = ([sem(f"{what}{j}") for j in range(2)] for what in ("q_in", "head_scored"))
        s_ready, biased, exped, t_ready, t_copied = ([sem(f"{what}{c}") for c in range(2)] for what in ("s_ready", "biased", "exped", "t_ready", "t_copied"))
        valued, joined, combined = sem("valued"), sem("joined"), sem("combined")
        block = ctx.enter_context(nc.Block())
        z_rows = G.z.rearrange("m p n -> (m p) n")
        JOIN = 4

        def wide(u):
            w = min(u % TILES + 1, W_TILES) * P
            return w, WK - w

        @block.gpsimd
        def _(pool):
            pool.memset(q[:], 0.0).then_inc(q_cleared, 1)

        @block.sync
        def _(sp):
            sp.dma_start(k[:, 0, :], G.z[Z_NKV + 2, :, 0:SEQ]).then_inc(kv_in, 16)
            sp.dma_start(k[:, 1, :], G.z[Z_NKV + 4, :, 0:SEQ]).then_inc(kv_in, 16)
            sp.dma_start(v[:, 0, :, :], G.nsa_p[:, 384:512].rearrange("(i p) d -> p i d", p=P)).then_inc(kv_in, 16)
            sp.dma_start(v[:, 1, :, :], G.kvw[0:SEQ, 128:256].rearrange("(i p) d -> p i d", p=P)).then_inc(kv_in, 16)
            with sp.Fori(0, GRP) as g:
                for j in range(2):
                    sp.wait_ge(q_cleared, 1)
                    sp.wait_ge(head_scored[j], g)
                    sp.dma_start(q[j * HD:(j + 1) * HD, j, :], z_rows[bass.ds(g * HD + (Z_NQ * P + j * GRP * HD), HD), 0:SEQ]).then_inc(q_in[j], 16)

        @block.tensor
        def _(pe):
            def scores(g, u, c):
                i, j = u % TILES, u // TILES
                queries = q[:, j, i * P:(i + 1) * P]
                if i == 0 and c == 0:
                    pe.wait_ge(q_scaled, g * 2 + j + 1)
                pe.wait_ge(biased[c], g * U + u)
                n, first = ((i + 1) * P, 0) if c == 0 else (wide(u)[0], (i + 1) * P - wide(u)[0])
                for n0 in range(0, n, 512):
                    m = min(512, n - n0)
                    last = pe.matmul(G.ps[:, 2 * c + n0 // 512, 0:m], queries, k[:, c, first + n0:first + n0 + m], start=True, stop=True)
                if c == 1:
                    last = pe.matmul(G.ps[:, 3, P:P + NCB], queries, G.ckT[:, NB, :].rearrange("d (a c) -> d c a", c=2), start=True, stop=True)
                last.then_inc(s_ready[c], 1)

            def turn(g, u, c):
                pe.wait_ge(exped[c], g * U + u + 1)
                pe.wait_ge(t_copied[1 - c], g * U + u + c)
                count = (u % TILES + 1) if c == 0 else wide(u)[0] // P
                src = (probs_s, probs_w)[c]
                for t in range(count):
                    last = pe.transpose(G.ps[:, 4 + t // 4, (t % 4) * P:(t % 4 + 1) * P], src[:, u % 4, t * P:(t + 1) * P], G.ident[:])
                if c == 1:
                    last = pe.transpose(G.ps[0:NCB, 4 + count // 4, (count % 4) * P:(count % 4 + 1) * P],
                                        src[:, u % 4, WK:WK + NCB], G.ident[:])
                last.then_inc(t_ready[c], 1)

            def values(g, u, c):
                i, j = u % TILES, u // TILES
                pe.wait_ge(t_copied[c], g * U + u + 1)
                if c == 0:
                    pe.wait_ge(joined, (g * U + max(u - 1, 0)) * JOIN)
                    for t in range(i + 1):
                        pe.matmul(G.ps[:, 6 + u % 2, P:2 * P], sT[:, u % 2, t * P:(t + 1) * P], v[:, 0, t, :], start=(t == 0), stop=(t == i))
                else:
                    count = wide(u)[0] // P
                    for t in range(count):
                        pe.matmul(G.ps[:, 6 + u % 2, 2 * P:3 * P], wT[:, u % 2, t * P:(t + 1) * P], v[:, 1, i + 1 - count + t, :],
                                  start=(t == 0), stop=(t == count - 1))
                    pe.matmul(G.ps[:, 6 + u % 2, 0:P], wT[0:NCB, u % 2, count * P:(count + 1) * P], G.cv[:, NB, :],
                              start=True, stop=True).then_inc(valued, 1)

            pe.wait_ge(kv_in, 64)
            with pe.Fori(0, GRP) as g:
                for u in range(U + 2):
                    if u >= 2:
                        turn(g, u - 2, 0)
                    if u < U:
                        scores(g, u, 0)
                    if u >= 2:
                        turn(g, u - 2, 1)
                        values(g, u - 2, 0)
                    if u < U:
                        scores(g, u, 1)
                    if u >= 2:
                        values(g, u - 2, 1)

        @block.vector
        def _(dve):
            def least_of(g, u, out, scores, bias, column, at):
                dve.memset(carrier[:, 3 * u + column:3 * u + column + 1], 0.0)
                return dve.tensor_tensor_reduce(out=out, in0=scores, in1=bias, scale=1.0, scalar=3e38, op0=ALU.add, op1=ALU.min,
                                                accum_out=least[:, u % 4, at:at + 1])

            def selected(g, u):
                i, j = u % TILES, u // TILES
                n = (i + 1) * P
                if i == 0:
                    dve.wait_ge(q_in[j], g * 16 + 16)
                    dve.tensor_scalar(q[:, j, :], q[:, j, :], -HD ** -0.5, None, ALU.mult).then_inc(q_scaled, 1)
                    dve.wait_ge(bias_made, g * 6 + j * 3 + 3)
                dve.wait_ge(t_ready[1], g * U + max(u - 3, 0))
                dve.wait_ge(s_ready[0], g * U + u + 1)
                least_of(g, u, probs_s[:, u % 4, 0:n], G.ps[:, 0:2, :].rearrange("p a n -> p (a n)")[:, 0:n], bias_s[:, j, SEQ - n:SEQ],
                         0, 1).then_inc(biased[0], 1)

            def window_and_compressed(g, u):
                i, j = u % TILES, u // TILES
                w, w0 = wide(u)
                dve.wait_ge(s_ready[1], g * U + u + 1)
                least_of(g, u, probs_w[:, u % 4, 0:w], G.ps[:, 2:4, :].rearrange("p a n -> p (a n)")[:, 0:w], bias_w[:, j, w0:WK], 1, 2)
                least_of(g, u, probs_w[:, u % 4, WK:WK + NCB], G.ps[:, 3, P:P + NCB], bias_c[:, j, i * NCB:(i + 1) * NCB],
                         2, 0).then_inc(biased[1], 1)
                if i == TILES - 1:
                    dve.memset(carrier[:, 3 * U + j:3 * U + j + 1], 0.0).then_inc(head_scored[j], 1)

            def copy_t(g, u):
                count = wide(u)[0] // P
                n = count * P
                dve.wait_ge(t_ready[1], g * U + u + 1)
                dve.wait_ge(valued, g * U + max(u - 1, 0))
                both = G.ps[:, 4:6, :].rearrange("p a n -> p (a n)")
                dve.tensor_copy(wT[:, u % 2, 0:n], both[:, 0:n])
                dve.tensor_copy(wT[0:NCB, u % 2, n:n + P], both[0:NCB, n:n + P]).then_inc(t_copied[1], 1)

            def combine(g, u):
                i, j = u % TILES, u // TILES
                s = u % 4
                done = (g * U + u) * JOIN
                o = G.ps[:, 6 + u % 2, 0:3 * P].rearrange("p (k d) -> p k d", k=3)[:, :, j * HD:(j + 1) * HD]
                out = G.o_n[:, i, bass.ds(g * P + j * HD, HD)]
                dve.wait_ge(valued, g * U + u + 1)
                dve.reciprocal(share[:, s, :], total[:, s, :]).then_inc(combined, 1)
                dve.wait_ge(combined, (g * U + u) * 2 + 1)
                dve.tensor_tensor(share[:, s, :], share[:, s, :], G.gates_t[:, i, bass.ds(g * 3 + j * GRP * 3, 3)], ALU.mult).then_inc(combined, 1)
                dve.wait_ge(combined, (g * U + u) * 2 + 2)
                dve.tensor_scalar(out, o[:, 0, :], share[:, s, 0:1], None, ALU.mult).then_inc(joined, 1)
                dve.wait_ge(joined, done + 1)
                dve.scalar_tensor_tensor(out, o[:, 1, :], share[:, s, 1:2], out, ALU.mult, ALU.add).then_inc(joined, 1)
                dve.wait_ge(joined, done + 2)
                dve.scalar_tensor_tensor(out, o[:, 2, :], share[:, s, 2:3], out, ALU.mult, ALU.add).then_inc(joined, 2)

            dve.wait_ge(q_cleared, 1)
            with dve.Fori(0, GRP) as g:
                for u in range(U + 3):
                    if u < U:
                        selected(g, u)
                    if 2 <= u < U + 2:
                        copy_t(g, u - 2)
                    if u < U:
                        window_and_compressed(g, u)
                    if u >= 3:
                        combine(g, u - 3)

        @block.scalar
        def _(act):
            def tables(g):
                act.wait_ge(biased[1], g * U)
                for j in range(2):
                    slope = G.slopes[:, bass.ds(g + (DIFF_H + j * GRP), 1)]
                    act.activation(bias_s[:, j, :], G.causal[:], ACT.Copy, scale=slope).then_inc(bias_made, 1)
                    act.activation(bias_w[:, j, :], G.causal_w[:], ACT.Copy, scale=slope).then_inc(bias_made, 1)
                    act.activation(bias_c[:, j, :], G.causal_c[:], ACT.Copy, scale=slope).then_inc(bias_made, 1)

            def exps(g, u):
                s, n, w = u % 4, (u % TILES + 1) * P, wide(u)[0]
                act.wait_ge(biased[0], g * U + u + 1)
                act.wait_ge(joined, (g * U + max(u - 3, 0)) * JOIN)
                for c, x, at in ((0, probs_s[:, s, 0:n], 1), (1, probs_w[:, s, 0:w], 2), (1, probs_w[:, s, WK:WK + NCB], 0)):
                    if at == 2:
                        act.wait_ge(biased[1], g * U + u + 1)
                    last = act.activation(x, x, ACT.Exp, bias=least[:, s, at:at + 1], scale=-1.0, accum_out=total[:, s, at:at + 1])
                    if at != 2:
                        last.then_inc(exped[c], 1)

            def copy_t(g, u):
                n = (u % TILES + 1) * P
                act.wait_ge(t_ready[0], g * U + u + 1)
                act.wait_ge(valued, g * U + max(u - 1, 0))
                act.activation(sT[:, u % 2, 0:n], G.ps[:, 4:6, :].rearrange("p a n -> p (a n)")[:, 0:n], ACT.Copy).then_inc(t_copied[0], 1)

            with act.Fori(0, GRP) as g:
                tables(g)
                for u in range(U + 2):
                    if u >= 2:
                        copy_t(g, u - 2)
                    if u < U:
                        exps(g, u)


def turn_outputs(nc, G):
    BW = 4 * P
    with ExitStack() as ctx:
        def sb(name, shape, dt=F32):
            return ctx.enter_context(nc.sbuf_tensor(f"to_{name}", shape, dt))
        sq, ss, sq_s, rms_s = sb("sq", [P, TILES * DIFF_H, VD]), sb("ss", [P, TILES * DIFF_H]), sb("sq_s", [P, DIFF_H * NS]), sb("rms_s", [P, DIFF_H * NS])
        sem = sem_maker(nc, ctx, "to")
        step, s_summed, rooted, turned, high, low, s_high = (sem(x) for x in ("step", "s_summed", "rooted", "turned", "high", "low", "s_high"))
        block = ctx.enter_context(nc.Block())
        od = G.od[:].rearrange("p i (h d) -> p (i h) d", d=VD)
        s_od = G.s_odT[:].rearrange("p h b t -> p (h b t)")
        groups = 2 * TILES
        SCALED = 6

        @block.tensor
        def _(pe):
            for n in range(groups):
                which, i = n // TILES, n % TILES
                if n >= 4:
                    pe.wait_ge(low, n - 3)
                if n == TILES:
                    pe.wait_ge(step, SCALED)
                src = (G.o_n, G.od)[which]
                for t in range(4):
                    last = pe.transpose(G.ps[:, n % 4, t * P:(t + 1) * P], src[:, i, t * P:(t + 1) * P], G.ident[:])
                last.then_inc(turned, 1)
                if n == 3:
                    pe.wait_ge(step, 1)
                    pe.matmul(G.ps[:, 4, 0:DIFF_H * NS], G.ones[:], sq_s[:], start=True, stop=True).then_inc(s_summed, 1)

        @block.scalar
        def _(act):
            def hi(n):
                dst = (G.onh, G.odh)[n // TILES][:, :, (n % TILES) * P:(n % TILES + 1) * P]
                act.wait_ge(turned, n + 1)
                act.activation(dst, G.ps[:, n % 4, 0:BW].rearrange("p (k t) -> p k t", k=4), ACT.Copy).then_inc(high, 1)

            act.activation(G.onh[:, :, SEQ:SEQ + NS], G.s_onT[:].rearrange("p a b t -> p a (b t)"), ACT.Copy).then_inc(s_high, 1)
            for n in range(4):
                hi(n)
            act.wait_ge(step, 3)
            act.wait_ge(s_summed, 1)
            act.activation(ss[:], ss[:], ACT.Sqrt, bias=G.eps[:], scale=1.0 / VD)
            act.activation(rms_s[:], G.ps[:, 4, 0:DIFF_H * NS], ACT.Sqrt, bias=G.eps[:], scale=1.0 / VD).then_inc(rooted, 1)
            for n in range(4, TILES):
                hi(n)
            act.wait_ge(step, SCALED + 1)
            act.activation(G.odh[:, :, SEQ:SEQ + NS], G.s_odT[:].rearrange("p a b t -> p a (b t)"), ACT.Copy).then_inc(s_high, 1)
            for n in range(TILES, groups):
                hi(n)

        @block.vector
        def _(dve):
            done = [0]

            def then(ins):
                done[0] += 1
                ins.then_inc(step, 1)
                dve.wait_ge(step, done[0])

            def lo(n):
                part = slice((n % TILES) * P, (n % TILES + 1) * P)
                h, l = ((G.onh, G.onl), (G.odh, G.odl))[n // TILES]
                dve.wait_ge(high, n + 1)
                dve.tensor_tensor(l[:, :, part], G.ps[:, n % 4, 0:BW].rearrange("p (k t) -> p k t", k=4), h[:, :, part].bitcast(F32),
                                  ALU.subtract).then_inc(low, 1)

            then(dve.tensor_tensor(sq_s[:], s_od, s_od, ALU.mult))
            then(dve.tensor_tensor(sq[:], od, od, ALU.mult))
            then(dve.tensor_reduce(ss[:], sq[:], AX, ALU.add))
            for n in range(4):
                lo(n)
            dve.wait_ge(rooted, 1)
            then(dve.reciprocal(ss[:], ss[:]))
            then(dve.reciprocal(rms_s[:], rms_s[:]))
            then(dve.tensor_tensor(od, od, ss[:].rearrange("p (n o) -> p n o", o=1).to_broadcast([P, TILES * DIFF_H, VD]), ALU.mult))
            then(dve.tensor_tensor(s_od, s_od, rms_s[:], ALU.mult))
            for n in range(4, TILES):
                lo(n)
            dve.wait_ge(s_high, 2)
            for h, l, s in ((G.onh, G.onl, G.s_onT), (G.odh, G.odl, G.s_odT)):
                dve.tensor_tensor(l[:, :, SEQ:SEQ + NS], s[:].rearrange("p a b t -> p a (b t)"), h[:, :, SEQ:SEQ + NS].bitcast(F32), ALU.subtract)
            for n in range(TILES, groups):
                lo(n)

        @block.gpsimd
        def _(pool):
            for x in (G.onh, G.onl, G.odh, G.odl):
                pool.memset(x[:, :, SEQ + NS:NT].bitcast(F32), 0.0)


def merge_up(nc, G):
    rounds = KD // 2
    with ExitStack() as ctx:
        def sb(name, shape, dt=F32):
            return ctx.enter_context(nc.sbuf_tensor(f"mu_{name}", shape, dt))
        raw, wh, wl = sb("raw", [P, 4, 4 * P]), sb("wh", [P, 4, 4 * P], F32R), sb("wl", [P, 4, 4 * P], F32R)
        gate = sb("gate", [P, 4, NT])
        gain = sb("gain", [P, 1])
        sem = sem_maker(nc, ctx, "mu")
        raw_in, gate_in, w_high, w_split, acc_ready, opened, weighed = (
            [sem(f"{what}{q}") for q in range(4)] for what in ("raw_in", "gate_in", "w_high", "w_split", "acc_ready", "opened", "weighed"))
        m_made, m_out = ([sem(f"{what}{p}") for p in range(2)] for what in ("m_made", "m_out"))
        gain_in, gain_scaled = sem("gain_in"), sem("gain_scaled")
        block = ctx.enter_context(nc.Block())
        operands = ((G.onh, G.onl), (G.odh, G.odl))
        w = (wh, wl)
        LOADS = (2, 1)

        @block.sync
        def _(sp):
            sp.dma_start(gain[:], G.g_subln).then_inc(gain_in, 16)
            with sp.Fori(0, rounds) as r:
                for q in range(4):
                    p, s = q // 2, q % 2
                    cols = bass.ds(r * (2 * P) + p * P, P)
                    dst = raw[:, q, :].rearrange("p (k n) -> p k n", k=4)
                    sp.wait_ge(w_split[q], r)
                    if s == 0:
                        src = G.w_up_nsa[:, cols].rearrange("(h g d) n -> h d g n", h=KVH, g=GRP)
                        for h in range(KVH):
                            sp.dma_start(dst[h * HD:(h + 1) * HD, :, :], src[h]).then_inc(raw_in[q], 16)
                    else:
                        sp.dma_start(dst, G.w_up_diff[:, cols].rearrange("(k p) n -> p k n", p=P)).then_inc(raw_in[q], 16)
                for q in range(4):
                    p, s = q // 2, q % 2
                    if s == 0:
                        sp.wait_ge(m_out[p], r * 16)
                    else:
                        sp.wait_ge(m_made[p], r)
                    sp.dma_start(gate[:, q, :], G.z[bass.ds(r * 2 + (Z_MG + s * KD + p), 1), :, :].rearrange("o p n -> (o p) n")).then_inc(gate_in[q], 16)

        @block.gpsimd
        def _(pool):
            with pool.Fori(0, rounds) as r:
                for p in range(2):
                    pool.wait_ge(m_made[p], r + 1)
                    pool.dma_start(G.m[bass.ds(r * 2 + p, 1), :, :].rearrange("o p n -> (o p) n"), gate[:, 2 * p, :]).then_inc(m_out[p], 16)
            for p in range(2):
                pool.wait_ge(m_out[p], 16 * rounds)

        @block.scalar
        def _(act):
            def hi(r, q):
                act.wait_ge(raw_in[q], (r + 1) * (16 * LOADS[q % 2]))
                act.wait_ge(acc_ready[q], r)
                act.activation(wh[:, q, :], raw[:, q, :], ACT.Copy, scale=gain[:] if q % 2 else 1.0).then_inc(w_high[q], 1)

            def open_gate(r, q):
                act.wait_ge(gate_in[q], (r + 1) * 16)
                act.activation(gate[:, q, :], gate[:, q, :], ACT.Sigmoid).then_inc(opened[q], 1)

            act.wait_ge(gain_scaled, 1)
            for q in range(4):
                hi(0, q)
            with act.Fori(0, rounds - 1) as r:
                for q in range(4):
                    open_gate(r, q)
                for q in range(4):
                    hi(r + 1, q)
            for q in range(4):
                open_gate(rounds - 1, q)

        @block.vector
        def _(dve):
            def lo(r, q):
                dve.wait_ge(w_high[q], r + 1)
                if q % 2:
                    dve.scalar_tensor_tensor(wl[:, q, :], raw[:, q, :], gain[:], wh[:, q, :].bitcast(F32), ALU.mult, ALU.subtract).then_inc(w_split[q], 1)
                else:
                    dve.tensor_tensor(wl[:, q, :], raw[:, q, :], wh[:, q, :].bitcast(F32), ALU.subtract).then_inc(w_split[q], 1)

            def weigh(r, q):
                s = q % 2
                dve.wait_ge(opened[q], r + 1)
                dve.wait_ge(acc_ready[q], r + 1)
                x = chunks(gate[:, q, :])
                dve.tensor_tensor(x, x, G.ps[:, 3 * s:3 * s + NCH, 0:CH], ALU.mult).then_inc(weighed[q], 1)

            def add(r, p):
                for s in range(2):
                    dve.wait_ge(weighed[2 * p + s], r + 1)
                dve.tensor_tensor(gate[:, 2 * p, :], gate[:, 2 * p, :], gate[:, 2 * p + 1, :], ALU.add).then_inc(m_made[p], 1)

            dve.wait_ge(gain_in, 16)
            dve.tensor_scalar(gain[:], gain[:], 1.0 - LAM_INIT, None, ALU.mult).then_inc(gain_scaled, 1)
            dve.wait_ge(gain_scaled, 1)
            for q in range(4):
                lo(0, q)
            with dve.Fori(0, rounds - 1) as r:
                for q in range(4):
                    weigh(r, q)
                    if q % 2:
                        add(r, q // 2)
                    lo(r + 1, q)
            for q in range(4):
                weigh(rounds - 1, q)
                if q % 2:
                    add(rounds - 1, q // 2)

        @block.tensor
        def _(pe):
            with pe.Fori(0, rounds) as r:
                for q in range(4):
                    p, s = q // 2, q % 2
                    pe.wait_ge(w_split[q], r + 1)
                    pe.wait_ge(weighed[s + 2 * (1 - p)], r + p)
                    for c in range(NCH):
                        for k in range(4):
                            for n, (a, b) in enumerate(PAIRS):
                                last = pe.matmul(G.ps[:, 3 * s + c, 0:CH], w[a][:, q, k * P:(k + 1) * P], operands[s][b][:, k, c * CH:(c + 1) * CH],
                                                 start=(k == 0 and n == 0), stop=(k == 3 and n == 2))
                    last.then_inc(acc_ready[q], 1)


def merge_out(nc, G):
    rounds = KD // 2
    with ExitStack() as ctx:
        def sb(name, shape, dt):
            return ctx.enter_context(nc.sbuf_tensor(f"mo_{name}", shape, dt))
        hh, hl = sb("hh", [P, KD, NT], F32R), sb("hl", [P, KD, NT], F32R)
        tmp = [sb(f"tmp{i}", [P, NT], F32) for i in range(2)]
        f = sb("f", [P, KD, NT], F32)
        with ExitStack() as inner:
            raw = inner.enter_context(nc.sbuf_tensor("mo_raw", [P, 2, D], F32))
            wh = inner.enter_context(nc.sbuf_tensor("mo_wh", [P, 2, D], F32R))
            wl = inner.enter_context(nc.sbuf_tensor("mo_wl", [P, 2, D], F32R))
            sem = sem_maker(nc, inner, "mo")
            m_in, m_high, m_split = [sem(f"m_in{k}") for k in range(KD)], sem("m_high"), sem("m_split")
            raw_in, w_high, w_split, f_ready, f_copied = (
                [sem(f"{what}{j}") for j in range(2)] for what in ("raw_in", "w_high", "w_split", "f_ready", "f_copied"))
            x_in = sem("x_in")
            block = inner.enter_context(nc.Block())
            w, h = (wh, wl), (hh, hl)

            @block.sync
            def _(sp):
                for k in range(KD):
                    sp.dma_start(f[:, k, :], G.m[k]).then_inc(m_in[k], 16)
                for k in range(KD):
                    sp.dma_start(G.xT[:, k, :], G.x_kept[k]).then_inc(x_in, 16)
                sp.wait_ge(x_in, 16 * KD)

            @block.gpsimd
            def _(pool):
                with pool.Fori(0, rounds) as r:
                    for j in range(2):
                        pool.wait_ge(w_split[j], r)
                        pool.dma_start(raw[:, j, :].rearrange("p (k n) -> p k n", k=KD),
                                       G.w_out[:, bass.ds(r * (2 * P) + j * P, P)].rearrange("(k p) n -> p k n", p=P)).then_inc(raw_in[j], 16)

            @block.scalar
            def _(act):
                def hi(r, j):
                    act.wait_ge(raw_in[j], r * 16 + 16)
                    act.wait_ge(f_ready[j], r)
                    act.activation(wh[:, j, :], raw[:, j, :], ACT.Copy).then_inc(w_high[j], 1)

                def copy_f(r, j):
                    act.wait_ge(f_ready[j], r + 1)
                    act.activation(f[:, bass.ds(r * 2 + j, 1), :].rearrange("p o (c n) -> p (o c) n", c=NCH), G.ps[:, 3 * j:3 * j + NCH, 0:CH],
                                   ACT.Copy).then_inc(f_copied[j], 1)

                hi(0, 0)
                hi(0, 1)
                for k in range(KD):
                    act.wait_ge(m_in[k], 16)
                    act.activation(hh[:, k, :], f[:, k, :], ACT.Copy).then_inc(m_high, 1)
                with act.Fori(0, rounds - 1) as r:
                    for j in range(2):
                        copy_f(r, j)
                        hi(r + 1, j)
                for j in range(2):
                    copy_f(rounds - 1, j)

            @block.vector
            def _(dve):
                def lo(r, j):
                    dve.wait_ge(w_high[j], r + 1)
                    dve.tensor_tensor(wl[:, j, :], raw[:, j, :], wh[:, j, :].bitcast(F32), ALU.subtract).then_inc(w_split[j], 1)

                lo(0, 0)
                lo(0, 1)
                for k in range(KD):
                    dve.wait_ge(m_high, k + 1)
                    dve.tensor_tensor(hl[:, k, :], f[:, k, :], hh[:, k, :].bitcast(F32), ALU.subtract).then_inc(m_split, 1)
                with dve.Fori(1, rounds) as r:
                    lo(r, 0)
                    lo(r, 1)

            @block.tensor
            def _(pe):
                pe.wait_ge(m_split, KD)
                with pe.Fori(0, rounds) as r:
                    for j in range(2):
                        pe.wait_ge(w_split[j], r + 1)
                        pe.wait_ge(f_copied[j], r)
                        for c in range(NCH):
                            for k in range(KD):
                                for n, (a, b) in enumerate(PAIRS):
                                    last = pe.matmul(G.ps[:, 3 * j + c, 0:CH], w[a][:, j, k * P:(k + 1) * P], h[b][:, k, c * CH:(c + 1) * CH],
                                                     start=(k == 0 and n == 0), stop=(k == KD - 1 and n == 2))
                        last.then_inc(f_ready[j], 1)
        norm_add(nc, G, "mop", G.gains["g_mix_post"], f, 1.0, tmp)


def store_tokens(nc, G):
    tiles = SEQ // P + 1
    with ExitStack() as ctx:
        rows = ctx.enter_context(nc.sbuf_tensor("st_rows", [P, 3, D], F32))
        sem = sem_maker(nc, ctx, "st")
        transposed = sem("transposed")
        copied = [sem("copied_act"), sem("copied_dve")]
        rows_out = [sem(f"rows_out{i}") for i in range(3)]
        block = ctx.enter_context(nc.Block())

        def size(i):
            return P if i < tiles - 1 else NS

        @block.sync
        def _(sp):
            for i in range(tiles):
                for c in copied:
                    sp.wait_ge(c, i + 1)
                dst = G.y_prompt[i * P:(i + 1) * P, :] if i < tiles - 1 else G.y_sample
                sp.dma_start(dst, rows[0:size(i), i % 3, :]).then_inc(rows_out[i % 3], 16)
            for i in range(3):
                sp.wait_ge(rows_out[i], 16 * (tiles // 3))

        @block.tensor
        def _(pe):
            for i in range(tiles):
                for half in range(2):
                    if i >= 2:
                        pe.wait_ge(copied[half], i - 1)
                    for t in range(4):
                        last = pe.transpose(G.ps[0:size(i), 2 * half + i % 2, t * P:(t + 1) * P], G.xT[:, 4 * half + t, i * P:i * P + size(i)],
                                            G.ident[:])
                    last.then_inc(transposed, 1)

        def copy_half(eng, half, copy):
            for i in range(tiles):
                eng.wait_ge(transposed, 2 * i + half + 1)
                if i >= 3:
                    eng.wait_ge(rows_out[i % 3], 16 * (i // 3))
                copy(rows[0:size(i), i % 3, half * 512:(half + 1) * 512], G.ps[0:size(i), 2 * half + i % 2, :]).then_inc(copied[half], 1)

        @block.scalar
        def _(act):
            copy_half(act, 0, lambda dst, src: act.activation(dst, src, ACT.Copy))

        @block.vector
        def _(dve):
            copy_half(dve, 1, lambda dst, src: dve.tensor_copy(dst, src))


def step_kernel(nc, a):
    G = Parts()
    G.x_prompt, G.x_sample, G.c_ident = a["x_prompt"], a["x_sample"], a["t_ident"]
    G.w_in, G.w_out, G.w_up_nsa, G.w_up_diff = a["w_in"], a["w_out"], a["w_up_nsa"], a["w_up_diff"]
    G.cmp_w1, G.cmp_w2, G.cmp_b1 = a["cmp_w1"], a["cmp_w2"], a["cmp_b1"].rearrange("k e -> e k")
    G.cache_nsa, G.cache_diff, G.win, G.page_table = a["cache_nsa_kv"], a["cache_diff_kv"], a["state_win_kv"], a["page_table"]
    G.lambda_qk = a["lambda_qk"]
    G.g_subln = a["g_diff_subln"].rearrange("(p o) -> p o", o=1)
    G.y_prompt, G.y_sample = a["y_prompt"], a["y_sample"]
    G.nsa_p, G.nsa_s, G.diff_p, G.diff_s = a["nsa_kv_prompt"], a["nsa_kv_sample"], a["diff_kv_prompt"], a["diff_kv_sample"]
    G.win_p, G.win_s = a["win_kv_prompt"], a["win_kv_sample"]
    G.z = nc.dram_tensor("z_scratch", [Z_NG + 1, P, NT], F32).ap()
    G.m = nc.dram_tensor("m_scratch", [KD, P, NT], F32).ap()
    G.x_kept = nc.dram_tensor("x_scratch", [KD, P, NT], F32).ap()
    G.kvw = nc.dram_tensor("kvw_scratch", [SEQ + NS, 2 * KV1], F32).ap()
    G.tr_stores = {}
    G.gains = {n: a[n].rearrange("(k p) -> p k", p=P) for n in
               ("g_ffn1_pre", "g_ffn1_post", "g_mix_pre", "g_mix_post", "g_ffn2_pre", "g_ffn2_post")}
    with ExitStack() as ctx:
        ctx.enter_context(nc.allow_non_contiguous_dma(reason="gain vectors and gates, a few kilobytes"))

        def placer(stack):
            def sb(name, shape, dt=F32):
                return stack.enter_context(nc.sbuf_tensor(name, shape, dt))
            return sb

        sb = placer(ctx)
        G.ps = ctx.enter_context(nc.psum_tensor("ps", [P, 8, 512], F32))
        G.ident, G.ones, G.eps = sb("ident", [P, P]), sb("ones", [P, P]), sb("eps", [P, 1])
        G.gain = sb("gain", [P, KD])

        def with_tokens(part):
            with ExitStack() as inner:
                place = placer(inner)
                G.xT, G.rms = place("xT_" + part.__name__, [P, KD, NT]), place("rms_" + part.__name__, [P, NT])
                part()

        def before():
            load_tokens(nc, G)
            ffn(nc, G, "f1", a["ffn1_w1"], a["ffn1_w3"], a["ffn1_w2"], G.gains["g_ffn1_pre"], G.gains["g_ffn1_post"])
            project(nc, G)

        def after():
            merge_out(nc, G)
            ffn(nc, G, "f2", a["ffn2_w1"], a["ffn2_w3"], a["ffn2_w2"], G.gains["g_ffn2_pre"], G.gains["g_ffn2_post"])
            store_tokens(nc, G)

        with_tokens(before)
        token_rows(nc, G)
        with ExitStack() as mix:
            place = placer(mix)
            tables = []

            def table(put, name):
                t = put("c_" + name, list(a["t_" + name].shape))
                tables.append((t[:], a["t_" + name]))
                return t

            G.s_odT, G.s_onT = place("s_odT", [P, DIFF_H, NB, TS]), place("s_onT", [P, GRP, NB, TS])
            G.nlam, G.sgn_d = place("nlam", [P, 1]), place("sgn_d", [P, 1])
            G.gates_t, G.gates_s = place("gates_t", [P, TILES, N_GATE]), place("gates_s", [ROWS, NB, 3])
            G.ckT, G.cv = place("ckT", [P, NB + 1, NBLK]), place("cv", [NBLK, NB + 1, P])
            G.slopes, G.row_valid, component = table(place, "slopes"), table(place, "row_valid"), table(place, "component")
            fill(nc, G, "shared", tables)
            lambda_scale(nc, G)
            sign(nc, G, component)
            gates(nc, G)
            with ExitStack() as part:
                put = placer(part)
                G.pt = put("pt", [1, NB * PAGES], I32)
                G.o_cmp, G.drop = put("o_cmp", [ROWS, NB, P]), put("drop", [ROWS, NB, NBLK])
                compress(nc, G)
                tables.clear()
                G.bias_cmp, G.group_sum = table(put, "bias_cmp"), table(put, "group_sum")
                G.bias_d, G.bias_new_d, G.off_d, G.comb_d = (table(put, x) for x in ("bias_d", "bias_new_d", "off_d", "comb_d"))
                G.bias_n, G.bias_w, G.bias_new_n, G.off_n = (table(put, x) for x in ("bias_n", "bias_w", "bias_new_n", "off_n"))
                fill(nc, G, "sample", tables)
                sample_select(nc, G)
                sample_attend(nc, G)
            with ExitStack() as part:
                put = placer(part)
                G.onh, G.onl, G.odh, G.odl = (put(x, [P, 4, NT], F32R) for x in ("onh", "onl", "odh", "odl"))
                with ExitStack() as rows:
                    put_rows = placer(rows)
                    G.od, G.o_n = put_rows("od", [P, TILES, DIFF_H * VD]), put_rows("o_n", [P, TILES, NSA_H * HD])
                    with ExitStack() as attend:
                        put_tables = placer(attend)
                        tables.clear()
                        G.causal, G.causal_w, G.causal_c = (table(put_tables, x) for x in ("causal", "causal_w", "causal_c"))
                        fill(nc, G, "prompt", tables)
                        prompt_diff(nc, G)
                        prompt_nsa(nc, G)
                    turn_outputs(nc, G)
                merge_up(nc, G)
        with_tokens(after)


def sign(nc, G, component):
    with ExitStack() as ctx:
        signed = sem_maker(nc, ctx, "sg")("signed")
        block = ctx.enter_context(nc.Block())

        @block.vector
        def _(dve):
            dve.tensor_tensor(G.sgn_d[:], G.nlam[:], component[:, 1:2], ALU.mult).then_inc(signed, 1)
            dve.wait_ge(signed, 1)
            dve.tensor_tensor(G.sgn_d[:], G.sgn_d[:], component[:, 0:1], ALU.add)


def shape_tables():
    import numpy as np
    far, masked = 1e32, 1e30
    d_slope = 2.0 ** (-8.0 * np.arange(1, DIFF_H + 1) / DIFF_H)
    n_slope = 2.0 ** (-8.0 * np.arange(1, NSA_H + 1) / NSA_H)
    t = {"ident": np.eye(P)}
    t["slopes"] = np.tile(np.concatenate([d_slope, n_slope]), (P, 1))
    tok = np.arange(P)[:, None]
    t["row_valid"] = tok >= BLK - 1
    r = np.arange(P - SEQ, P)[None]
    t["causal"] = np.where(r <= tok, -r, far)
    r = np.arange(-WIN, P)[None]
    t["causal_w"] = np.where((r <= tok) & (tok - r < WIN), -r, far)
    half, page = np.arange(NCB) // PAGES, np.arange(NCB) % PAGES
    end = (2 * page + half + 1) * BLK - 1
    qpos = (np.arange(TILES)[None, :, None] * P + tok[:, :, None])
    t["causal_c"] = np.where((page < TILES) & (end <= qpos), -end, far).reshape(P, TILES * NCB)
    i = np.arange(P)
    head, comp, tt = i // 32, (i % 32) // TS, (i % TS)[:, None]
    t["component"] = np.stack([comp == 0, comp == 1], 1)
    sd = np.where(comp < 2, d_slope[head], 0.0)[:, None]
    past = PAGES * PAGE
    t["bias_d"] = -sd * np.arange(QT)
    t["bias_new_d"] = np.where(np.arange(TS) > tt, masked, -sd * np.arange(TS))
    t["off_d"] = np.concatenate([-sd * (QT * np.arange(QUADS) - past), 0 * sd], 1)
    comb = np.zeros((P, 32))
    on = comp < 2
    comb[i[on], TS * head[on] + i[on] % TS] = 1
    t["comb_d"] = comb
    i = np.arange(ROWS)
    sn, tt = n_slope[i // TS][:, None], (i % TS)[:, None]
    t["bias_n"] = -sn * np.arange(QT)
    t["bias_w"] = np.where(np.arange(WIN) <= tt, masked, -sn * np.arange(WIN))
    t["bias_new_n"] = np.where(np.arange(TS) > tt, masked, -sn * np.arange(TS))
    t["off_n"] = np.concatenate([-sn * (QT * np.arange(QUADS) - past), 0 * sn, sn * WIN, 0 * sn], 1)
    t["bias_cmp"] = -sn * (end - past)
    t["group_sum"] = (i[:, None] // (GRP * TS) == i // (GRP * TS)) & (i[:, None] % TS == i % TS)
    return {"t_" + k: np.ascontiguousarray(v, dtype=np.float32) for k, v in t.items()}


OUTPUTS = (
    ("y_prompt", (SEQ, D), (1, SEQ, D)),
    ("y_sample", (NS, D), (NB, TS, D)),
    ("nsa_kv_prompt", (SEQ, 512), (1, 1, SEQ, 4, KVH, HD)),
    ("nsa_kv_sample", (NS, 512), (1, NB, TS, 4, KVH, HD)),
    ("diff_kv_prompt", (SEQ, 1024), (1, 1, SEQ, 2, DIFF_H, VD)),
    ("diff_kv_sample", (NS, 1024), (1, NB, TS, 2, DIFF_H, VD)),
    ("win_kv_prompt", (WIN, 256), (1, 1, WIN, 2, KVH, HD)),
    ("win_kv_sample", (NB, WIN, 256), (1, NB, WIN, 2, KVH, HD)),
)
SHAPES = {
    "x_prompt": (SEQ, D), "x_sample": (NS, D), "page_table": (1, NB * PAGES),
    "cache_nsa_kv": (N_POOL, PAGE, 512), "cache_diff_kv": (N_POOL, PAGE, 1024), "state_win_kv": (NB, WIN, 256),
}


def kernel(**inputs):
    import numpy as np
    import concourse.bacc as bacc
    from concourse.bass_utils import run_bass_kernel_spmd

    arrays = {}
    for name, x in inputs.items():
        x = np.ascontiguousarray(x)
        arrays[name] = x.reshape(SHAPES.get(name, x.shape[1:]))
    arrays.update(shape_tables())
    nc = bacc.Bacc("TRN2", target_bir_lowering=False, num_devices=1)
    a = {name: nc.dram_tensor(name, x.shape, mybir.dt.from_np(x.dtype), kind="ExternalInput").ap() for name, x in arrays.items()}
    for name, shape, _ in OUTPUTS:
        a[name] = nc.dram_tensor(name, shape, F32, kind="ExternalOutput").ap()
    step_kernel(nc, a)
    result = run_bass_kernel_spmd(nc, [arrays], core_ids=[0]).results[0]
    return tuple(result[name].reshape(shape) for name, _, shape in OUTPUTS)
```

```python
from contextlib import ExitStack

import concourse.bass as bass
from concourse import mybir

F32 = mybir.dt.float32
F32R = mybir.dt.float32r
I32 = mybir.dt.int32
ALU = mybir.AluOpType
ACT = mybir.ActivationFunctionType
AX = mybir.AxisListType.X

P = 128
D = 1024
KD = D // P
SEQ = 1024
NB = 8
TS = 8
NS = NB * TS
NCH = 3
CH = 364
NT = NCH * CH
D_FF = 2816
KF = D_FF // P
EPS = 1e-6
PAIRS = ((0, 0), (0, 1), (1, 0))


class Parts:
    pass


def sem_maker(nc, ctx, stage):
    made = []

    def give_back():
        nc.clear_and_free_semaphores(made)
        nc.all_engine_barrier()

    ctx.callback(give_back)

    def sem(name):
        made.append(nc.alloc_semaphore(f"{stage}_{name}"))
        return made[-1]
    return sem


def chunks(ap):
    return ap.rearrange("p (c n) -> p c n", c=NCH)


def load_tokens(nc, G):
    tiles = SEQ // P + 1
    with ExitStack() as ctx:
        sem = sem_maker(nc, ctx, "lt")
        rows = ctx.enter_context(nc.sbuf_tensor("lt_rows", [P, tiles, D], F32))
        row_in = [sem(f"row_in{i}") for i in range(tiles)]
        const_in, const_set, transposed, evacuated = sem("const_in"), sem("const_set"), sem("transposed"), sem("evacuated")
        block = ctx.enter_context(nc.Block())

        def size(i):
            return P if i < tiles - 1 else NS

        @block.sync
        def _(sp):
            sp.dma_start(G.ident[:], G.c_ident).then_inc(const_in, 16)
            for i in range(tiles):
                src = G.x_prompt[i * P:(i + 1) * P, :] if i < tiles - 1 else G.x_sample
                sp.dma_start(rows[0:size(i), i, :], src).then_inc(row_in[i], 16)

        @block.gpsimd
        def _(pool):
            pool.memset(G.ones[:], 1.0).then_inc(const_set, 1)
            pool.memset(G.eps[:], EPS).then_inc(const_set, 1)
            pool.memset(G.xT[:, :, SEQ + NS:NT], 0.0).then_inc(const_set, 1)

        @block.tensor
        def _(pe):
            pe.wait_ge(const_in, 16)
            for i in range(tiles):
                pe.wait_ge(row_in[i], 16)
                for half in range(2):
                    n = 2 * i + half
                    if n >= 2:
                        pe.wait_ge(evacuated, n - 1)
                    for j in range(4):
                        k = 4 * half + j
                        last = pe.transpose(G.ps[:, n % 2, j * P:j * P + size(i)], rows[0:size(i), i, k * P:(k + 1) * P],
                                            G.ident[0:size(i), 0:size(i)])
                    last.then_inc(transposed, 1)

        @block.vector
        def _(dve):
            for i in range(tiles):
                for half in range(2):
                    n = 2 * i + half
                    dve.wait_ge(transposed, n + 1)
                    src = G.ps[:, n % 2, :].rearrange("p (j t) -> p j t", j=4)[:, :, 0:size(i)]
                    dve.tensor_copy(G.xT[:, 4 * half:4 * half + 4, i * P:i * P + size(i)], src).then_inc(evacuated, 1)
            dve.wait_ge(const_set, 3)


def rms_engines(nc, G, sem, src, tmp):
    squared, gathered, summed, rooted, scale_ready = (sem(x) for x in ("squared", "gathered", "summed", "rooted", "scale_ready"))

    def act_part(act):
        for k in range(KD):
            if k >= 3:
                act.wait_ge(gathered, k - 2)
            act.activation(tmp[k % 2] if k else G.rms[:], src[:, k, :], ACT.Square).then_inc(squared, 1)
        for c in range(NCH):
            act.wait_ge(summed, c + 1)
            act.activation(chunks(G.rms[:])[:, c, :], G.ps[:, c, 0:CH], ACT.Sqrt, bias=G.eps[:], scale=1.0 / D).then_inc(rooted, 1)

    def pe_part(pe):
        pe.wait_ge(gathered, KD - 1)
        for c in range(NCH):
            pe.matmul(G.ps[:, c, 0:CH], G.ones[:], G.rms[:, c * CH:(c + 1) * CH], start=True, stop=True).then_inc(summed, 1)

    def dve_part(dve):
        for k in range(1, KD):
            dve.wait_ge(squared, k + 1)
            if k >= 2:
                dve.wait_ge(gathered, k - 1)
            dve.tensor_tensor(G.rms[:], G.rms[:], tmp[k % 2], ALU.add).then_inc(gathered, 1)
        for c in range(NCH):
            dve.wait_ge(rooted, c + 1)
            r = chunks(G.rms[:])[:, c, :]
            dve.reciprocal(r, r).then_inc(scale_ready, 1)

    return act_part, pe_part, dve_part, scale_ready


def root_engines(nc, G, sem):
    rooted, scale_ready = sem("rooted"), sem("scale_ready")

    def act_part(act):
        for c in range(NCH):
            act.activation(chunks(G.rms[:])[:, c, :], G.ps[:, NCH + c, 0:CH], ACT.Sqrt, bias=G.eps[:], scale=1.0 / D).then_inc(rooted, 1)

    def dve_part(dve):
        for c in range(NCH):
            dve.wait_ge(rooted, c + 1)
            r = chunks(G.rms[:])[:, c, :]
            dve.reciprocal(r, r).then_inc(scale_ready, 1)

    return act_part, None, dve_part, scale_ready


def norm_split(nc, G, stage, gain, hh, hl, tmp, summed):
    with ExitStack() as ctx:
        sem = sem_maker(nc, ctx, stage)
        act_part, pe_part, dve_part, scale_ready = root_engines(nc, G, sem) if summed else rms_engines(nc, G, sem, G.xT, tmp)
        gain_in, normed, high = sem("gain_in"), sem("normed"), sem("high")
        low = [sem("low_even"), sem("low_odd")]
        block = ctx.enter_context(nc.Block())

        @block.sync
        def _(sp):
            sp.dma_start(G.gain[:], gain).then_inc(gain_in, 16)

        @block.scalar
        def _(act):
            act_part(act)
            for k in range(KD):
                act.wait_ge(normed, k + 1)
                act.activation(hh[:, k, :], tmp[k % len(tmp)], ACT.Copy).then_inc(high, 1)

        if pe_part:
            block.tensor(pe_part)

        def lo(eng, k):
            eng.wait_ge(high, k + 1)
            eng.tensor_tensor(hl[:, k, :], tmp[k % len(tmp)], hh[:, k, :].bitcast(F32), ALU.subtract).then_inc(low[k % 2], 1)

        @block.gpsimd
        def _(pool):
            for k in range(1, KD, 2):
                lo(pool, k)

        @block.vector
        def _(dve):
            dve_part(dve)
            dve.wait_ge(gain_in, 16)
            dve.wait_ge(scale_ready, NCH)
            for k in range(KD):
                if k >= len(tmp):
                    dve.wait_ge(low[k % 2], (k - len(tmp)) // 2 + 1)
                dve.scalar_tensor_tensor(tmp[k % len(tmp)], G.xT[:, k, :], G.gain[:, k:k + 1], G.rms[:],
                                         ALU.mult, ALU.mult).then_inc(normed, 1)
                if k % 2:
                    lo(dve, k - 1)


def norm_add(nc, G, stage, gain, src, factor, tmp, last=False):
    with ExitStack() as ctx:
        sem = sem_maker(nc, ctx, stage)
        act_part, pe_part, dve_part, scale_ready = rms_engines(nc, G, sem, src, tmp)
        gain_in, gain_scaled, normed, resquared = sem("gain_in"), sem("gain_scaled"), sem("normed"), sem("resquared")
        added = [sem("added_even"), sem("added_odd")]
        block = ctx.enter_context(nc.Block())

        @block.sync
        def _(sp):
            sp.dma_start(G.gain[:], gain).then_inc(gain_in, 16)

        @block.scalar
        def _(act):
            act_part(act)
            for k in range(0 if last else KD):
                act.wait_ge(added[k % 2], k // 2 + 1)
                act.activation(src[:, k, :], G.xT[:, k, :], ACT.Square).then_inc(resquared, 1)

        @block.tensor
        def _(pe):
            pe_part(pe)
            for k in range(0 if last else KD):
                pe.wait_ge(resquared, k + 1)
                for c in range(NCH):
                    pe.matmul(G.ps[:, NCH + c, 0:CH], G.ones[:], src[:, k, c * CH:(c + 1) * CH], start=(k == 0), stop=(k == KD - 1))

        def add(eng, k):
            eng.wait_ge(normed, k + 1)
            eng.tensor_tensor(G.xT[:, k, :], G.xT[:, k, :], src[:, k, :], ALU.add).then_inc(added[k % 2], 1)

        @block.gpsimd
        def _(pool):
            for k in range(1, KD, 2):
                add(pool, k)

        @block.vector
        def _(dve):
            dve.wait_ge(gain_in, 16)
            dve.tensor_scalar(G.gain[:], G.gain[:], factor, None, ALU.mult).then_inc(gain_scaled, 1)
            dve_part(dve)
            dve.wait_ge(gain_scaled, 1)
            dve.wait_ge(scale_ready, NCH)
            for k in range(KD):
                dve.scalar_tensor_tensor(src[:, k, :], src[:, k, :], G.gain[:, k:k + 1], G.rms[:],
                                         ALU.mult, ALU.mult).then_inc(normed, 1)
                if k % 2:
                    add(dve, k - 1)


def ffn(nc, G, stage, w1, w3, w2, g_pre, g_post, first):
    rounds = KF // 2
    with ExitStack() as ctx:
        def sb(name, shape, dt):
            return ctx.enter_context(nc.sbuf_tensor(f"{stage}_{name}", shape, dt))
        hh, hl = sb("hh", [P, KD, NT], F32R), sb("hl", [P, KD, NT], F32R)
        tmp = [sb(f"tmp{i}", [P, NT], F32) for i in range(2)]
        f = sb("f", [P, KD, NT], F32)
        norm_split(nc, G, f"{stage}n", g_pre, hh, hl, [f[:, k, :] for k in range(KD)], not first)
        with ExitStack() as inner:
            def sbi(name, shape, dt):
                return inner.enter_context(nc.sbuf_tensor(f"{stage}_{name}", shape, dt))
            raw = sbi("raw", [P, 3, D], F32)
            wh, wl = sbi("wh", [P, 3, D], F32R), sbi("wl", [P, 3, D], F32R)
            uh, ul = sbi("uh", [P, 2, NT], F32R), sbi("ul", [P, 2, NT], F32R)
            gate, u = chunks(tmp[0][:]), chunks(tmp[1][:])
            sem = sem_maker(nc, inner, stage)
            raw_in = [sem(f"raw_in{i}") for i in range(3)]
            w_high, w_split = sem("w_high"), sem("w_split")
            up1_ready, up3_ready, gated, u_made, u_high, u_split = (
                sem("up1_ready"), sem("up3_ready"), sem("gated"), sem("u_made"), sem("u_high"), sem("u_split"))
            down_ready, f_cleared = sem("down_ready"), sem("f_cleared")
            down_added = [sem("down_added_even"), sem("down_added_odd")]
            block = inner.enter_context(nc.Block())
            w = (wh, wl)
            h = (hh, hl)
            uu = (uh, ul)

            def piece_source(g, j):
                if j < 4:
                    wt = (w1, w3)[j % 2]
                    return wt[:, bass.ds((g * 2 + j // 2) * P, P)].rearrange("(k p) n -> p k n", p=P)
                return w2[bass.ds((g * 2 + j - 4) * P, P), :]

            def piece_buffer(buf, j):
                if j < 4:
                    return buf[:, j % 3, :].rearrange("p (k n) -> p k n", k=KD)
                return buf[:, j % 3, :]

            @block.sync
            def _(sp):
                for j in range(3):
                    sp.dma_start(piece_buffer(raw, j), piece_source(0, j)).then_inc(raw_in[j], 16)
                with sp.Fori(0, rounds - 1) as g:
                    for n in range(3, 9):
                        j = n % 6
                        sp.wait_ge(w_split, g * 6 + n - 2)
                        sp.dma_start(piece_buffer(raw, j), piece_source(g + n // 6, j)).then_inc(raw_in[n % 3], 16)
                for j in range(3, 6):
                    sp.wait_ge(w_split, (rounds - 1) * 6 + j - 2)
                    sp.dma_start(piece_buffer(raw, j), piece_source(rounds - 1, j)).then_inc(raw_in[j % 3], 16)

            @block.gpsimd
            def _(pool):
                pool.memset(f[:], 0.0).then_inc(f_cleared, 1)

            @block.scalar
            def _(act):
                def w_hi(g, j):
                    act.wait_ge(raw_in[j % 3], g * 32 + 16 * (j // 3 + 1))
                    freed, value = ((up3_ready, g * 6), (down_ready, g * KD), (down_ready, g * KD),
                                    (up1_ready, g * 6 + 3), (up3_ready, g * 6 + 3), (up1_ready, g * 6 + 6))[j]
                    act.wait_ge(freed, value)
                    act.activation(wh[:, j % 3, :], raw[:, j % 3, :], ACT.Copy).then_inc(w_high, 1)

                def silu(g, m, c):
                    act.wait_ge(up1_ready, g * 6 + m * NCH + c + 1)
                    act.wait_ge(u_made, g * 6 + m * (c + 1))
                    act.activation(gate[:, c, :], G.ps[:, c, 0:CH], ACT.Silu).then_inc(gated, 1)

                def u_hi(g, m, c):
                    act.wait_ge(u_made, g * 6 + m * NCH + c + 1)
                    act.activation(chunks(uh[:, m, :])[:, c, :], u[:, c, :], ACT.Copy).then_inc(u_high, 1)

                with act.Fori(0, rounds) as g:
                    for j in range(3):
                        w_hi(g, j)
                    for m in range(2):
                        for c in range(NCH):
                            silu(g, m, c)
                        for j in ((3,), (4, 5))[m]:
                            w_hi(g, j)
                        for c in range(NCH):
                            u_hi(g, m, c)

            @block.vector
            def _(dve):
                def w_lo(g, j):
                    dve.wait_ge(w_high, g * 6 + j + 1)
                    dve.tensor_tensor(wl[:, j % 3, :], raw[:, j % 3, :], wh[:, j % 3, :].bitcast(F32),
                                      ALU.subtract).then_inc(w_split, 1)

                def u_mul(g, m, c):
                    n = m * NCH + c
                    dve.wait_ge(up3_ready, g * 6 + n + 1)
                    dve.wait_ge(gated, g * 6 + n + 1)
                    dve.wait_ge(u_split, g * 6 + m * (c + 1))
                    dve.tensor_tensor(u[:, c, :], gate[:, c, :], G.ps[:, 3 + c, 0:CH], ALU.mult).then_inc(u_made, 1)

                def u_lo(g, m, c):
                    dve.wait_ge(u_high, g * 6 + m * NCH + c + 1)
                    dve.tensor_tensor(chunks(ul[:, m, :])[:, c, :], u[:, c, :], chunks(uh[:, m, :])[:, c, :].bitcast(F32),
                                      ALU.subtract).then_inc(u_split, 1)

                def round_(g, last):
                    for j in (1, 2):
                        w_lo(g, j)
                    for m in range(2):
                        for j in ((3,), (4, 5))[m]:
                            w_lo(g, j)
                        for c in range(NCH):
                            u_mul(g, m, c)
                            if c > 0:
                                u_lo(g, m, c - 1)
                        u_lo(g, m, NCH - 1)
                    for o in range(KD):
                        dve.wait_ge(down_ready, g * KD + o + 1)
                        acc = chunks(f[:, o, :])
                        s = 3 * (o % 2)
                        dve.tensor_tensor(acc, G.ps[:, s:s + NCH, 0:CH], acc, ALU.add).then_inc(down_added[o % 2], 1)
                        if o == KD - 3 and not last:
                            w_lo(g + 1, 0)

                dve.wait_ge(f_cleared, 1)
                w_lo(0, 0)
                with dve.Fori(0, rounds - 1) as g:
                    round_(g, False)
                round_(rounds - 1, True)

            @block.tensor
            def _(pe):
                def up(g, j):
                    s = 3 * (j % 2)
                    pe.wait_ge(w_split, g * 6 + j + 1)
                    if j < 2:
                        pe.wait_ge(down_added[j], g * (KD // 2))
                    for c in range(NCH):
                        if j == 2:
                            pe.wait_ge(gated, g * 6 + c + 1)
                        if j == 3:
                            pe.wait_ge(u_made, g * 6 + c + 1)
                        for k in range(KD):
                            for n, (a, b) in enumerate(PAIRS):
                                last = pe.matmul(G.ps[:, s + c, 0:CH], w[a][:, j % 3, k * P:(k + 1) * P],
                                                 h[b][:, k, c * CH:(c + 1) * CH],
                                                 start=(k == 0 and n == 0), stop=(k == KD - 1 and n == 2))
                        last.then_inc((up1_ready, up3_ready)[j % 2], 1)

                def down(g, o):
                    s = 3 * (o % 2)
                    if o >= 2:
                        pe.wait_ge(down_added[o % 2], g * (KD // 2) + o // 2)
                    for m in range(2):
                        if o == 0:
                            pe.wait_ge(w_split, g * 6 + 5 + m)
                        for c in range(NCH):
                            if o == 0:
                                pe.wait_ge(u_split, g * 6 + m * NCH + c + 1)
                                if m == 0:
                                    pe.wait_ge(gated, g * 6 + NCH + c + 1)
                            if o == 1 and m == 0:
                                pe.wait_ge(u_made, g * 6 + NCH + c + 1)
                            for n, (a, b) in enumerate(PAIRS):
                                last = pe.matmul(G.ps[:, s + c, 0:CH], w[a][:, (4 + m) % 3, o * P:(o + 1) * P],
                                                 uu[b][:, m, c * CH:(c + 1) * CH],
                                                 start=(m == 0 and n == 0), stop=(m == 1 and n == 2))
                    last.then_inc(down_ready, 1)

                with pe.Fori(0, rounds) as g:
                    for j in range(4):
                        up(g, j)
                    for o in range(KD):
                        down(g, o)
        norm_add(nc, G, f"{stage}p", g_post, f, 0.5, [t[:] for t in tmp], not first)


NSA_H, KVH, GRP, HD, DIFF_H = 8, 2, 4, 64, 4
Z_NQ, Z_NKV, Z_DQ, Z_DK, Z_DV, Z_MG, Z_NG = 0, 4, 10, 14, 18, 22, 38
N_GATE = 3 * NSA_H
NG_COL = 10 * P


def project(nc, G):
    with ExitStack() as ctx:
        def sb(name, shape, dt):
            return ctx.enter_context(nc.sbuf_tensor(f"pj_{name}", shape, dt))
        hh, hl = sb("hh", [P, KD, NT], F32R), sb("hl", [P, KD, NT], F32R)
        with nc.sbuf_tensor("pj_tmp", [P, 4, NT], F32) as tmp:
            norm_split(nc, G, "pjn", G.gains["g_mix_pre"], hh, hl, [tmp[:, i, :] for i in range(4)], True)
        raw = sb("raw", [P, 2, D], F32)
        wh, wl = sb("wh", [P, 2, D], F32R), sb("wl", [P, 2, D], F32R)
        z = sb("z", [P, 2, NT], F32)
        sem = sem_maker(nc, ctx, "pj")
        raw_in, w_high, w_split, z_ready, z_copied, z_out = (
            [sem(f"{what}{j}") for j in range(2)] for what in ("raw_in", "w_high", "w_split", "z_ready", "z_copied", "z_out"))
        x_stored, w1_cleared, w1_in = sem("x_stored"), sem("w1_cleared"), sem("w1_in")
        w, h = (wh, wl), (hh, hl)
        block = ctx.enter_context(nc.Block())
        before = NG_COL // P // 2
        rounds = Z_NG // 2

        @block.sync
        def _(sp):
            for k in range(KD):
                sp.dma_start(G.x_kept[k], G.xT[:, k, :]).then_inc(x_stored, 16)

            def load_w1():
                sp.wait_ge(w1_cleared, 2)
                for kind in range(2):
                    for half in range(2):
                        part = slice(half * HD, (half + 1) * HD)
                        sp.dma_start(G.w1[part, kind, :, part], G.cmp_w1[kind]).then_inc(w1_in, 16)

            def load(g, j, skipped, cols):
                sp.wait_ge(w_split[j], g)
                sp.dma_start(raw[:, j, 0:KD * cols].rearrange("p (k n) -> p k n", k=KD),
                             G.w_in[:, bass.ds(g * (2 * P) + (j * P + skipped), cols)].rearrange("(k p) n -> p k n", p=P)
                             ).then_inc(raw_in[j], 16)

            for first, end, skipped in ((0, before, 0), (before, rounds, N_GATE)):
                with sp.Fori(first, end) as g:
                    for j in range(2):
                        load(g, j, skipped, P)
                if first == 0:
                    load_w1()
            sp.wait_ge(w_split[0], rounds)
            sp.dma_start(raw[:, 0, 0:KD * N_GATE].rearrange("p (k n) -> p k n", k=KD),
                         G.w_in[:, NG_COL:NG_COL + N_GATE].rearrange("(k p) n -> p k n", p=P)).then_inc(raw_in[0], 16)
            sp.wait_ge(x_stored, 16 * KD)
            sp.wait_ge(w1_in, 16 * 4)

        @block.gpsimd
        def _(pool):
            for half in range(2):
                pool.memset(G.w1[half * HD:(half + 1) * HD, :, :, (1 - half) * HD:(2 - half) * HD], 0.0).then_inc(w1_cleared, 1)
            with pool.Fori(0, rounds) as g:
                for j in range(2):
                    pool.wait_ge(z_copied[j], g + 1)
                    pool.dma_start(G.z[bass.ds(g * 2 + j, 1), :, :].rearrange("a p n -> (a p) n"), z[:, j, :]).then_inc(z_out[j], 16)
            pool.wait_ge(z_copied[0], rounds + 1)
            pool.dma_start(G.z[Z_NG, 0:N_GATE, :], z[0:N_GATE, 0, :]).then_inc(z_out[0], 16)
            pool.wait_ge(z_out[0], 16 * (rounds + 1))
            pool.wait_ge(z_out[1], 16 * rounds)

        @block.scalar
        def _(act):
            def hi(g, j):
                act.wait_ge(raw_in[j], (g + 1) * 16)
                act.wait_ge(z_ready[j], g)
                act.activation(wh[:, j, :], raw[:, j, :], ACT.Copy).then_inc(w_high[j], 1)

            def send(g, j, rows):
                act.wait_ge(z_ready[j], g + 1)
                act.wait_ge(z_out[j], g * 16)
                act.activation(chunks(z[0:rows, j, :]), G.ps[0:rows, 3 * j:3 * j + NCH, 0:CH], ACT.Copy).then_inc(z_copied[j], 1)

            hi(0, 0)
            hi(0, 1)
            with act.Fori(0, rounds - 1) as g:
                for j in range(2):
                    send(g, j, P)
                    hi(g + 1, j)
            send(rounds - 1, 0, P)
            hi(rounds, 0)
            send(rounds - 1, 1, P)
            send(rounds, 0, N_GATE)

        @block.vector
        def _(dve):
            def lo(g, j):
                dve.wait_ge(w_high[j], g + 1)
                dve.tensor_tensor(wl[:, j, :], raw[:, j, :], wh[:, j, :].bitcast(F32), ALU.subtract).then_inc(w_split[j], 1)

            with dve.Fori(0, rounds) as g:
                lo(g, 0)
                lo(g, 1)
            lo(rounds, 0)

        @block.tensor
        def _(pe):
            def tile(g, j, cols):
                pe.wait_ge(w_split[j], g + 1)
                pe.wait_ge(z_copied[j], g)
                for c in range(NCH):
                    for k in range(KD):
                        for n, (a, b) in enumerate(PAIRS):
                            last = pe.matmul(G.ps[0:cols, 3 * j + c, 0:CH], w[a][:, j, k * cols:(k + 1) * cols],
                                             h[b][:, k, c * CH:(c + 1) * CH],
                                             start=(k == 0 and n == 0), stop=(k == KD - 1 and n == 2))
                last.then_inc(z_ready[j], 1)

            with pe.Fori(0, rounds) as g:
                tile(g, 0, P)
                tile(g, 1, P)
            tile(rounds, 0, N_GATE)


TOK = 14
WIN = 512


def token_rows(nc, G):
    tiles = SEQ // P + 1
    with ExitStack() as ctx:
        feat = ctx.enter_context(nc.sbuf_tensor("tr_feat", [P, TOK, SEQ + NS], F32))
        rows = ctx.enter_context(nc.sbuf_tensor("tr_rows", [P, 3, TOK * P], F32))
        sem = sem_maker(nc, ctx, "tr")
        feat_in, window_moved, transposed = sem("feat_in"), sem("window_moved"), sem("transposed")
        copied = [sem("copied_act"), sem("copied_dve")]
        rows_out = [sem(f"rows_out{i}") for i in range(3)]
        block = ctx.enter_context(nc.Block())
        groups = (TOK + 3) // 4

        def size(i):
            return P if i < tiles - 1 else NS

        def in_group(q):
            return min(4, TOK - 4 * q)

        @block.gpsimd
        def _(pool):
            pool.dma_start(G.win_s[:, 0:WIN - TS, :], G.win[:, TS:WIN, :]).then_inc(window_moved, 16)
            pool.wait_ge(window_moved, 16)

        @block.sync
        def _(sp):
            sp.dma_start(feat[:, 0:6, :], G.z[Z_NKV:Z_NKV + 6, :, 0:SEQ + NS].rearrange("m p n -> p m n")).then_inc(feat_in, 16)
            sp.dma_start(feat[:, 6:TOK, :], G.z[Z_DK:Z_DK + 8, :, 0:SEQ + NS].rearrange("m p n -> p m n")).then_inc(feat_in, 16)
            stores = [0, 0, 0]
            for i in range(tiles):
                for a in range(2):
                    sp.wait_ge(copied[a], (i + 1) * (groups // 2))
                r = rows[0:size(i), i % 3, :]
                if i < tiles - 1:
                    t = slice(i * P, (i + 1) * P)
                    outs = [(G.nsa_p[t, :], r[:, 0:512]), (G.diff_p[t, :], r[:, 768:1792])]
                    if i >= tiles - 1 - WIN // P:
                        o = i * P - (SEQ - WIN)
                        outs.append((G.win_p[o:o + P, :], r[:, 512:768]))
                else:
                    outs = [(G.nsa_s, r[:, 0:512]), (G.diff_s, r[:, 768:1792])]
                    outs += [(G.win_s[b, WIN - TS:WIN, :], rows[b * TS:(b + 1) * TS, i % 3, 512:768]) for b in range(NB)]
                for dst, src in outs + [(G.kvw[i * P:i * P + size(i), :], r[:, 512:768])]:
                    sp.dma_start(dst, src).then_inc(rows_out[i % 3], 16)
                    stores[i % 3] += 1
                G.tr_stores[i] = stores[i % 3]
            for i in range(3):
                sp.wait_ge(rows_out[i], 16 * stores[i])

        @block.tensor
        def _(pe):
            pe.wait_ge(feat_in, 32)
            n = 0
            for i in range(tiles):
                for q in range(groups):
                    if n >= 2:
                        pe.wait_ge(copied[n % 2], n // 2)
                    for j in range(in_group(q)):
                        last = pe.transpose(G.ps[0:size(i), n % 2, j * P:(j + 1) * P], feat[:, 4 * q + j, i * P:i * P + size(i)],
                                            G.ident[:])
                    last.then_inc(transposed, 1)
                    n += 1

        def copy_groups(eng, parity, copy):
            stores = {}
            for i in range(tiles):
                for q in range(parity, groups, 2):
                    n = i * groups + q
                    eng.wait_ge(transposed, n + 1)
                    if i >= 3 and q == parity:
                        eng.wait_ge(rows_out[i % 3], 16 * G.tr_stores[i - 3])
                    w = in_group(q) * P
                    copy(rows[0:size(i), i % 3, 4 * q * P:4 * q * P + w], G.ps[0:size(i), n % 2, 0:w]).then_inc(copied[parity], 1)

        @block.scalar
        def _(act):
            copy_groups(act, 0, lambda dst, src: act.activation(dst, src, ACT.Copy))

        @block.vector
        def _(dve):
            copy_groups(dve, 1, lambda dst, src: dve.tensor_copy(dst, src))


TILES = SEQ // P
VD = 2 * HD
LAM_INIT = 0.2


def lambda_scale(nc, G):
    with ExitStack() as ctx:
        sem = sem_maker(nc, ctx, "lam")
        l = ctx.enter_context(nc.sbuf_tensor("lam_l", [P, 2, 2, HD], F32))
        dots = ctx.enter_context(nc.sbuf_tensor("lam_dots", [P, 2], F32))
        l_in, stepped, exped = sem("l_in"), sem("stepped"), sem("exped")
        block = ctx.enter_context(nc.Block())

        @block.sync
        def _(sp):
            sp.dma_start(l[:].rearrange("p a b d -> p (a b d)"), G.lambda_qk.rearrange("(o a) d -> o (a d)", o=1).to_broadcast([P, 4 * HD])).then_inc(l_in, 16)

        @block.vector
        def _(dve):
            dve.wait_ge(l_in, 16)
            dve.tensor_tensor(l[:, :, 0, :], l[:, :, 0, :], l[:, :, 1, :], ALU.mult).then_inc(stepped, 1)
            dve.wait_ge(stepped, 1)
            dve.tensor_reduce(dots[:], l[:, :, 0, :], AX, ALU.add).then_inc(stepped, 1)
            dve.wait_ge(exped, 1)
            dve.tensor_tensor(G.nlam[:], dots[:, 1:2], dots[:, 0:1], ALU.subtract).then_inc(stepped, 1)
            dve.wait_ge(stepped, 3)
            dve.tensor_scalar(G.nlam[:], G.nlam[:], -LAM_INIT, None, ALU.add).then_inc(stepped, 1)

        @block.scalar
        def _(act):
            act.wait_ge(stepped, 2)
            act.activation(dots[:], dots[:], ACT.Exp).then_inc(exped, 1)


def prompt_diff(nc, G):
    with ExitStack() as ctx:
        def sb(name, shape, dt=F32):
            return ctx.enter_context(nc.sbuf_tensor(f"pd_{name}", shape, dt))
        q, k, v = sb("q", [P, 2, 2, SEQ]), sb("k", [P, 2, SEQ]), sb("v", [P, 2, TILES, VD])
        bias = sb("bias", [P, 2, SEQ])
        probs = sb("probs", [P, 4, 2, SEQ])
        carrier = sb("carrier", [P, 2 * 2 * TILES])
        aT = sb("aT", [P, 2, SEQ])
        nmax, total, inv = sb("nmax", [P, 4, 2]), sb("total", [P, 4, 2]), sb("inv", [P, 4, 2])
        sem = sem_maker(nc, ctx, "pd")
        head_in = [sem(f"head_in{j}") for j in range(2)]
        q_scaled = sem("q_scaled")
        s_ready, biased, exped = ([sem(f"{what}{c}") for c in range(2)] for what in ("s_ready", "biased", "exped"))
        q_cleared, bias_made = sem("q_cleared"), sem("bias_made")
        inverted, weighed, scaled, combined = sem("inverted"), sem("weighed"), sem("scaled"), sem("combined")
        t_ready, t_copied, pv_done, o_copied = sem("t_ready"), sem("t_copied"), sem("pv_done"), sem("o_copied")
        block = ctx.enter_context(nc.Block())
        U = 2 * TILES
        rounds = DIFF_H // 2

        @block.gpsimd
        def _(pool):
            pool.memset(q[HD:P, :, 0, :], 0.0).then_inc(q_cleared, 1)
            pool.memset(q[0:HD, :, 1, :], 0.0).then_inc(q_cleared, 1)

        @block.sync
        def _(sp):
            for h in range(DIFF_H):
                if h >= 2:
                    sp.wait_ge(pv_done, (h - 1) * TILES)
                j = h % 2
                sp.dma_start(q[0:HD, j, 0, :], G.z[Z_DQ + h, 0:HD, 0:SEQ]).then_inc(head_in[j], 16)
                sp.dma_start(q[HD:P, j, 1, :], G.z[Z_DQ + h, HD:P, 0:SEQ]).then_inc(head_in[j], 16)
                sp.dma_start(k[:, j, :], G.z[Z_DK + h, :, 0:SEQ]).then_inc(head_in[j], 16)
                sp.dma_start(v[:, j, :, :], G.diff_p[:, 512 + h * VD:512 + (h + 1) * VD].rearrange("(i p) d -> p i d", p=P)).then_inc(head_in[j], 16)

        @block.tensor
        def _(pe):
            def scores(g, u, c):
                i, j = u % TILES, u // TILES
                n = (i + 1) * P
                if i == 0 and c == 0:
                    pe.wait_ge(q_scaled, g * 2 + j + 1)
                pe.wait_ge(biased[c], g * U + u)
                for n0 in range(0, n, 512):
                    m = min(512, n - n0)
                    last = pe.matmul(G.ps[:, 2 * c + n0 // 512, 0:m], q[:, j, c, i * P:(i + 1) * P], k[:, j, n0:n0 + m],
                                     start=True, stop=True)
                last.then_inc(s_ready[c], 1)

            def turn(g, u):
                pe.wait_ge(combined, g * U + u + 1)
                pe.wait_ge(t_copied, g * U + u)
                for t in range(u % TILES + 1):
                    last = pe.transpose(G.ps[:, 4 + t // 4, (t % 4) * P:(t % 4 + 1) * P], probs[:, u % 4, 0, t * P:(t + 1) * P], G.ident[:])
                last.then_inc(t_ready, 1)

            def values(g, u):
                i, j = u % TILES, u // TILES
                pe.wait_ge(t_copied, g * U + u + 1)
                pe.wait_ge(o_copied, g * U + max(u - 1, 0))
                for t in range(i + 1):
                    last = pe.matmul(G.ps[:, 6 + u % 2, 0:VD], aT[:, u % 2, t * P:(t + 1) * P], v[:, j, t, :], start=(t == 0), stop=(t == i))
                last.then_inc(pv_done, 1)

            with pe.Fori(0, rounds) as g:
                for u in range(U + 2):
                    if u < U:
                        scores(g, u, 0)
                    if u >= 2:
                        turn(g, u - 2)
                    if u < U:
                        scores(g, u, 1)
                    if u >= 2:
                        values(g, u - 2)

        @block.vector
        def _(dve):
            def negated_scores(g, u, c):
                i, j = u % TILES, u // TILES
                n = (i + 1) * P
                if i == 0 and c == 0:
                    dve.wait_ge(bias_made, g * 2 + j + 1)
                    dve.wait_ge(head_in[j], g * 64 + 64)
                    dve.wait_ge(q_cleared, 2)
                    dve.tensor_scalar(q[:, j, :, :], q[:, j, :, :], -HD ** -0.5, None, ALU.mult).then_inc(q_scaled, 1)
                dve.wait_ge(s_ready[c], g * U + u + 1)
                if c == 0:
                    dve.wait_ge(t_ready, g * U + max(u - 3, 0))
                    dve.wait_ge(combined, g * U + max(u - 3, 0))
                dve.memset(carrier[:, 2 * u + c:2 * u + c + 1], 0.0)
                dve.tensor_tensor_reduce(out=probs[:, u % 4, c, 0:n], in0=G.ps[:, 2 * c:2 * c + 2, :].rearrange("p a n -> p (a n)")[:, 0:n],
                                         in1=bias[:, j, SEQ - n:SEQ], scale=1.0, scalar=3e38, op0=ALU.add, op1=ALU.min,
                                         accum_out=nmax[:, u % 4, c:c + 1]).then_inc(biased[c], 1)

            def combine(g, u):
                n = (u % TILES + 1) * P
                p0, p1 = probs[:, u % 4, 0, 0:n], probs[:, u % 4, 1, 0:n]
                for c in range(2):
                    dve.wait_ge(exped[c], g * U + u + 1)
                dve.reciprocal(inv[:, u % 4, :], total[:, u % 4, :]).then_inc(inverted, 1)
                dve.wait_ge(inverted, g * U + u + 1)
                dve.tensor_scalar(p0, p0, inv[:, u % 4, 0:1], None, ALU.mult).then_inc(scaled, 1)
                dve.tensor_tensor(inv[:, u % 4, 1:2], inv[:, u % 4, 1:2], G.nlam[:], ALU.mult).then_inc(weighed, 1)
                dve.wait_ge(scaled, g * U + u + 1)
                dve.wait_ge(weighed, g * U + u + 1)
                dve.scalar_tensor_tensor(p0, p1, inv[:, u % 4, 1:2], p0, ALU.mult, ALU.add).then_inc(combined, 1)

            with dve.Fori(0, rounds) as g:
                for u in range(U + 1):
                    if u < U:
                        negated_scores(g, u, 0)
                    if u >= 1:
                        combine(g, u - 1)
                    if u < U:
                        negated_scores(g, u, 1)

        @block.scalar
        def _(act):
            def exps(g, u):
                n = (u % TILES + 1) * P
                if u == 0:
                    act.wait_ge(biased[1], g * U)
                    for j in range(2):
                        act.activation(bias[:, j, :], G.causal[:], ACT.Copy, scale=G.slopes[:, bass.ds(g * 2 + j, 1)]).then_inc(bias_made, 1)
                for c in range(2):
                    act.wait_ge(biased[c], g * U + u + 1)
                    act.activation(probs[:, u % 4, c, 0:n], probs[:, u % 4, c, 0:n], ACT.Exp, bias=nmax[:, u % 4, c:c + 1], scale=-1.0,
                                   accum_out=total[:, u % 4, c:c + 1]).then_inc(exped[c], 1)

            def copy_t(g, u):
                n = (u % TILES + 1) * P
                act.wait_ge(t_ready, g * U + u + 1)
                act.wait_ge(pv_done, g * U + max(u - 1, 0))
                act.activation(aT[:, u % 2, 0:n], G.ps[:, 4:6, :].rearrange("p a n -> p (a n)")[:, 0:n], ACT.Copy).then_inc(t_copied, 1)

            def copy_o(g, u):
                i, j = u % TILES, u // TILES
                act.wait_ge(pv_done, g * U + u + 1)
                act.activation(G.od[:, i, bass.ds(g * (2 * VD) + j * VD, VD)], G.ps[:, 6 + u % 2, 0:VD], ACT.Copy).then_inc(o_copied, 1)

            with act.Fori(0, rounds) as g:
                for u in range(U + 3):
                    if 2 <= u < U + 2:
                        copy_t(g, u - 2)
                    if u < U:
                        exps(g, u)
                    if u >= 3:
                        copy_o(g, u - 3)


PAGE = 128
PAGES = 32
BLK = 64
NBLK = 64
N_POOL = 320


TRIO = 3
CHUNK = TRIO * PAGES // 2


def load_pages(nc, G, eng, which, g, c, s):
    share, unroll = CHUNK // 3, 8
    with eng.Fori(0, share // unroll) as p:
        _, numbers = nc.values_load_multi_w_load_instructions(
            G.pt[0:1, bass.ds(g * (TRIO * PAGES) + c * CHUNK + s * share + p * unroll, unroll)], engines=[which], min_val=0, max_val=N_POOL - 1)
        for n, page in enumerate(numbers):
            eng.dma_start(G.pages[:, c, bass.ds(p * unroll + (s * share + n), 1), :, :, :].rearrange("t a k h d -> t (a k h d)"),
                          G.cache_nsa[bass.ds(page, 1), :, 0:2 * P].rearrange("a t n -> (a t) n")).then_inc(G.page_in[c][s], 16)


def compress(nc, G):
    trio, chunk, share = TRIO, CHUNK, CHUNK // 3
    rounds = (NB + 1) // trio
    npages = trio * PAGES
    with ExitStack() as ctx:
        def sb(name, shape, dt=F32):
            return ctx.enter_context(nc.sbuf_tensor(f"cp_{name}", shape, dt))
        w1 = G.w1
        w2k, w2v, b1 = sb("w2k", [P, 2, KVH, P]), sb("w2v", [P, 2, HD]), sb("b1", [P, 2])
        pages, page_in = G.pages, G.page_in
        hid = sb("hid", [P, 2, npages, KVH])
        sem = sem_maker(nc, ctx, "cp")
        cleared, weights_in = sem("cleared"), sem("weights_in")
        hid_ready, hid_done = sem("hid_ready"), [sem(f"hid_done{kind}") for kind in range(2)]
        multiplied = [sem(f"multiplied{c}") for c in range(2)]
        c_ready, c_copied = sem("c_ready"), sem("c_copied")
        block = ctx.enter_context(nc.Block())

        def load(eng, which, g, c, s):
            eng.wait_ge(cleared, 2)
            eng.wait_ge(multiplied[c], g)
            load_pages(nc, G, eng, which, g, c, s)

        @block.gpsimd
        def _(pool):
            pool.memset(w2k[:], 0.0).then_inc(cleared, 1)
            pool.memset(w2v[:], 0.0).then_inc(cleared, 1)
            load(pool, mybir.EngineType.Pool, 0, 1, 2)
            with pool.Fori(1, rounds - 1) as g:
                for c in range(2):
                    load(pool, mybir.EngineType.Pool, g, c, 2)
            load(pool, mybir.EngineType.Pool, rounds - 1, 0, 2)
            pool.wait_ge(multiplied[1], rounds - 1)
            pool.dma_start(pages[:, 1, share:share + TILES, :, :, :].rearrange("t a k h d -> t a (k h d)"),
                           G.nsa_p[:, 0:2 * P].rearrange("(a t) n -> t a n", t=P)).then_inc(page_in[1][2], 16)

        @block.sync
        def _(sp):
            load(sp, mybir.EngineType.SP, 0, 1, 0)
            with sp.Fori(1, rounds) as g:
                for c in range(2):
                    load(sp, mybir.EngineType.SP, g, c, 0)

        @block.tensor
        def _(pe):
            def hidden(g, c, last=False):
                for s in range(3):
                    pe.wait_ge(page_in[c][s], g * (16 * share) + (16 * share, 0, 16)[s if last else 0])
                for kind in range(2):
                    pe.wait_ge(hid_done[kind], g * 2 + c)
                    for d in range(HD):
                        mm = pe.matmul(G.ps[:, kind, 0:chunk * KVH], w1[:, kind, d, :], pages[:, c, :, kind, :, d],
                                       start=(d == 0), stop=(d == HD - 1))
                        if d == HD - 1 and kind == 0:
                            mm.then_inc(hid_ready, 1)
                mm.then_inc(multiplied[c], 1)

            def project_blocks(g):
                pe.wait_ge(hid_done[0], g * 2 + 2)
                pe.wait_ge(c_copied, g)
                for half in range(2):
                    keys = G.ps[:, 2, 0:2 * npages].rearrange("d (a b) -> d a b", b=2)[:, :, half]
                    for h in range(KVH):
                        pe.matmul(keys, w2k[:, half, h, :], hid[:, 0, :, h], start=(h == 0), stop=(h == KVH - 1))
                pe.wait_ge(hid_done[1], g * 2 + 2)
                for s in range(trio):
                    for half in range(2):
                        for h in range(KVH):
                            last = pe.matmul(G.ps[half * PAGES:(half + 1) * PAGES, 3, s * P + h * HD:s * P + (h + 1) * HD],
                                             hid[:, 1, s * PAGES:(s + 1) * PAGES, h], w2v[:, half, :], start=True, stop=True)
                last.then_inc(c_ready, 1)

            pe.wait_ge(weights_in, 16 * 8)
            with pe.Fori(0, rounds - 1) as g:
                hidden(g, 0)
                hidden(g, 1)
                project_blocks(g)
            hidden(rounds - 1, 0)
            hidden(rounds - 1, 1, last=True)
            project_blocks(rounds - 1)

        @block.scalar
        def _(act):
            act.wait_ge(cleared, 2)
            for kind in range(2):
                for half in range(2):
                    part = slice(half * HD, (half + 1) * HD)
                    for h in range(KVH):
                        dst = w2k[part, half, h, h * HD:(h + 1) * HD] if kind == 0 else w2v[part, half, :]
                        if kind == 0 or h == 0:
                            act.dma_start(dst, G.cmp_w2[kind]).then_inc(weights_in, 16)
            for half in range(2):
                act.dma_start(b1[half * HD:(half + 1) * HD, :], G.cmp_b1).then_inc(weights_in, 16)

            def gelu(g, c):
                for kind in range(2):
                    ready, count = ((hid_ready, g * 2 + c + 1), (multiplied[c], g + 1))[kind]
                    act.wait_ge(weights_in, 16 * 8)
                    act.wait_ge(ready, count)
                    act.wait_ge(c_ready, g)
                    act.activation(hid[:, kind, c * chunk:(c + 1) * chunk, :], G.ps[:, kind, 0:chunk * KVH].rearrange("p (a h) -> p a h", h=KVH),
                                   ACT.Gelu_apprx_tanh, bias=b1[:, kind:kind + 1]).then_inc(hid_done[kind], 1)

            load(act, mybir.EngineType.Activation, 0, 1, 1)
            with act.Fori(0, rounds - 2) as g:
                for c in range(2):
                    gelu(g, c)
                    load(act, mybir.EngineType.Activation, g + 1, c, 1)
            gelu(rounds - 2, 0)
            load(act, mybir.EngineType.Activation, rounds - 1, 0, 1)
            gelu(rounds - 2, 1)
            for c in range(2):
                gelu(rounds - 1, c)

        @block.vector
        def _(dve):
            with dve.Fori(0, rounds) as g:
                dve.wait_ge(c_ready, g + 1)
                dve.tensor_copy(G.ckT[:, bass.ds(g * trio, trio), :], G.ps[:, 2, 0:2 * npages].rearrange("p (s b) -> p s b", s=trio))
                dve.tensor_copy(G.cv[:, bass.ds(g * trio, trio), :], G.ps[0:2 * PAGES, 3, 0:trio * P].rearrange("p (s b) -> p s b", s=trio)
                                ).then_inc(c_copied, 1)


QUAD = 4
QT = QUAD * PAGE
QUADS = PAGES // QUAD
STEPS = QUADS + 2
S_WIN, S_NEW = QUADS, QUADS + 1
KV1 = KVH * HD
RING = 4
AHEAD = 3
FOLDS = 9


def page_numbers(nc, G, which, g, q):
    _, numbers = nc.values_load_multi_w_load_instructions(
        G.pt[0:1, bass.ds(g * (2 * PAGES) + q * QUAD, QUAD)], engines=[which], min_val=0, max_val=N_POOL - 1)
    return numbers


def load_diff_quad(nc, G, sp, g, q):
    for a, page in enumerate(page_numbers(nc, G, mybir.EngineType.SP, g, q)):
        sp.dma_start(G.dpage[:, q % RING, a, :, :].rearrange("t k n -> t (k n)"),
                     G.cache_diff[bass.ds(page, 1), :, :].rearrange("o t n -> (o t) n")).then_inc(G.d_in[q % RING], 16)


def load_nsa_quad(nc, G, pool, g, q):
    for a, page in enumerate(page_numbers(nc, G, mybir.EngineType.Pool, g, q)):
        pool.dma_start(G.npage[:, q % RING, a, :, :].rearrange("t k n -> t (k n)"),
                       G.cache_nsa[bass.ds(page, 1), :, 2 * KV1:4 * KV1].rearrange("o t n -> (o t) n")).then_inc(G.n_in[q % RING], 16)


N_TOP = 16
ROWS = KVH * GRP * TS
ROW0 = SEQ


def sample_select(nc, G):
    with ExitStack() as ctx:
        def sb(name, shape, dt=F32):
            return ctx.enter_context(nc.sbuf_tensor(f"ss_{name}", shape, dt))
        q = sb("q", [P, NB, ROWS])
        s, p = sb("s", [ROWS, NB, NBLK]), sb("p", [ROWS, NB, NBLK])
        work, top = sb("work", [ROWS, NB, NBLK + 2]), sb("top", [ROWS, NB, 2, 8])
        least, total = sb("least", [ROWS, NB]), sb("total", [ROWS, NB])
        pT = sb("pT", [NBLK, NB, ROWS])
        sem = sem_maker(nc, ctx, "ss")
        q_cleared, q_in, step, scored, exped = sem("q_cleared"), sem("q_in"), sem("step"), sem("scored"), sem("exped")
        normed, summed, turned, turned_copied, valued = sem("normed"), sem("summed"), sem("turned"), sem("turned_copied"), sem("valued")
        drop_made, drop_moved = sem("drop_made"), sem("drop_moved")
        block = ctx.enter_context(nc.Block())

        @block.gpsimd
        def _(pool):
            pool.memset(q[:], 0.0).then_inc(q_cleared, 1)
            for first in range(AHEAD):
                load_nsa_quad(nc, G, pool, 0, first)

        @block.sync
        def _(sp):
            sp.wait_ge(q_cleared, 1)
            rows = G.z.rearrange("m p n -> (m p) n")
            for h in range(KVH):
                for g in range(GRP):
                    r = Z_NQ * P + (h * GRP + g) * HD
                    c = (h * GRP + g) * TS
                    sp.dma_start(q[h * HD:(h + 1) * HD, :, c:c + TS],
                                 rows[r:r + HD, ROW0:ROW0 + NS].rearrange("d (b t) -> d b t", t=TS)).then_inc(q_in, 16)
            for first in range(AHEAD):
                load_diff_quad(nc, G, sp, 0, first)

        @block.tensor
        def _(pe):
            pe.wait_ge(step, 1)
            for b in range(NB):
                last = pe.matmul(G.ps[0:ROWS, 0, b * NBLK:(b + 1) * NBLK], q[:, b, :],
                                 G.ckT[:, b, :].rearrange("d (a c) -> d c a", c=2), start=True, stop=True)
            last.then_inc(scored, 1)
            pe.wait_ge(normed, 1)
            pe.matmul(G.ps[0:ROWS, 1, :], G.group_sum[:], p[:].rearrange("r b n -> r (b n)"), start=True, stop=True).then_inc(summed, 1)
            for b in range(NB):
                last = pe.transpose(G.ps[0:NBLK, 2, b * ROWS:(b + 1) * ROWS], p[:, b, :], G.ident[0:ROWS, 0:ROWS])
            last.then_inc(turned, 1)
            pe.wait_ge(turned_copied, 1)
            for b in range(NB):
                last = pe.matmul(G.ps[0:ROWS, 3 + b // 4, (b % 4) * P:(b % 4 + 1) * P], pT[:, b, :], G.cv[:, b, :], start=True, stop=True)
            last.then_inc(valued, 1)

        @block.scalar
        def _(act):
            act.wait_ge(step, 4)
            act.activation(p[:], s[:], ACT.Exp, scale=-1.0).then_inc(exped, 1)
            act.wait_ge(turned, 1)
            act.activation(pT[:].rearrange("n b r -> n (b r)"), G.ps[0:NBLK, 2, :], ACT.Copy).then_inc(turned_copied, 1)
            act.wait_ge(valued, 1)
            for a in range(2):
                act.activation(G.o_cmp[:, 4 * a:4 * a + 4, :].rearrange("r b d -> r (b d)"), G.ps[0:ROWS, 3 + a, :], ACT.Copy)
            shift = QT // BLK // 2
            act.wait_ge(drop_made, 1)
            act.dma_start(G.drop[ROWS:P, :, 0:NBLK - shift], G.drop[0:ROWS, :, shift:NBLK]).then_inc(drop_moved, 16)
            act.wait_ge(drop_moved, 16)

        @block.vector
        def _(dve):
            n = [0]

            def then(ins):
                n[0] += 1
                ins.then_inc(step, 1)
                dve.wait_ge(step, n[0])

            dve.wait_ge(q_in, 16 * NSA_H)
            then(dve.tensor_scalar(q[:], q[:], -HD ** -0.5, None, ALU.mult))
            dve.wait_ge(scored, 1)
            then(dve.tensor_tensor(s[:], G.ps[0:ROWS, 0, :].rearrange("r (b n) -> r b n", b=NB),
                                   G.bias_cmp[:].rearrange("r (o n) -> r o n", o=1).to_broadcast([ROWS, NB, NBLK]), ALU.add))
            then(dve.tensor_reduce(least[:], s[:], AX, ALU.min))
            then(dve.tensor_tensor(s[:], s[:], least[:].rearrange("r (b o) -> r b o", o=1).to_broadcast([ROWS, NB, NBLK]), ALU.subtract))
            dve.wait_ge(exped, 1)
            then(dve.tensor_reduce(total[:], p[:], AX, ALU.add))
            then(dve.reciprocal(total[:], total[:]))
            dve.tensor_tensor(p[:], p[:], total[:].rearrange("r (b o) -> r b o", o=1).to_broadcast([ROWS, NB, NBLK]), ALU.mult).then_inc(normed, 1)
            dve.wait_ge(summed, 1)
            dve.memset(work[:, :, NBLK:NBLK + 2], -5.0)
            for half in range(2):
                last = dve.tensor_copy(work[:, :, 0:NBLK].rearrange("r b (a c) -> r b a c", c=2)[:, :, :, half],
                                       G.ps[0:ROWS, 1, :].rearrange("r (b c a) -> r b c a", b=NB, c=2)[:, :, half, :])
            then(last)
            then(dve.memset(work[:, :, 0:1], -3.0))
            for b in range(NB):
                last = dve.max(top[:, b, 0, :], work[:, b, :])
            then(last)
            for b in range(NB):
                last = dve.match_replace(out=work[:, b, :], in_to_replace=top[:, b, 0, :], in_values=work[:, b, :], imm_value=-1.0)
            then(last)
            for b in range(NB):
                last = dve.max(top[:, b, 1, :], work[:, b, :])
            then(last)
            then(dve.memset(top[:, :, 1, N_TOP - 2 - 8:8], -5.0))
            for b in range(NB):
                last = dve.match_replace(out=work[:, b, :], in_to_replace=top[:, b, 1, :], in_values=work[:, b, :], imm_value=-1.0)
            then(last)
            then(dve.tensor_scalar(G.drop[0:ROWS, :, :], work[:, :, 0:NBLK], -1.0, 1e30, ALU.not_equal, ALU.mult))
            dve.memset(G.drop[0:ROWS, :, 0:1], 0.0).then_inc(drop_made, 1)


def sample_attend(nc, G):
    rounds = NB // 2
    N = 2 * STEPS
    PAGE_STEPS = [n for n in range(N) if n % STEPS not in (S_WIN, S_NEW)]
    D_STEPS = [n for n in range(N) if n % STEPS != S_WIN]
    ND, NN = QUADS + 1, QUADS + 2
    NSUM = NN + 1
    NSTAT = NN + 1
    N_SEL = QUADS + 1

    def seq(n):
        return n // STEPS

    def is_page(n):
        return n in PAGE_STEPS

    def quad(n):
        return PAGE_STEPS.index(n)

    def wait(eng, sem, value):
        if not isinstance(value, int) or value > 0:
            eng.wait_ge(sem, value)

    def at(g, n, lag):
        if n >= lag:
            return (g, n - lag) if n - lag < N else None
        return None if isinstance(g, int) and g == 0 else (g - 1, n - lag + N)

    def ended(g, n, lag):
        if n - lag in (STEPS, N):
            return [(g, (n - lag) // STEPS - 1)]
        return [(g - 1, 1)] if n == lag and not isinstance(g, int) else []

    def all_beats(eng, beat):
        for n in range(N):
            beat(0, n)
        with eng.Fori(1, rounds) as g:
            for n in range(N):
                beat(g, n)
        for n in range(N, N + 5):
            beat(rounds - 1, n)

    def before(steps, n):
        return sum(1 for m in steps if m < n)

    def key_tiles(n):
        return tuple(range(5)) if is_page(n) else (4,) if n % STEPS == S_WIN else ()

    def turned_before(n, t):
        order = [(m, u) for m in range(N) for u in key_tiles(m)]
        seen = [x for x in order if x < (n, t)]
        return len(seen), sum(1 for x in seen if x[1] % 2 == 0), sum(1 for x in seen if x[1] % 2)

    ALL_T, EVEN_T, ODD_T = turned_before(N, 0)
    KEY_BANKS = (0, 1, 7)

    HT = QT // 2
    with ExitStack() as ctx:
        def sb(name, shape, dt=F32):
            return ctx.enter_context(nc.sbuf_tensor(f"sa_{name}", shape, dt))
        window = sb("window", [P, 2, QUAD, 2, KV1])
        qd, qn = sb("qd", [P, 2, DIFF_H, 32]), sb("qn", [P, 2, ROWS])
        new_k = sb("new_k", [P, 2, 6, TS])
        new_v = sb("new_v", [P, 2, DIFF_H * VD + 2 * KV1])
        kT = sb("kT", [P, 2, 5, QT])
        pd, pn = sb("pd", [P, 2, QT]), sb("pn", [P, 2, HT])
        pdT, pnT = sb("pdT", [P, 2, QT]), sb("pnT", [P, 2, 2 * P])
        masked = sb("masked", [P, 2, HT])
        od, on = sb("od", [P, 2, ND, VD]), sb("on", [P, 2, NSUM, KV1])
        min_d, tot_d = sb("min_d", [P, 2, ND]), sb("tot_d", [P, 2, ND])
        stat_n = sb("stat_n", [P, 2, 2, NN])
        both_n = sb("both_n", [P, 2, NSTAT, 2])
        w_d, w_n, own_n = sb("w_d", [P, ND]), sb("w_n", [P, NSTAT, 2]), sb("own_n", [P, NSUM])
        wt_d = sb("wt_d", [P, ND])
        base_d, base_n = sb("base_d", [P, 1]), sb("base_n", [P, 2])
        join_d, join_n = sb("join_d", [P, ND, 32]), sb("join_n", [P, NSUM, ROWS])
        carrier = sb("carrier", [P, 3 * N])
        sem = sem_maker(nc, ctx, "sa")
        cleared, scaled, small_in = sem("cleared"), sem("scaled"), [sem(f"small_in{j}") for j in range(2)]
        dpage, npage, d_in, n_in = G.dpage, G.npage, G.d_in, G.n_in
        k_turned, k_even, k_odd = sem("k_turned"), sem("k_even"), sem("k_odd")
        sd_ready, sn_ready, soft_d, soft_n, exp_d, exp_n = (sem(x) for x in ("sd_ready", "sn_ready", "soft_d", "soft_n", "exp_d", "exp_n"))
        mask_made, p_turned, p_copied, o_copied = sem("mask_made"), sem("p_turned"), sem("p_copied"), sem("o_copied")
        used = [sem(f"used{r}") for r in range(RING)]
        tail = [sem(f"tail{j}") for j in range(2)]
        weighed, folded, join_ready, join_copied = (sem(x) for x in ("weighed", "folded", "join_ready", "join_copied"))
        joined = [sem(f"joined{j}") for j in range(2)]
        swapped, swap_read = sem("swapped"), sem("swap_read")
        block = ctx.enter_context(nc.Block())
        z_rows = G.z.rearrange("m p n -> (m p) n")

        SMALL = 16 * 10

        @block.sync
        def _(sp):
            def small(g, j):
                sp.wait_ge(cleared, 4)
                wait(sp, tail[j], g * 2)
                col = bass.ds(g * (2 * TS) + (ROW0 + j * TS), TS)
                row = bass.ds(g * (2 * TS) + j * TS, TS)
                loads = []
                for c in range(2):
                    part = slice(c * HD, (c + 1) * HD)
                    loads.append((qd[part, j, :, c * TS:(c + 1) * TS], G.z[Z_DQ:Z_DQ + DIFF_H, part, col].rearrange("h d t -> d h t")))
                for h in range(KVH):
                    r = (Z_NQ * P) + h * GRP * HD
                    loads.append((qn[h * HD:(h + 1) * HD, j, h * GRP * TS:(h + 1) * GRP * TS].rearrange("d (g t) -> d g t", g=GRP),
                                  z_rows[r:r + GRP * HD, col].rearrange("(g d) t -> d g t", g=GRP)))
                loads.append((new_k[:, j, 0:4, :], G.z[Z_DK:Z_DK + 4, :, col].rearrange("h d t -> d h t")))
                loads.append((new_k[:, j, 4:6, :], G.z[Z_NKV + 2:Z_NKV + 5:2, :, col].rearrange("h d t -> d h t")))
                loads.append((new_v[0:TS, j, 0:512], G.diff_s[row, 512:1024]))
                loads.append((new_v[0:TS, j, 512:640], G.nsa_s[row, 384:512]))
                loads.append((new_v[0:TS, j, 640:768], G.kvw[bass.ds(g * (2 * TS) + (SEQ + j * TS), TS), 128:256]))
                loads.append((window[:, j, :, :, :].rearrange("p a k d -> p a (k d)"),
                              G.win[bass.ds(g * 2 + j, 1), :, :].rearrange("o (a p) n -> p (o a) n", p=P)))
                for dst, src in loads:
                    sp.dma_start(dst, src).then_inc(small_in[j], 16)

            def round_(g, first=0):
                for q in range(first, 2 * QUADS):
                    r = q % RING
                    if not isinstance(g, int):
                        sp.wait_ge(cleared, 4)
                    wait(sp, used[r], g * (2 * QUADS // RING) + q // RING)
                    load_diff_quad(nc, G, sp, g, q)
                    if q in (0, 4) and not first:
                        small(g, q // 4)

            small(0, 0)
            small(0, 1)
            round_(0, AHEAD)
            with sp.Fori(1, rounds) as g:
                round_(g)

        @block.gpsimd
        def _(pool):
            def load(g, q):
                r = q % RING
                if not isinstance(g, int):
                    pool.wait_ge(cleared, 4)
                wait(pool, used[r], g * (2 * QUADS // RING) + q // RING)
                load_nsa_quad(nc, G, pool, g, q)

            for x in (qd, qn):
                pool.memset(x[:], 0.0).then_inc(cleared, 1)
            pool.memset(new_v[:], 0.0).then_inc(cleared, 1)
            pool.wait_ge(cleared, 3)
            pool.memset(on[ROWS:P, :, NN, :], 0.0).then_inc(cleared, 1)

            def mask(g, q):
                n = PAGE_STEPS[q]
                m = PAGE_STEPS[q - 2] if q >= 2 else None
                pool.wait_ge(cleared, 4)
                wait(pool, soft_n, g * N + (m + 1 if q >= 2 else 0))
                first = (q % QUADS) * (QT // BLK)
                blocks = G.drop[:, bass.ds(g * 2 + seq(n), 1), first:first + HT // BLK]
                pool.tensor_tensor(masked[:, q % 2, :].rearrange("r (a b) -> r a b", b=BLK),
                                   G.bias_n[:].rearrange("r (a b) -> r a b", b=BLK),
                                   blocks.rearrange("r o (a b) -> r (o a) b", b=1).to_broadcast([P, HT // BLK, BLK]), ALU.add).then_inc(mask_made, 1)

            def round_(g, last):
                for q in range(2 * QUADS):
                    mask(g, q)
                    if q + AHEAD < 2 * QUADS:
                        load(g, q + AHEAD)
                    elif not last:
                        load(g + 1, q + AHEAD - 2 * QUADS)

            round_(0, False)
            with pool.Fori(1, rounds - 1) as g:
                round_(g, False)
            round_(rounds - 1, True)

        @block.tensor
        def _(pe):
            def turn_keys(g, n):
                if is_page(n):
                    r = quad(n) % RING
                    arrived = g * (16 * QUAD * (2 * QUADS // RING)) + 16 * QUAD * (quad(n) // RING + 1)
                    pe.wait_ge(d_in[r], arrived)
                    pe.wait_ge(n_in[r], arrived)
                elif key_tiles(n):
                    pe.wait_ge(small_in[seq(n)], g * SMALL + SMALL)
                for t in key_tiles(n):
                    m, _, _ = turned_before(n, t)
                    if m >= len(KEY_BANKS):
                        a, b = [(x, u) for x in range(N) for u in key_tiles(x)][m - len(KEY_BANKS)]
                        _, even, odd = turned_before(a, b)
                        if b % 2 == 0:
                            pe.wait_ge(k_even, g * EVEN_T + even + 1)
                        else:
                            pe.wait_ge(k_odd, g * ODD_T + odd + 1)
                    else:
                        wait(pe, k_even, g * EVEN_T)
                        wait(pe, k_odd, g * ODD_T)
                    for a in range(QUAD):
                        if not is_page(n):
                            keys = window[:, seq(n), a, 0, :]
                        elif t < 4:
                            keys = dpage[:, quad(n) % RING, a, 0, t * P:(t + 1) * P]
                        else:
                            keys = npage[:, quad(n) % RING, a, 0, :]
                        last = pe.transpose(G.ps[:, KEY_BANKS[m % len(KEY_BANKS)], a * PAGE:(a + 1) * PAGE], keys, G.ident[:])
                    last.then_inc(k_turned, 1)

            def scores(g, n):
                j = seq(n)
                if n % STEPS == 0:
                    pe.wait_ge(scaled, g * 4 + 2 * j + 2)
                _, even, odd = turned_before(n + 1, 0)
                if key_tiles(n):
                    pe.wait_ge(k_even, g * EVEN_T + even)
                    pe.wait_ge(k_odd, g * ODD_T + odd)
                new = n % STEPS == S_NEW
                width = TS if new else QT
                if n in D_STEPS:
                    wait(pe, soft_d, g * len(D_STEPS) + before(D_STEPS, n))
                    for h in range(DIFF_H):
                        keys = new_k[:, j, h, :] if new else kT[:, n % 2, h, :]
                        last = pe.matmul(G.ps[32 * h:32 * h + 32, 2, 0:width], qd[:, j, h, :], keys, start=True, stop=True)
                    last.then_inc(sd_ready, 1)
                wait(pe, soft_n, g * N + n)
                for half in range(2):
                    for h in range(KVH):
                        keys = new_k[:, j, 4 + half, :] if new else kT[:, n % 2, 4, half * HT:(half + 1) * HT]
                        row = ROWS * half + 32 * h
                        last = pe.matmul(G.ps[row:row + 32, 3, 0:TS if new else HT], qn[:, j, 32 * h:32 * h + 32], keys,
                                         start=True, stop=True)
                last.then_inc(sn_ready, 1)

            def turn_probs(g, n):
                new = n % STEPS == S_NEW
                wait(pe, p_copied, g * N + n)
                if n in D_STEPS:
                    pe.wait_ge(exp_d, g * len(D_STEPS) + before(D_STEPS, n) + 1)
                pe.wait_ge(exp_n, g * N + (n + 1))
                if new:
                    pe.transpose(G.ps[0:TS, 4, 0:P], pd[:, n % 2, 0:TS], G.ident[:])
                    last = pe.transpose(G.ps[0:TS, 5, 0:P], pn[:, n % 2, 0:TS], G.ident[:])
                else:
                    for a in range(QUAD):
                        if n in D_STEPS:
                            pe.transpose(G.ps[:, 4, a * P:(a + 1) * P], pd[:, n % 2, a * PAGE:(a + 1) * PAGE], G.ident[:])
                    for a in range(2):
                        last = pe.transpose(G.ps[:, 5, a * P:(a + 1) * P], pn[:, n % 2, a * PAGE:(a + 1) * PAGE], G.ident[:])
                last.then_inc(p_turned, 1)

            def values(g, n):
                j, new = seq(n), n % STEPS == S_NEW
                pe.wait_ge(p_copied, g * N + n + 1)
                wait(pe, o_copied, g * N + n)
                wait(pe, join_copied, g * 2 + (1 if n > STEPS + 2 else 0) - (1 if n <= 2 else 0))
                if new:
                    for h in range(DIFF_H):
                        pe.matmul(G.ps[32 * h:32 * h + 32, 6, 0:VD], pdT[:, n % 2, 32 * h:32 * h + 32],
                                  new_v[:, j, h * VD:(h + 1) * VD], start=True, stop=True)
                    for part in range(2):
                        last = pe.matmul(G.ps[part * ROWS:(part + 1) * ROWS, 6, VD:VD + KV1], pnT[:, n % 2, part * ROWS:(part + 1) * ROWS],
                                         new_v[:, j, 512 + part * P:512 + (part + 1) * P], start=True, stop=True)
                    last.then_inc(tail[j], 1)
                    return
                if n in D_STEPS:
                    for a in range(QUAD):
                        for h in range(DIFF_H):
                            pe.matmul(G.ps[32 * h:32 * h + 32, 6, 0:VD], pdT[:, n % 2, a * P + 32 * h:a * P + 32 * h + 32],
                                      dpage[:, quad(n) % RING, a, 1, h * VD:(h + 1) * VD], start=(a == 0), stop=(a == QUAD - 1))
                for a in range(2):
                    for half in range(2):
                        page = 2 * half + a
                        v = npage[:, quad(n) % RING, page, 1, :] if is_page(n) else window[:, j, page, 1, :]
                        rows = slice(half * ROWS, (half + 1) * ROWS)
                        last = pe.matmul(G.ps[rows, 6, VD:VD + KV1], pnT[:, n % 2, a * P + half * ROWS:a * P + (half + 1) * ROWS], v,
                                         start=(a == 0), stop=(a == 1))
                last.then_inc(used[quad(n) % RING] if is_page(n) else tail[j], 1)

            def swap(g, j):
                wait(pe, p_copied, g * N + (j + 1) * STEPS)
                pe.wait_ge(exp_n, g * N + (j + 1) * STEPS)
                pe.matmul(G.ps[:, 5, 0:2 * NN], G.swap_n[:], stat_n[:, j, :, :].rearrange("p a s -> p (a s)"), start=True, stop=True).then_inc(swapped, 1)
                pe.wait_ge(swap_read, g * 2 + j + 1)

            def join(g, j, last):
                pe.wait_ge(join_ready, g * 4 + 2 * j + 2)
                pe.wait_ge(o_copied, g * N + (N if last else (j + 1) * STEPS + 3))
                wait(pe, join_copied, g * 2 + j)
                for s in range(ND):
                    pe.matmul(G.ps[:, 6, 0:32], od[:, j, s, :], join_d[:, s, :], start=(s == 0), stop=(s == ND - 1))
                for s in range(NSUM):
                    last = pe.matmul(G.ps[:, 6, VD:VD + ROWS], on[:, j, s, :], join_n[:, s, :], start=(s == 0), stop=(s == NSUM - 1))
                last.then_inc(joined[j], 1)

            def beat(g, n):
                now, one, two = (at(g, n, lag) for lag in range(3))
                if one:
                    scores(*one)
                if two:
                    values(*two)
                if now:
                    turn_keys(*now)
                for which in ended(g, n, 1):
                    swap(*which)
                if one:
                    turn_probs(*one)
                for which in ended(g, n, 4):
                    join(*which, n >= N)

            all_beats(pe, beat)

        def key_copies(eng, g, n, t, copied, copy):
            m, _, _ = turned_before(n, t)
            wait(eng, sn_ready, g * N + (n - 1))
            eng.wait_ge(k_turned, g * ALL_T + m + 1)
            copy(kT[:, n % 2, t, :], G.ps[:, KEY_BANKS[m % len(KEY_BANKS)], :]).then_inc(copied, 1)

        def slot(n):
            return quad(n) % QUADS if is_page(n) else QUADS + 1 if n % STEPS == S_WIN else QUADS

        @block.scalar
        def _(act):
            def exps_d(g, n):
                if n not in D_STEPS:
                    return
                width, o = (TS if n % STEPS == S_NEW else QT), slot(n)
                act.wait_ge(soft_d, g * len(D_STEPS) + before(D_STEPS, n) + 1)
                act.activation(pd[:, n % 2, 0:width], pd[:, n % 2, 0:width], ACT.Exp, bias=min_d[:, seq(n), o:o + 1], scale=-1.0,
                               accum_out=tot_d[:, seq(n), o:o + 1]).then_inc(exp_d, 1)

            def exps_n(g, n):
                x, o = pn[:, n % 2, 0:TS if n % STEPS == S_NEW else HT], slot(n)
                act.wait_ge(soft_n, g * N + n + 1)
                act.activation(x, x, ACT.Exp, bias=stat_n[:, seq(n), 0, o:o + 1], scale=-1.0,
                               accum_out=stat_n[:, seq(n), 1, o:o + 1]).then_inc(exp_n, 1)

            def copy_o(g, n):
                j = seq(n)
                if is_page(n):
                    act.wait_ge(used[quad(n) % RING], g * (2 * QUADS // RING) + quad(n) // RING + 1)
                else:
                    act.wait_ge(tail[j], g * 2 + (1 if n % STEPS == S_WIN else 2))
                wait(act, joined[j], g)
                if n in D_STEPS:
                    act.activation(od[:, j, slot(n), :], G.ps[:, 6, 0:VD], ACT.Copy)
                if n % STEPS == S_WIN:
                    act.activation(on[0:ROWS, j, NN:NN + 1, :], G.o_cmp[:, bass.ds(g * 2 + j, 1), :], ACT.Copy)
                act.activation(on[:, j, slot(n), :], G.ps[:, 6, VD:VD + KV1], ACT.Copy).then_inc(o_copied, 1)

            def weigh(g, j):
                act.wait_ge(folded, (g * 2 + j) * FOLDS + 3)
                act.activation(w_d[:], wt_d[:], ACT.Exp, bias=base_d[:], scale=-1.0).then_inc(weighed, 1)
                for branch, part in enumerate((slice(0, N_SEL), slice(N_SEL, NSTAT))):
                    act.activation(w_n[:, part, :], both_n[:, 0, part, :], ACT.Exp, bias=base_n[:, branch:branch + 1], scale=-1.0).then_inc(weighed, 1)

            def copy_joined(g, j):
                act.wait_ge(joined[j], g + 1)
                b = bass.ds(g * 2 + j, 1)
                act.activation(G.s_odT[:, :, b, :], G.ps[:, 6, 0:32].rearrange("p (h b t) -> p h b t", b=1, t=TS), ACT.Copy)
                for h in range(KVH):
                    part = slice(h * HD, (h + 1) * HD)
                    last = act.activation(G.s_onT[part, :, b, :],
                                          G.ps[part, 6, VD + h * 32:VD + (h + 1) * 32].rearrange("p (a b t) -> p a b t", b=1, t=TS), ACT.Copy)
                last.then_inc(join_copied, 1)

            def beat(g, n):
                now, one, two = (at(g, n, lag) for lag in range(3))
                even = [t for t in (key_tiles(n) if now else ()) if t % 2 == 0]
                for i in range(3):
                    if i < len(even):
                        key_copies(act, g, n, even[i], k_even, lambda dst, src: act.activation(dst, src, ACT.Copy))
                    if one and i < 2:
                        (exps_d, exps_n)[i](*one)
                if two:
                    copy_o(*two)
                for which in ended(g, n, 1):
                    weigh(*which)
                for which in ended(g, n, 4):
                    copy_joined(*which)

            all_beats(act, beat)

        @block.vector
        def _(dve):
            def soft(g, n):
                new = n % STEPS == S_NEW
                o = slot(n)
                if n in D_STEPS:
                    width = TS if new else QT
                    wait(dve, p_turned, g * N + (n - 1))
                    dve.wait_ge(sd_ready, g * len(D_STEPS) + before(D_STEPS, n) + 1)
                    dve.memset(carrier[:, 3 * n:3 * n + 1], 0.0)
                    dve.tensor_tensor_reduce(out=pd[:, n % 2, 0:width], in0=G.ps[:, 2, 0:width], in1=(G.bias_new_d if new else G.bias_d)[:],
                                             scale=1.0, scalar=3e38, op0=ALU.add, op1=ALU.min,
                                             accum_out=min_d[:, seq(n), o:o + 1]).then_inc(soft_d, 1)
                width = TS if new else HT
                wait(dve, p_turned, g * N + (n - 1))
                dve.wait_ge(sn_ready, g * N + n + 1)
                if is_page(n):
                    dve.wait_ge(mask_made, g * (2 * QUADS) + quad(n) + 1)
                dve.memset(carrier[:, 3 * n + 1:3 * n + 2], 0.0)
                bias = masked[:, quad(n) % 2, :] if is_page(n) else (G.bias_new_n if new else G.bias_w)[:]
                dve.tensor_tensor_reduce(out=pn[:, n % 2, 0:width], in0=G.ps[:, 3, 0:width], in1=bias,
                                         scale=1.0, scalar=3e38, op0=ALU.add, op1=ALU.min,
                                         accum_out=stat_n[:, seq(n), 0, o:o + 1]).then_inc(soft_n, 1)

            def copy_p(g, n):
                new = n % STEPS == S_NEW
                dve.wait_ge(p_turned, g * N + n + 1)
                wait(dve, o_copied, g * N + (n - 1))
                rows, dw, nw = (TS, P, P) if new else (P, QT, 2 * P)
                if n in D_STEPS:
                    dve.tensor_copy(pdT[0:rows, n % 2, 0:dw], G.ps[0:rows, 4, 0:dw])
                dve.tensor_copy(pnT[0:rows, n % 2, 0:nw], G.ps[0:rows, 5, 0:nw]).then_inc(p_copied, 1)

            def read_swap(g, j):
                dve.wait_ge(swapped, g * 2 + j + 1)
                other = G.ps[:, 5, 0:2 * NN].rearrange("p (a s) -> p a s", a=2)
                dve.tensor_copy(both_n[:, :, 0:NN, 1], other)
                dve.tensor_copy(both_n[:, :, NN, 1], other[:, :, QUADS]).then_inc(swap_read, 1)

            def fold(g, j):
                done = [0]

                def then(last):
                    done[0] += 1
                    last.then_inc(folded, 1)
                    dve.wait_ge(folded, (g * 2 + j) * FOLDS + done[0])

                def flat(x, part):
                    return x[:, part, :].rearrange("p s o -> p (s o)")

                sel, win = slice(0, N_SEL), slice(N_SEL, NSTAT)
                wait(dve, joined[1 - j], g + j)
                dve.wait_ge(exp_d, g * len(D_STEPS) + before(D_STEPS, (j + 1) * STEPS))
                dve.wait_ge(exp_n, g * N + (j + 1) * STEPS)
                dve.tensor_copy(both_n[:, :, 0:NN, 0], stat_n[:, j, :, :])
                then(dve.tensor_copy(both_n[:, :, NN, 0], stat_n[:, j, :, QUADS]))
                least, total = both_n[:, 0, :, :], both_n[:, 1, :, :]
                dve.tensor_tensor(wt_d[:], min_d[:, j, :], G.off_d[:], ALU.add)
                then(dve.tensor_tensor(least, least, G.off_n[:], ALU.add))
                dve.tensor_reduce(base_d[:], wt_d[:], AX, ALU.min)
                dve.tensor_reduce(base_n[:, 0:1], flat(least, sel), AX, ALU.min)
                then(dve.tensor_reduce(base_n[:, 1:2], flat(least, win), AX, ALU.min))
                dve.wait_ge(weighed, (g * 2 + j) * 3 + 3)
                dve.tensor_tensor(wt_d[:], w_d[:], tot_d[:, j, :], ALU.mult)
                then(dve.tensor_tensor(total, total, w_n[:], ALU.mult))
                dve.tensor_reduce(base_d[:], wt_d[:], AX, ALU.add)
                dve.tensor_reduce(base_n[:, 0:1], flat(total, sel), AX, ALU.add)
                then(dve.tensor_reduce(base_n[:, 1:2], flat(total, win), AX, ALU.add))
                dve.reciprocal(base_d[:], base_d[:])
                then(dve.reciprocal(base_n[:], base_n[:]))
                gate = G.gates_s[:, bass.ds(g * 2 + j, 1), :].rearrange("p o k -> p (o k)")
                dve.tensor_tensor(base_d[:], base_d[:], G.sgn_d[:], ALU.mult)
                dve.tensor_copy(own_n[:, NN:NSUM], gate[:, 0:1])
                then(dve.tensor_tensor(base_n[:], base_n[:], gate[:, 1:3], ALU.mult))
                dve.tensor_scalar(w_d[:], w_d[:], base_d[:], None, ALU.mult)
                dve.tensor_scalar(own_n[:, 0:N_SEL], w_n[:, sel, 0], base_n[:, 0:1], None, ALU.mult)
                then(dve.tensor_scalar(own_n[:, N_SEL:NN], w_n[:, N_SEL:NN, 0], base_n[:, 1:2], None, ALU.mult))
                then(dve.scalar_tensor_tensor(own_n[:, QUADS:N_SEL], w_n[:, NN:NSTAT, 0], base_n[:, 1:2], own_n[:, QUADS:N_SEL], ALU.mult, ALU.add))
                dve.tensor_tensor(join_d[:], G.comb_d[:].rearrange("p (o n) -> p o n", o=1).to_broadcast([P, ND, 32]),
                                  w_d[:].rearrange("p (s o) -> p s o", o=1).to_broadcast([P, ND, 32]), ALU.mult).then_inc(join_ready, 1)
                dve.tensor_tensor(join_n[:], G.comb_n[:].rearrange("p (o n) -> p o n", o=1).to_broadcast([P, NSUM, ROWS]),
                                  own_n[:].rearrange("p (s o) -> p s o", o=1).to_broadcast([P, NSUM, ROWS]), ALU.mult).then_inc(join_ready, 1)

            def beat(g, n):
                now, one = (at(g, n, lag) for lag in range(2))
                if one:
                    soft(*one)
                for t in (key_tiles(n) if now else ()):
                    if t % 2:
                        key_copies(dve, g, n, t, k_odd, lambda dst, src: dve.tensor_copy(dst, src))
                if now and n % STEPS == 0:
                    j = seq(n)
                    dve.wait_ge(small_in[j], g * SMALL + SMALL)
                    dve.tensor_scalar(qd[:, j, :, :], qd[:, j, :, :], -HD ** -0.5, None, ALU.mult).then_inc(scaled, 1)
                    dve.tensor_scalar(qn[:, j, :], qn[:, j, :], -HD ** -0.5, None, ALU.mult).then_inc(scaled, 1)
                for which in ended(g, n, 1):
                    read_swap(*which)
                if one:
                    copy_p(*one)
                for which in ended(g, n, 1):
                    fold(*which)

            all_beats(dve, beat)


def fill(nc, G, stage, pairs):
    with ExitStack() as ctx:
        filled = sem_maker(nc, ctx, stage)("filled")
        block = ctx.enter_context(nc.Block())

        @block.sync
        def _(sp):
            for dst, src in pairs:
                sp.dma_start(dst, src).then_inc(filled, 16)
            sp.wait_ge(filled, 16 * len(pairs))


def gates(nc, G):
    with ExitStack() as ctx:
        raw = ctx.enter_context(nc.sbuf_tensor("gt_raw", [N_GATE, SEQ], F32))
        sem = sem_maker(nc, ctx, "gt")
        raw_in, sample_in, turned, opened = sem("raw_in"), sem("sample_in"), sem("turned"), sem("opened")
        block = ctx.enter_context(nc.Block())

        def sample_gates(eng, odd):
            for n in range(odd, NSA_H, 2):
                for k in range(3):
                    eng.dma_start(G.gates_s[n * TS:(n + 1) * TS, :, k],
                                  G.z[Z_NG, n * 3 + k, ROW0:ROW0 + NS].rearrange("(b t) -> t b", t=TS)).then_inc(sample_in, 16)

        @block.sync
        def _(sp):
            sp.dma_start(raw[:], G.z[Z_NG, 0:N_GATE, 0:SEQ]).then_inc(raw_in, 16)
            sample_gates(sp, 0)
            load_pages(nc, G, sp, mybir.EngineType.SP, 0, 0, 0)
            sp.wait_ge(sample_in, 16 * N_GATE)
            sp.dma_start(G.gates_s[ROWS:P, :, :], G.gates_s[0:ROWS, :, :]).then_inc(sample_in, 16)


        @block.gpsimd
        def _(pool):
            load_pages(nc, G, pool, mybir.EngineType.Pool, 0, 0, 2)

        @block.tensor
        def _(pe):
            pe.wait_ge(raw_in, 16)
            for i in range(TILES):
                last = pe.transpose(G.ps[:, 0, i * N_GATE:(i + 1) * N_GATE], raw[:, i * P:(i + 1) * P], G.ident[0:N_GATE, 0:N_GATE])
            last.then_inc(turned, 1)

        @block.scalar
        def _(act):
            sample_gates(act, 1)
            load_pages(nc, G, act, mybir.EngineType.Activation, 0, 0, 1)
            act.wait_ge(turned, 1)
            act.activation(G.gates_t[:], G.ps[:, 0, 0:TILES * N_GATE].rearrange("p (i n) -> p i n", i=TILES), ACT.Sigmoid).then_inc(opened, 1)
            act.wait_ge(sample_in, 16 * (N_GATE + 1))
            act.activation(G.gates_s[:], G.gates_s[:], ACT.Sigmoid)

        @block.vector
        def _(dve):
            dve.wait_ge(opened, 1)
            g = G.gates_t[:, 0, 0:N_GATE:3]
            dve.tensor_scalar(g, g, G.row_valid[:], None, ALU.mult)


W_TILES = WIN // P + 1
NCB = 2 * PAGES


def prompt_nsa(nc, G):
    U = 2 * TILES
    WK = W_TILES * P
    with ExitStack() as ctx:
        def sb(name, shape, dt=F32):
            return ctx.enter_context(nc.sbuf_tensor(f"pn_{name}", shape, dt))
        q, k, v = sb("q", [P, 2, SEQ]), sb("k", [P, 2, SEQ]), sb("v", [P, 2, TILES, P])
        bias_s, bias_w, bias_c = sb("bias_s", [P, 2, SEQ]), sb("bias_w", [P, 2, WK]), sb("bias_c", [P, 2, TILES * NCB])
        probs_s, probs_w = sb("probs_s", [P, 4, SEQ]), sb("probs_w", [P, 4, WK + NCB])
        sT, wT = sb("sT", [P, 2, SEQ]), sb("wT", [P, 2, WK + P])
        least, total, share = sb("least", [P, 4, 3]), sb("total", [P, 4, 3]), sb("share", [P, 4, 3])
        carrier = sb("carrier", [P, 3 * U + 2])
        sem = sem_maker(nc, ctx, "pn")
        q_cleared, kv_in, bias_made, q_scaled = sem("q_cleared"), sem("kv_in"), sem("bias_made"), sem("q_scaled")
        q_in, head_scored = ([sem(f"{what}{j}") for j in range(2)] for what in ("q_in", "head_scored"))
        s_ready, biased, exped, t_ready, t_copied = ([sem(f"{what}{c}") for c in range(2)] for what in ("s_ready", "biased", "exped", "t_ready", "t_copied"))
        valued, joined, combined = sem("valued"), sem("joined"), sem("combined")
        block = ctx.enter_context(nc.Block())
        z_rows = G.z.rearrange("m p n -> (m p) n")
        JOIN = 4

        def wait(eng, sem, value):
            if not isinstance(value, int) or value > 0:
                eng.wait_ge(sem, value)

        def back(g, u, lag):
            if u >= lag:
                return (g, u - lag) if u - lag < U else None
            return None if isinstance(g, int) and g == 0 else (g - 1, u - lag + U)

        def all_beats(eng, beat):
            for u in range(U):
                beat(0, u)
            with eng.Fori(1, GRP - 1) as g:
                for u in range(U):
                    beat(g, u)
            for u in range(U + 3):
                beat(GRP - 1, u)

        def is_last(g):
            return isinstance(g, int) and g == GRP - 1

        def wide(u):
            w = min(u % TILES + 1, W_TILES) * P
            return w, WK - w

        @block.gpsimd
        def _(pool):
            pool.memset(q[:], 0.0).then_inc(q_cleared, 1)

        @block.sync
        def _(sp):
            sp.dma_start(k[:, 0, :], G.z[Z_NKV + 2, :, 0:SEQ]).then_inc(kv_in, 16)
            sp.dma_start(k[:, 1, :], G.z[Z_NKV + 4, :, 0:SEQ]).then_inc(kv_in, 16)
            sp.dma_start(v[:, 0, :, :], G.nsa_p[:, 384:512].rearrange("(i p) d -> p i d", p=P)).then_inc(kv_in, 16)
            sp.dma_start(v[:, 1, :, :], G.kvw[0:SEQ, 128:256].rearrange("(i p) d -> p i d", p=P)).then_inc(kv_in, 16)
            with sp.Fori(0, GRP) as g:
                for j in range(2):
                    sp.wait_ge(q_cleared, 1)
                    sp.wait_ge(head_scored[j], g)
                    sp.dma_start(q[j * HD:(j + 1) * HD, j, :], z_rows[bass.ds(g * HD + (Z_NQ * P + j * GRP * HD), HD), 0:SEQ]).then_inc(q_in[j], 16)

        @block.tensor
        def _(pe):
            def scores(g, u, c):
                i, j = u % TILES, u // TILES
                queries = q[:, j, i * P:(i + 1) * P]
                if i == 0 and c == 0:
                    pe.wait_ge(q_scaled, g * 2 + j + 1)
                wait(pe, biased[c], g * U + u)
                n, first = ((i + 1) * P, 0) if c == 0 else (wide(u)[0], (i + 1) * P - wide(u)[0])
                for n0 in range(0, n, 512):
                    m = min(512, n - n0)
                    last = pe.matmul(G.ps[:, 2 * c + n0 // 512, 0:m], queries, k[:, c, first + n0:first + n0 + m], start=True, stop=True)
                if c == 1:
                    last = pe.matmul(G.ps[:, 3, P:P + NCB], queries, G.ckT[:, NB, :].rearrange("d (a c) -> d c a", c=2), start=True, stop=True)
                last.then_inc(s_ready[c], 1)

            def turn(g, u, c):
                pe.wait_ge(exped[c], g * U + u + 1)
                wait(pe, t_copied[1 - c], g * U + u + c)
                count = (u % TILES + 1) if c == 0 else wide(u)[0] // P
                src = (probs_s, probs_w)[c]
                for t in range(count):
                    last = pe.transpose(G.ps[:, 4 + t // 4, (t % 4) * P:(t % 4 + 1) * P], src[:, u % 4, t * P:(t + 1) * P], G.ident[:])
                if c == 1:
                    last = pe.transpose(G.ps[0:NCB, 4 + count // 4, (count % 4) * P:(count % 4 + 1) * P],
                                        src[:, u % 4, WK:WK + NCB], G.ident[:])
                last.then_inc(t_ready[c], 1)

            def values(g, u, c):
                i, j = u % TILES, u // TILES
                pe.wait_ge(t_copied[c], g * U + u + 1)
                if c == 0:
                    wait(pe, joined, (g * U + (u - 1)) * JOIN)
                    for t in range(i + 1):
                        pe.matmul(G.ps[:, 6 + u % 2, P:2 * P], sT[:, u % 2, t * P:(t + 1) * P], v[:, 0, t, :], start=(t == 0), stop=(t == i))
                else:
                    count = wide(u)[0] // P
                    for t in range(count):
                        pe.matmul(G.ps[:, 6 + u % 2, 2 * P:3 * P], wT[:, u % 2, t * P:(t + 1) * P], v[:, 1, i + 1 - count + t, :],
                                  start=(t == 0), stop=(t == count - 1))
                    pe.matmul(G.ps[:, 6 + u % 2, 0:P], wT[0:NCB, u % 2, count * P:(count + 1) * P], G.cv[:, NB, :],
                              start=True, stop=True).then_inc(valued, 1)

            pe.wait_ge(kv_in, 64)
            def beat(g, u):
                now, two = back(g, u, 0), back(g, u, 2)
                if two:
                    turn(*two, 0)
                if now:
                    scores(*now, 0)
                if two:
                    turn(*two, 1)
                    values(*two, 0)
                if now:
                    scores(*now, 1)
                if two:
                    values(*two, 1)

            all_beats(pe, beat)

        @block.vector
        def _(dve):
            def least_of(g, u, out, scores, bias, column, at):
                dve.memset(carrier[:, 3 * u + column:3 * u + column + 1], 0.0)
                return dve.tensor_tensor_reduce(out=out, in0=scores, in1=bias, scale=1.0, scalar=3e38, op0=ALU.add, op1=ALU.min,
                                                accum_out=least[:, u % 4, at:at + 1])

            def scale(g, j):
                dve.wait_ge(q_in[j], g * 16 + 16)
                dve.tensor_scalar(q[:, j, :], q[:, j, :], -HD ** -0.5, None, ALU.mult).then_inc(q_scaled, 1)

            def selected(g, u):
                i, j = u % TILES, u // TILES
                n = (i + 1) * P
                if i == 0:
                    dve.wait_ge(bias_made, g * 6 + j * 3 + 3)
                wait(dve, t_ready[1], g * U + (u - 3))
                dve.wait_ge(s_ready[0], g * U + u + 1)
                least_of(g, u, probs_s[:, u % 4, 0:n], G.ps[:, 0:2, :].rearrange("p a n -> p (a n)")[:, 0:n], bias_s[:, j, SEQ - n:SEQ],
                         0, 1).then_inc(biased[0], 1)

            def window_and_compressed(g, u):
                i, j = u % TILES, u // TILES
                w, w0 = wide(u)
                dve.wait_ge(s_ready[1], g * U + u + 1)
                least_of(g, u, probs_w[:, u % 4, 0:w], G.ps[:, 2:4, :].rearrange("p a n -> p (a n)")[:, 0:w], bias_w[:, j, w0:WK], 1, 2)
                least_of(g, u, probs_w[:, u % 4, WK:WK + NCB], G.ps[:, 3, P:P + NCB], bias_c[:, j, i * NCB:(i + 1) * NCB],
                         2, 0).then_inc(biased[1], 1)
                if i == TILES - 1:
                    dve.memset(carrier[:, 3 * U + j:3 * U + j + 1], 0.0).then_inc(head_scored[j], 1)

            def copy_t(g, u):
                count = wide(u)[0] // P
                n = count * P
                dve.wait_ge(t_ready[1], g * U + u + 1)
                wait(dve, valued, g * U + (u - 1))
                both = G.ps[:, 4:6, :].rearrange("p a n -> p (a n)")
                dve.tensor_copy(wT[:, u % 2, 0:n], both[:, 0:n])
                dve.tensor_copy(wT[0:NCB, u % 2, n:n + P], both[0:NCB, n:n + P]).then_inc(t_copied[1], 1)

            def combine(g, u):
                i, j = u % TILES, u // TILES
                s = u % 4
                done = (g * U + u) * JOIN
                o = G.ps[:, 6 + u % 2, 0:3 * P].rearrange("p (k d) -> p k d", k=3)[:, :, j * HD:(j + 1) * HD]
                out = G.o_n[:, i, bass.ds(g * P + j * HD, HD)]
                dve.wait_ge(valued, g * U + u + 1)
                dve.reciprocal(share[:, s, :], total[:, s, :]).then_inc(combined, 1)
                dve.wait_ge(combined, (g * U + u) * 2 + 1)
                dve.tensor_tensor(share[:, s, :], share[:, s, :], G.gates_t[:, i, bass.ds(g * 3 + j * GRP * 3, 3)], ALU.mult).then_inc(combined, 1)
                dve.wait_ge(combined, (g * U + u) * 2 + 2)
                dve.tensor_scalar(out, o[:, 0, :], share[:, s, 0:1], None, ALU.mult).then_inc(joined, 1)
                dve.wait_ge(joined, done + 1)
                dve.scalar_tensor_tensor(out, o[:, 1, :], share[:, s, 1:2], out, ALU.mult, ALU.add).then_inc(joined, 1)
                dve.wait_ge(joined, done + 2)
                dve.scalar_tensor_tensor(out, o[:, 2, :], share[:, s, 2:3], out, ALU.mult, ALU.add).then_inc(joined, 2)

            dve.wait_ge(q_cleared, 1)
            scale(0, 0)

            def beat(g, u):
                now, two, three = back(g, u, 0), back(g, u, 2), back(g, u, 3)
                if now:
                    selected(*now)
                if two:
                    copy_t(*two)
                if now:
                    window_and_compressed(*now)
                if three:
                    combine(*three)
                if u == TILES // 2:
                    scale(g, 1)
                if u == TILES + TILES // 2 and not is_last(g):
                    scale(g + 1, 0)

            all_beats(dve, beat)

        @block.scalar
        def _(act):
            def table(g, j, k):
                dst, src = ((bias_s, G.causal), (bias_w, G.causal_w), (bias_c, G.causal_c))[k]
                act.activation(dst[:, j, :], src[:], ACT.Copy, scale=G.slopes[:, bass.ds(g + (DIFF_H + j * GRP), 1)]).then_inc(bias_made, 1)

            def exps(g, u):
                s, n, w = u % 4, (u % TILES + 1) * P, wide(u)[0]
                act.wait_ge(biased[0], g * U + u + 1)
                wait(act, joined, (g * U + (u - 3)) * JOIN)
                for c, x, at in ((0, probs_s[:, s, 0:n], 1), (1, probs_w[:, s, 0:w], 2), (1, probs_w[:, s, WK:WK + NCB], 0)):
                    if at == 2:
                        act.wait_ge(biased[1], g * U + u + 1)
                    last = act.activation(x, x, ACT.Exp, bias=least[:, s, at:at + 1], scale=-1.0, accum_out=total[:, s, at:at + 1])
                    if at != 2:
                        last.then_inc(exped[c], 1)

            def copy_t(g, u):
                n = (u % TILES + 1) * P
                act.wait_ge(t_ready[0], g * U + u + 1)
                wait(act, valued, g * U + (u - 1))
                act.activation(sT[:, u % 2, 0:n], G.ps[:, 4:6, :].rearrange("p a n -> p (a n)")[:, 0:n], ACT.Copy).then_inc(t_copied[0], 1)

            for k in range(3):
                table(0, 0, k)

            def beat(g, u):
                now, two = back(g, u, 0), back(g, u, 2)
                if two:
                    copy_t(*two)
                if now:
                    exps(*now)
                if 1 <= u < 4:
                    table(g, 1, u - 1)
                if TILES + 1 <= u < TILES + 4 and not is_last(g):
                    table(g + 1, 0, u - TILES - 1)

            all_beats(act, beat)


def turn_outputs(nc, G):
    BW = 4 * P
    with ExitStack() as ctx:
        def sb(name, shape, dt=F32):
            return ctx.enter_context(nc.sbuf_tensor(f"to_{name}", shape, dt))
        sq, ss, sq_s, rms_s = sb("sq", [P, TILES * DIFF_H, VD]), sb("ss", [P, TILES * DIFF_H]), sb("sq_s", [P, DIFF_H * NS]), sb("rms_s", [P, DIFF_H * NS])
        sem = sem_maker(nc, ctx, "to")
        step, s_summed, rooted, turned, high, low, s_high = (sem(x) for x in ("step", "s_summed", "rooted", "turned", "high", "low", "s_high"))
        block = ctx.enter_context(nc.Block())
        od = G.od[:].rearrange("p i (h d) -> p (i h) d", d=VD)
        s_od = G.s_odT[:].rearrange("p h b t -> p (h b t)")
        groups = 2 * TILES
        SCALED = 6

        @block.tensor
        def _(pe):
            for n in range(groups):
                which, i = n // TILES, n % TILES
                if n >= 4:
                    pe.wait_ge(low, n - 3)
                if n == TILES:
                    pe.wait_ge(step, SCALED)
                src = (G.o_n, G.od)[which]
                for t in range(4):
                    last = pe.transpose(G.ps[:, n % 4, t * P:(t + 1) * P], src[:, i, t * P:(t + 1) * P], G.ident[:])
                last.then_inc(turned, 1)
                if n == 3:
                    pe.wait_ge(step, 1)
                    pe.matmul(G.ps[:, 4, 0:DIFF_H * NS], G.ones[:], sq_s[:], start=True, stop=True).then_inc(s_summed, 1)

        @block.scalar
        def _(act):
            def hi(n):
                dst = (G.onh, G.odh)[n // TILES][:, :, (n % TILES) * P:(n % TILES + 1) * P]
                act.wait_ge(turned, n + 1)
                act.activation(dst, G.ps[:, n % 4, 0:BW].rearrange("p (k t) -> p k t", k=4), ACT.Copy).then_inc(high, 1)

            act.activation(G.onh[:, :, SEQ:SEQ + NS], G.s_onT[:].rearrange("p a b t -> p a (b t)"), ACT.Copy).then_inc(s_high, 1)
            for n in range(4):
                hi(n)
            act.wait_ge(step, 3)
            act.wait_ge(s_summed, 1)
            act.activation(ss[:], ss[:], ACT.Sqrt, bias=G.eps[:], scale=1.0 / VD)
            act.activation(rms_s[:], G.ps[:, 4, 0:DIFF_H * NS], ACT.Sqrt, bias=G.eps[:], scale=1.0 / VD).then_inc(rooted, 1)
            for n in range(4, TILES):
                hi(n)
            act.wait_ge(step, SCALED + 1)
            act.activation(G.odh[:, :, SEQ:SEQ + NS], G.s_odT[:].rearrange("p a b t -> p a (b t)"), ACT.Copy).then_inc(s_high, 1)
            for n in range(TILES, groups):
                hi(n)

        @block.vector
        def _(dve):
            done = [0]

            def then(ins):
                done[0] += 1
                ins.then_inc(step, 1)
                dve.wait_ge(step, done[0])

            def lo(n):
                part = slice((n % TILES) * P, (n % TILES + 1) * P)
                h, l = ((G.onh, G.onl), (G.odh, G.odl))[n // TILES]
                dve.wait_ge(high, n + 1)
                dve.tensor_tensor(l[:, :, part], G.ps[:, n % 4, 0:BW].rearrange("p (k t) -> p k t", k=4), h[:, :, part].bitcast(F32),
                                  ALU.subtract).then_inc(low, 1)

            then(dve.tensor_tensor(sq_s[:], s_od, s_od, ALU.mult))
            then(dve.tensor_tensor(sq[:], od, od, ALU.mult))
            then(dve.tensor_reduce(ss[:], sq[:], AX, ALU.add))
            for n in range(4):
                lo(n)
            dve.wait_ge(rooted, 1)
            then(dve.reciprocal(ss[:], ss[:]))
            then(dve.reciprocal(rms_s[:], rms_s[:]))
            then(dve.tensor_tensor(od, od, ss[:].rearrange("p (n o) -> p n o", o=1).to_broadcast([P, TILES * DIFF_H, VD]), ALU.mult))
            then(dve.tensor_tensor(s_od, s_od, rms_s[:], ALU.mult))
            for n in range(4, TILES):
                lo(n)
            dve.wait_ge(s_high, 2)
            for h, l, s in ((G.onh, G.onl, G.s_onT), (G.odh, G.odl, G.s_odT)):
                dve.tensor_tensor(l[:, :, SEQ:SEQ + NS], s[:].rearrange("p a b t -> p a (b t)"), h[:, :, SEQ:SEQ + NS].bitcast(F32), ALU.subtract)
            for n in range(TILES, groups):
                lo(n)

        @block.gpsimd
        def _(pool):
            for x in (G.onh, G.onl, G.odh, G.odl):
                pool.memset(x[:, :, SEQ + NS:NT].bitcast(F32), 0.0)


def merge_up(nc, G):
    rounds = KD // 2
    with ExitStack() as ctx:
        def sb(name, shape, dt=F32):
            return ctx.enter_context(nc.sbuf_tensor(f"mu_{name}", shape, dt))
        raw, wh, wl = sb("raw", [P, 4, 4 * P]), sb("wh", [P, 4, 4 * P], F32R), sb("wl", [P, 4, 4 * P], F32R)
        gate = sb("gate", [P, 4, NT])
        gain = sb("gain", [P, 1])
        sem = sem_maker(nc, ctx, "mu")
        raw_in, gate_in, w_high, w_split, acc_ready, opened, weighed = (
            [sem(f"{what}{q}") for q in range(4)] for what in ("raw_in", "gate_in", "w_high", "w_split", "acc_ready", "opened", "weighed"))
        m_made, m_out = ([sem(f"{what}{p}") for p in range(2)] for what in ("m_made", "m_out"))
        gain_in, gain_scaled = sem("gain_in"), sem("gain_scaled")
        block = ctx.enter_context(nc.Block())
        operands = ((G.onh, G.onl), (G.odh, G.odl))
        w = (wh, wl)
        LOADS = (2, 1)

        @block.sync
        def _(sp):
            sp.dma_start(gain[:], G.g_subln).then_inc(gain_in, 16)
            with sp.Fori(0, rounds) as r:
                for q in range(4):
                    p, s = q // 2, q % 2
                    cols = bass.ds(r * (2 * P) + p * P, P)
                    dst = raw[:, q, :].rearrange("p (k n) -> p k n", k=4)
                    sp.wait_ge(w_split[q], r)
                    if s == 0:
                        src = G.w_up_nsa[:, cols].rearrange("(h g d) n -> h d g n", h=KVH, g=GRP)
                        for h in range(KVH):
                            sp.dma_start(dst[h * HD:(h + 1) * HD, :, :], src[h]).then_inc(raw_in[q], 16)
                    else:
                        sp.dma_start(dst, G.w_up_diff[:, cols].rearrange("(k p) n -> p k n", p=P)).then_inc(raw_in[q], 16)
                for q in range(4):
                    p, s = q // 2, q % 2
                    if s == 0:
                        sp.wait_ge(m_out[p], r * 16)
                    else:
                        sp.wait_ge(m_made[p], r)
                    sp.dma_start(gate[:, q, :], G.z[bass.ds(r * 2 + (Z_MG + s * KD + p), 1), :, :].rearrange("o p n -> (o p) n")).then_inc(gate_in[q], 16)

        @block.gpsimd
        def _(pool):
            with pool.Fori(0, rounds) as r:
                for p in range(2):
                    pool.wait_ge(m_made[p], r + 1)
                    pool.dma_start(G.m[bass.ds(r * 2 + p, 1), :, :].rearrange("o p n -> (o p) n"), gate[:, 2 * p, :]).then_inc(m_out[p], 16)
            for p in range(2):
                pool.wait_ge(m_out[p], 16 * rounds)

        @block.scalar
        def _(act):
            def hi(r, q):
                act.wait_ge(raw_in[q], (r + 1) * (16 * LOADS[q % 2]))
                act.wait_ge(acc_ready[q], r)
                act.activation(wh[:, q, :], raw[:, q, :], ACT.Copy, scale=gain[:] if q % 2 else 1.0).then_inc(w_high[q], 1)

            def open_gate(r, q):
                act.wait_ge(gate_in[q], (r + 1) * 16)
                act.activation(gate[:, q, :], gate[:, q, :], ACT.Sigmoid).then_inc(opened[q], 1)

            act.wait_ge(gain_scaled, 1)
            for q in range(4):
                hi(0, q)
            with act.Fori(0, rounds - 1) as r:
                for q in range(4):
                    open_gate(r, q)
                for q in range(4):
                    hi(r + 1, q)
            for q in range(4):
                open_gate(rounds - 1, q)

        @block.vector
        def _(dve):
            def lo(r, q):
                dve.wait_ge(w_high[q], r + 1)
                if q % 2:
                    dve.scalar_tensor_tensor(wl[:, q, :], raw[:, q, :], gain[:], wh[:, q, :].bitcast(F32), ALU.mult, ALU.subtract).then_inc(w_split[q], 1)
                else:
                    dve.tensor_tensor(wl[:, q, :], raw[:, q, :], wh[:, q, :].bitcast(F32), ALU.subtract).then_inc(w_split[q], 1)

            def weigh(r, q):
                s = q % 2
                dve.wait_ge(opened[q], r + 1)
                dve.wait_ge(acc_ready[q], r + 1)
                x = chunks(gate[:, q, :])
                dve.tensor_tensor(x, x, G.ps[:, 3 * s:3 * s + NCH, 0:CH], ALU.mult).then_inc(weighed[q], 1)

            def add(r, p):
                for s in range(2):
                    dve.wait_ge(weighed[2 * p + s], r + 1)
                dve.tensor_tensor(gate[:, 2 * p, :], gate[:, 2 * p, :], gate[:, 2 * p + 1, :], ALU.add).then_inc(m_made[p], 1)

            dve.wait_ge(gain_in, 16)
            dve.tensor_scalar(gain[:], gain[:], 1.0 - LAM_INIT, None, ALU.mult).then_inc(gain_scaled, 1)
            dve.wait_ge(gain_scaled, 1)
            for q in range(4):
                lo(0, q)
            with dve.Fori(0, rounds - 1) as r:
                for q in range(4):
                    weigh(r, q)
                    if q % 2:
                        add(r, q // 2)
                    lo(r + 1, q)
            for q in range(4):
                weigh(rounds - 1, q)
                if q % 2:
                    add(rounds - 1, q // 2)

        @block.tensor
        def _(pe):
            with pe.Fori(0, rounds) as r:
                for q in range(4):
                    p, s = q // 2, q % 2
                    pe.wait_ge(w_split[q], r + 1)
                    pe.wait_ge(weighed[s + 2 * (1 - p)], r + p)
                    for c in range(NCH):
                        for k in range(4):
                            for n, (a, b) in enumerate(PAIRS):
                                last = pe.matmul(G.ps[:, 3 * s + c, 0:CH], w[a][:, q, k * P:(k + 1) * P], operands[s][b][:, k, c * CH:(c + 1) * CH],
                                                 start=(k == 0 and n == 0), stop=(k == 3 and n == 2))
                    last.then_inc(acc_ready[q], 1)


def merge_out(nc, G):
    rounds = KD // 2
    with ExitStack() as ctx:
        def sb(name, shape, dt):
            return ctx.enter_context(nc.sbuf_tensor(f"mo_{name}", shape, dt))
        hh, hl = sb("hh", [P, KD, NT], F32R), sb("hl", [P, KD, NT], F32R)
        tmp = [sb(f"tmp{i}", [P, NT], F32) for i in range(2)]
        f = sb("f", [P, KD, NT], F32)
        with ExitStack() as inner:
            raw = inner.enter_context(nc.sbuf_tensor("mo_raw", [P, 2, D], F32))
            wh = inner.enter_context(nc.sbuf_tensor("mo_wh", [P, 2, D], F32R))
            wl = inner.enter_context(nc.sbuf_tensor("mo_wl", [P, 2, D], F32R))
            sem = sem_maker(nc, inner, "mo")
            m_in, m_high, m_split = [sem(f"m_in{k}") for k in range(KD)], sem("m_high"), sem("m_split")
            raw_in, w_high, w_split, f_ready, f_copied = (
                [sem(f"{what}{j}") for j in range(2)] for what in ("raw_in", "w_high", "w_split", "f_ready", "f_copied"))
            x_in = sem("x_in")
            block = inner.enter_context(nc.Block())
            w, h = (wh, wl), (hh, hl)

            @block.sync
            def _(sp):
                for k in range(KD):
                    sp.dma_start(f[:, k, :], G.m[k]).then_inc(m_in[k], 16)
                for k in range(KD):
                    sp.dma_start(G.xT[:, k, :], G.x_kept[k]).then_inc(x_in, 16)
                sp.wait_ge(x_in, 16 * KD)

            @block.gpsimd
            def _(pool):
                with pool.Fori(0, rounds) as r:
                    for j in range(2):
                        pool.wait_ge(w_split[j], r)
                        pool.dma_start(raw[:, j, :].rearrange("p (k n) -> p k n", k=KD),
                                       G.w_out[:, bass.ds(r * (2 * P) + j * P, P)].rearrange("(k p) n -> p k n", p=P)).then_inc(raw_in[j], 16)

            @block.scalar
            def _(act):
                def hi(r, j):
                    act.wait_ge(raw_in[j], r * 16 + 16)
                    act.wait_ge(f_ready[j], r)
                    act.activation(wh[:, j, :], raw[:, j, :], ACT.Copy).then_inc(w_high[j], 1)

                def copy_f(r, j):
                    act.wait_ge(f_ready[j], r + 1)
                    act.activation(f[:, bass.ds(r * 2 + j, 1), :].rearrange("p o (c n) -> p (o c) n", c=NCH), G.ps[:, 3 * j:3 * j + NCH, 0:CH],
                                   ACT.Copy).then_inc(f_copied[j], 1)

                hi(0, 0)
                hi(0, 1)
                for k in range(KD):
                    act.wait_ge(m_in[k], 16)
                    act.activation(hh[:, k, :], f[:, k, :], ACT.Copy).then_inc(m_high, 1)
                with act.Fori(0, rounds - 1) as r:
                    for j in range(2):
                        copy_f(r, j)
                        hi(r + 1, j)
                for j in range(2):
                    copy_f(rounds - 1, j)

            @block.vector
            def _(dve):
                def lo(r, j):
                    dve.wait_ge(w_high[j], r + 1)
                    dve.tensor_tensor(wl[:, j, :], raw[:, j, :], wh[:, j, :].bitcast(F32), ALU.subtract).then_inc(w_split[j], 1)

                lo(0, 0)
                lo(0, 1)
                for k in range(KD):
                    dve.wait_ge(m_high, k + 1)
                    dve.tensor_tensor(hl[:, k, :], f[:, k, :], hh[:, k, :].bitcast(F32), ALU.subtract).then_inc(m_split, 1)
                with dve.Fori(1, rounds) as r:
                    lo(r, 0)
                    lo(r, 1)

            @block.tensor
            def _(pe):
                with pe.Fori(0, rounds) as r:
                    for j in range(2):
                        pe.wait_ge(w_split[j], r + 1)
                        pe.wait_ge(f_copied[j], r)
                        for k in range(KD):
                            if j == 0:
                                pe.wait_ge(m_split, k + 1)
                            for n, (a, b) in enumerate(PAIRS):
                                for c in range(NCH):
                                    last = pe.matmul(G.ps[:, 3 * j + c, 0:CH], w[a][:, j, k * P:(k + 1) * P], h[b][:, k, c * CH:(c + 1) * CH],
                                                     start=(k == 0 and n == 0), stop=(k == KD - 1 and n == 2))
                        last.then_inc(f_ready[j], 1)
        norm_add(nc, G, "mop", G.gains["g_mix_post"], f, 1.0, [t[:] for t in tmp])


def store_tokens(nc, G):
    tiles = SEQ // P + 1
    with ExitStack() as ctx:
        rows = ctx.enter_context(nc.sbuf_tensor("st_rows", [P, 3, D], F32))
        sem = sem_maker(nc, ctx, "st")
        transposed = sem("transposed")
        copied = [sem("copied_act"), sem("copied_dve")]
        rows_out = [sem(f"rows_out{i}") for i in range(3)]
        block = ctx.enter_context(nc.Block())

        def size(i):
            return P if i < tiles - 1 else NS

        @block.sync
        def _(sp):
            for i in range(tiles):
                for c in copied:
                    sp.wait_ge(c, i + 1)
                dst = G.y_prompt[i * P:(i + 1) * P, :] if i < tiles - 1 else G.y_sample
                sp.dma_start(dst, rows[0:size(i), i % 3, :]).then_inc(rows_out[i % 3], 16)
            for i in range(3):
                sp.wait_ge(rows_out[i], 16 * (tiles // 3))

        @block.tensor
        def _(pe):
            for i in range(tiles):
                for half in range(2):
                    if i >= 2:
                        pe.wait_ge(copied[half], i - 1)
                    for t in range(4):
                        last = pe.transpose(G.ps[0:size(i), 2 * half + i % 2, t * P:(t + 1) * P], G.xT[:, 4 * half + t, i * P:i * P + size(i)],
                                            G.ident[:])
                    last.then_inc(transposed, 1)

        def copy_half(eng, half, copy):
            for i in range(tiles):
                eng.wait_ge(transposed, 2 * i + half + 1)
                if i >= 3:
                    eng.wait_ge(rows_out[i % 3], 16 * (i // 3))
                copy(rows[0:size(i), i % 3, half * 512:(half + 1) * 512], G.ps[0:size(i), 2 * half + i % 2, :]).then_inc(copied[half], 1)

        @block.scalar
        def _(act):
            copy_half(act, 0, lambda dst, src: act.activation(dst, src, ACT.Copy))

        @block.vector
        def _(dve):
            copy_half(dve, 1, lambda dst, src: dve.tensor_copy(dst, src))


def step_kernel(nc, a):
    G = Parts()
    G.x_prompt, G.x_sample, G.c_ident = a["x_prompt"], a["x_sample"], a["t_ident"]
    G.w_in, G.w_out, G.w_up_nsa, G.w_up_diff = a["w_in"], a["w_out"], a["w_up_nsa"], a["w_up_diff"]
    G.cmp_w1, G.cmp_w2, G.cmp_b1 = a["cmp_w1"], a["cmp_w2"], a["cmp_b1"].rearrange("k e -> e k")
    G.cache_nsa, G.cache_diff, G.win, G.page_table = a["cache_nsa_kv"], a["cache_diff_kv"], a["state_win_kv"], a["page_table"]
    G.lambda_qk = a["lambda_qk"]
    G.g_subln = a["g_diff_subln"].rearrange("(p o) -> p o", o=1)
    G.y_prompt, G.y_sample = a["y_prompt"], a["y_sample"]
    G.nsa_p, G.nsa_s, G.diff_p, G.diff_s = a["nsa_kv_prompt"], a["nsa_kv_sample"], a["diff_kv_prompt"], a["diff_kv_sample"]
    G.win_p, G.win_s = a["win_kv_prompt"], a["win_kv_sample"]
    G.z = nc.dram_tensor("z_scratch", [Z_NG + 1, P, NT], F32).ap()
    G.m = nc.dram_tensor("m_scratch", [KD, P, NT], F32).ap()
    G.x_kept = nc.dram_tensor("x_scratch", [KD, P, NT], F32).ap()
    G.kvw = nc.dram_tensor("kvw_scratch", [SEQ + NS, 2 * KV1], F32).ap()
    G.tr_stores = {}
    G.gains = {n: a[n].rearrange("(k p) -> p k", p=P) for n in
               ("g_ffn1_pre", "g_ffn1_post", "g_mix_pre", "g_mix_post", "g_ffn2_pre", "g_ffn2_post")}
    with ExitStack() as ctx:
        ctx.enter_context(nc.allow_non_contiguous_dma(reason="gain vectors and gates, a few kilobytes"))

        def placer(stack):
            def sb(name, shape, dt=F32):
                return stack.enter_context(nc.sbuf_tensor(name, shape, dt))
            return sb

        sb = placer(ctx)
        G.ps = ctx.enter_context(nc.psum_tensor("ps", [P, 8, 512], F32))
        G.ident, G.ones, G.eps = sb("ident", [P, P]), sb("ones", [P, P]), sb("eps", [P, 1])
        G.gain = sb("gain", [P, KD])

        def with_tokens(part):
            with ExitStack() as inner:
                place = placer(inner)
                G.xT, G.rms = place("xT_" + part.__name__, [P, KD, NT]), place("rms_" + part.__name__, [P, NT])
                part()

        def before():
            load_tokens(nc, G)
            ffn(nc, G, "f1", a["ffn1_w1"], a["ffn1_w3"], a["ffn1_w2"], G.gains["g_ffn1_pre"], G.gains["g_ffn1_post"], True)
            G.w1 = shelf.enter_context(nc.sbuf_tensor("w1", [P, 2, HD, 2 * HD], F32, side="right"))
            project(nc, G)

        def after():
            merge_out(nc, G)
            ffn(nc, G, "f2", a["ffn2_w1"], a["ffn2_w3"], a["ffn2_w2"], G.gains["g_ffn2_pre"], G.gains["g_ffn2_post"], False)
            store_tokens(nc, G)

        shelf = ctx.enter_context(ExitStack())
        with_tokens(before)
        token_rows(nc, G)
        with ExitStack() as mix:
            place = placer(mix)
            tables = []

            def table(put, name):
                t = put("c_" + name, list(a["t_" + name].shape))
                tables.append((t[:], a["t_" + name]))
                return t

            G.s_odT, G.s_onT = place("s_odT", [P, DIFF_H, NB, TS]), place("s_onT", [P, GRP, NB, TS])
            G.nlam, G.sgn_d = place("nlam", [P, 1]), place("sgn_d", [P, 1])
            G.gates_t, G.gates_s = place("gates_t", [P, TILES, N_GATE]), place("gates_s", [P, NB, 3])
            G.ckT, G.cv = place("ckT", [P, NB + 1, NBLK]), place("cv", [NBLK, NB + 1, P])
            G.slopes, G.row_valid, component = table(place, "slopes"), table(place, "row_valid"), table(place, "component")
            with ExitStack() as part:
                put = placer(part)
                G.pt = put("pt", [1, NB * PAGES], I32)
                tables.append((G.pt[:], G.page_table))
                fill(nc, G, "shared", tables)
                G.o_cmp, G.drop = put("o_cmp", [ROWS, NB, P]), put("drop", [P, NB, NBLK])
                with ExitStack() as loaded:
                    chunk_sem = sem_maker(nc, loaded, "pages")
                    G.page_in = [[chunk_sem(f"page_in{c}_{s}") for s in range(3)] for c in range(2)]
                    G.pages = placer(loaded)("pages", [P, 2, CHUNK, 2, KVH, HD])
                    gates(nc, G)
                    lambda_scale(nc, G)
                    sign(nc, G, component)
                    compress(nc, G)
                shelf.close()
                tables.clear()
                G.bias_cmp, G.group_sum = table(put, "bias_cmp"), table(put, "group_sum")
                G.bias_d, G.bias_new_d, G.off_d, G.comb_d = (table(put, x) for x in ("bias_d", "bias_new_d", "off_d", "comb_d"))
                G.bias_n, G.bias_w, G.bias_new_n, G.off_n = (table(put, x) for x in ("bias_n", "bias_w", "bias_new_n", "off_n"))
                G.comb_n, G.swap_n = table(put, "comb_n"), table(put, "swap_n")
                fill(nc, G, "sample", tables)
                quads = sem_maker(nc, part, "quads")
                G.d_in, G.n_in = ([quads(f"{what}{r}") for r in range(RING)] for what in ("d_in", "n_in"))
                G.dpage, G.npage = put("dpage", [P, RING, QUAD, 2, DIFF_H * VD]), put("npage", [P, RING, QUAD, 2, KV1])
                sample_select(nc, G)
                sample_attend(nc, G)
            with ExitStack() as part:
                put = placer(part)
                G.onh, G.onl, G.odh, G.odl = (put(x, [P, 4, NT], F32R) for x in ("onh", "onl", "odh", "odl"))
                with ExitStack() as rows:
                    put_rows = placer(rows)
                    G.od, G.o_n = put_rows("od", [P, TILES, DIFF_H * VD]), put_rows("o_n", [P, TILES, NSA_H * HD])
                    with ExitStack() as attend:
                        put_tables = placer(attend)
                        tables.clear()
                        G.causal, G.causal_w, G.causal_c = (table(put_tables, x) for x in ("causal", "causal_w", "causal_c"))
                        fill(nc, G, "prompt", tables)
                        prompt_diff(nc, G)
                        prompt_nsa(nc, G)
                    turn_outputs(nc, G)
                merge_up(nc, G)
        with_tokens(after)


def sign(nc, G, component):
    with ExitStack() as ctx:
        signed = sem_maker(nc, ctx, "sg")("signed")
        block = ctx.enter_context(nc.Block())

        @block.vector
        def _(dve):
            dve.tensor_tensor(G.sgn_d[:], G.nlam[:], component[:, 1:2], ALU.mult).then_inc(signed, 1)
            dve.wait_ge(signed, 1)
            dve.tensor_tensor(G.sgn_d[:], G.sgn_d[:], component[:, 0:1], ALU.add)


def shape_tables():
    import numpy as np
    far, masked = 1e32, 1e30
    d_slope = 2.0 ** (-8.0 * np.arange(1, DIFF_H + 1) / DIFF_H)
    n_slope = 2.0 ** (-8.0 * np.arange(1, NSA_H + 1) / NSA_H)
    t = {"ident": np.eye(P)}
    t["slopes"] = np.tile(np.concatenate([d_slope, n_slope]), (P, 1))
    tok = np.arange(P)[:, None]
    t["row_valid"] = tok >= BLK - 1
    r = np.arange(P - SEQ, P)[None]
    t["causal"] = np.where(r <= tok, -r, far)
    r = np.arange(-WIN, P)[None]
    t["causal_w"] = np.where((r <= tok) & (tok - r < WIN), -r, far)
    half, page = np.arange(NCB) // PAGES, np.arange(NCB) % PAGES
    end = (2 * page + half + 1) * BLK - 1
    qpos = (np.arange(TILES)[None, :, None] * P + tok[:, :, None])
    t["causal_c"] = np.where((page < TILES) & (end <= qpos), -end, far).reshape(P, TILES * NCB)
    i = np.arange(P)
    head, comp, tt = i // 32, (i % 32) // TS, (i % TS)[:, None]
    t["component"] = np.stack([comp == 0, comp == 1], 1)
    sd = np.where(comp < 2, d_slope[head], 0.0)[:, None]
    past = PAGES * PAGE
    t["bias_d"] = -sd * np.arange(QT)
    t["bias_new_d"] = np.where(np.arange(TS) > tt, masked, -sd * np.arange(TS))
    t["off_d"] = np.concatenate([-sd * (QT * np.arange(QUADS) - past), 0 * sd], 1)
    comb = np.zeros((P, 32))
    on = comp < 2
    comb[i[on], TS * head[on] + i[on] % TS] = 1
    t["comb_d"] = comb
    i = np.arange(ROWS)
    sn, tt = n_slope[i // TS][:, None], (i % TS)[:, None]
    i2 = np.arange(P)
    second, sn2, tt2 = (i2 // ROWS)[:, None], n_slope[i2 % ROWS // TS][:, None], (i2 % TS)[:, None]
    key = second * (QT // 2) + np.arange(QT // 2)
    t["bias_n"] = -sn2 * key
    t["bias_w"] = np.where(key <= tt2, masked, -sn2 * key)
    t["bias_new_n"] = np.where(np.arange(TS) > tt2, masked, -sn2 * np.arange(TS))
    off = np.zeros((P, QUADS + 3, 2))
    off[:, 0:QUADS, :] = (-sn2 * (QT * np.arange(QUADS) - past))[:, :, None]
    off[:, QUADS + 1, :] = sn2 * WIN
    is_second = np.stack([i2 >= ROWS, i2 < ROWS], 1)
    off[:, QUADS, :] = np.where(is_second, masked, 0)
    off[:, QUADS + 2, :] = np.where(is_second, 0, masked)
    t["off_n"] = off
    t["comb_n"] = i2[:, None] % ROWS == np.arange(ROWS)
    t["swap_n"] = i2[:, None] == (i2 + ROWS) % P
    t["bias_cmp"] = -sn * (end - past)
    t["group_sum"] = (i[:, None] // (GRP * TS) == i // (GRP * TS)) & (i[:, None] % TS == i % TS)
    return {"t_" + k: np.ascontiguousarray(v, dtype=np.float32) for k, v in t.items()}


OUTPUTS = (
    ("y_prompt", (SEQ, D), (1, SEQ, D)),
    ("y_sample", (NS, D), (NB, TS, D)),
    ("nsa_kv_prompt", (SEQ, 512), (1, 1, SEQ, 4, KVH, HD)),
    ("nsa_kv_sample", (NS, 512), (1, NB, TS, 4, KVH, HD)),
    ("diff_kv_prompt", (SEQ, 1024), (1, 1, SEQ, 2, DIFF_H, VD)),
    ("diff_kv_sample", (NS, 1024), (1, NB, TS, 2, DIFF_H, VD)),
    ("win_kv_prompt", (WIN, 256), (1, 1, WIN, 2, KVH, HD)),
    ("win_kv_sample", (NB, WIN, 256), (1, NB, WIN, 2, KVH, HD)),
)
SHAPES = {
    "x_prompt": (SEQ, D), "x_sample": (NS, D), "page_table": (1, NB * PAGES),
    "cache_nsa_kv": (N_POOL, PAGE, 512), "cache_diff_kv": (N_POOL, PAGE, 1024), "state_win_kv": (NB, WIN, 256),
}


def kernel(**inputs):
    import numpy as np
    import concourse.bacc as bacc
    from concourse.bass_utils import run_bass_kernel_spmd

    arrays = {}
    for name, x in inputs.items():
        x = np.ascontiguousarray(x)
        arrays[name] = x.reshape(SHAPES.get(name, x.shape[1:]))
    arrays.update(shape_tables())
    nc = bacc.Bacc("TRN2", target_bir_lowering=False, num_devices=1)
    a = {name: nc.dram_tensor(name, x.shape, mybir.dt.from_np(x.dtype), kind="ExternalInput").ap() for name, x in arrays.items()}
    for name, shape, _ in OUTPUTS:
        a[name] = nc.dram_tensor(name, shape, F32, kind="ExternalOutput").ap()
    step_kernel(nc, a)
    result = run_bass_kernel_spmd(nc, [arrays], core_ids=[0]).results[0]
    return tuple(result[name].reshape(shape) for name, _, shape in OUTPUTS)
```
